# Optimizing a Trainium2 kernel written in Bass

```python
import math
import functools
import jax
import jax.numpy as jnp
from jax import lax
import numpy as np

D_MODEL = 1024
BATCH = 1
SEQ = 2048
DEPTH = 1
DEC_BATCH = 8
DEC_SEQ = 4
PAST_LEN = 2048
PAGE_SIZE = 128

HEAD_DIM = 64
N_ATTN_HEADS = 8
ATTN_WIDTH = N_ATTN_HEADS * HEAD_DIM
CONV_WIDTH = D_MODEL - ATTN_WIDTH
CONV_KERNEL = 31
CONV_HIST = CONV_KERNEL - 1
IN_WIDTH = 3 * ATTN_WIDTH + 2 * CONV_WIDTH
DILATED_PATTERNS = ((128, 1), (512, 4), (2048, 16))
WINDOW_MAX = max(w for w, _ in DILATED_PATTERNS)
NUM_BUCKETS = 32
MAX_DISTANCE = WINDOW_MAX
D_FF = 4 * D_MODEL
N_MOD = 6
EPS = 1e-6

kernel_name = "hybrid_dilated_attn_conformer_conv_step"

def rms_norm(x, g):
    xf = x.astype(jnp.float32)
    y = xf * lax.rsqrt(jnp.mean(jnp.square(xf), axis=-1, keepdims=True) + EPS)
    return (y * g.astype(jnp.float32)).astype(x.dtype)

def layer_norm(x, g, b):
    xf = x.astype(jnp.float32)
    mu = jnp.mean(xf, axis=-1, keepdims=True)
    var = jnp.mean(jnp.square(xf - mu), axis=-1, keepdims=True)
    y = (xf - mu) * lax.rsqrt(var + EPS)
    return (y * g.astype(jnp.float32) + b.astype(jnp.float32)).astype(x.dtype)

def rel_bucket(dist):
    max_exact = NUM_BUCKETS // 2
    df = jnp.maximum(dist, 1).astype(jnp.float32)
    large = max_exact + (jnp.log(df / max_exact) / math.log(MAX_DISTANCE / max_exact)
                         * (NUM_BUCKETS - max_exact)).astype(jnp.int32)
    large = jnp.minimum(large, NUM_BUCKETS - 1)
    return jnp.where(dist < max_exact, dist, large)

def rel_bias_lookup(dist, rel_bias):
    return jnp.take(rel_bias, rel_bucket(dist), axis=0).astype(jnp.float32)

def dilated_prompt(q, k, v, rel_bias, window, dilation):
    B, S, H, Dh = q.shape
    nb = window // dilation
    Sp = -(-S // window) * window
    U = Sp // dilation
    nblk = U // nb

    def to_blocks(t):
        t = jnp.pad(t, ((0, 0), (0, Sp - S), (0, 0), (0, 0)))
        t = t.reshape(B, U, dilation, H, Dh).transpose(0, 2, 1, 3, 4)
        return t.reshape(B, dilation, nblk, nb, H, Dh)

    def with_prev(t):
        prev = jnp.concatenate([jnp.zeros_like(t[:, :, :1]), t[:, :, :-1]], axis=2)
        return jnp.concatenate([prev, t], axis=3)

    qb = to_blocks(q)
    kc = with_prev(to_blocks(k))
    vc = with_prev(to_blocks(v))
    i = jnp.arange(nb)[:, None]
    jj = jnp.arange(2 * nb)[None, :]
    delta = nb + i - jj
    blk = jnp.arange(nblk)[:, None, None]
    valid = (delta >= 0) & (delta <= nb) & (blk * nb + jj - nb >= 0)
    bias = rel_bias_lookup(jnp.maximum(delta, 0) * dilation, rel_bias).transpose(2, 0, 1)
    logits = jnp.einsum('brnqhd,brnkhd->brnhqk', qb, kc,
                        preferred_element_type=jnp.float32) * (HEAD_DIM ** -0.5) + bias
    logits = jnp.where(valid[None, None, :, None], logits, -jnp.inf)
    m = jnp.max(logits, axis=-1)
    e = jnp.exp(logits - m[..., None])
    l = jnp.sum(e, axis=-1)
    acc = jnp.einsum('brnhqk,brnkhd->brnqhd', e, vc.astype(jnp.float32))

    def stat_back(s):
        s = s.transpose(0, 1, 2, 4, 3).reshape(B, dilation, U, H).transpose(0, 2, 1, 3)
        return s.reshape(B, Sp, H)[:, :S]

    acc = acc.reshape(B, dilation, U, H, Dh).transpose(0, 2, 1, 3, 4).reshape(B, Sp, H, Dh)[:, :S]
    return stat_back(m), stat_back(l), acc

def dilated_cached(q, k_all, v_all, rel_bias, window, dilation, n_hist):
    T = q.shape[1]
    nb = window // dilation
    j = jnp.arange(nb + 1)
    idx = n_hist + jnp.arange(T)[:, None] - j[None, :] * dilation
    valid = idx >= 0
    idx_c = jnp.maximum(idx, 0)
    kg = k_all[:, idx_c]
    vg = v_all[:, idx_c]
    bias = rel_bias_lookup(j * dilation, rel_bias).T
    logits = jnp.einsum('bthd,btjhd->bthj', q, kg,
                        preferred_element_type=jnp.float32) * (HEAD_DIM ** -0.5) + bias
    logits = jnp.where(valid[None, :, None, :], logits, -jnp.inf)
    m = jnp.max(logits, axis=-1)
    e = jnp.exp(logits - m[..., None])
    l = jnp.sum(e, axis=-1)
    acc = jnp.einsum('bthj,btjhd->bthd', e, vg.astype(jnp.float32))
    return m, l, acc

def combine_dilations(parts):
    ms = jnp.stack([p[0] for p in parts])
    ls = jnp.stack([p[1] for p in parts])
    accs = jnp.stack([p[2] for p in parts])
    w = jnp.exp(ms - jnp.max(ms, axis=0, keepdims=True))
    return jnp.sum(w[..., None] * accs, axis=0) / jnp.sum(w * ls, axis=0)[..., None]

def attend_prompt(q, k, v, rel_bias):
    T = q.shape[1]
    parts = [dilated_prompt(q, k, v, rel_bias, w, d) for (w, d) in DILATED_PATTERNS]
    win = min(WINDOW_MAX, T)
    return combine_dilations(parts), k[:, T - win:], v[:, T - win:]

def attend_sample(q, k, v, cache_k_l, cache_v_l, rel_bias):
    n_hist = cache_k_l.shape[1]
    k_all = jnp.concatenate([cache_k_l, k.astype(cache_k_l.dtype)], axis=1)
    v_all = jnp.concatenate([cache_v_l, v.astype(cache_v_l.dtype)], axis=1)
    parts = [dilated_cached(q, k_all, v_all, rel_bias, w, d, n_hist) for (w, d) in DILATED_PATTERNS]
    return combine_dilations(parts), k_all[:, -n_hist:], v_all[:, -n_hist:]

def block(x, c, attend, conv_hist, norm1_g, norm2_g, w_ada, b_ada, w_in, q_norm_g, k_norm_g,
          conv_dw, conv_dw_b, conv_ln_g, conv_ln_b, w_pw2, w_o, w_ff1, w_ff2):
    B, T, _ = x.shape
    mod = (jax.nn.silu(c) @ w_ada + b_ada)[:, None, :]
    sh1, sc1, g1, sh2, sc2, g2 = jnp.split(mod, N_MOD, axis=-1)
    h = rms_norm(x, norm1_g) * (1 + sc1) + sh1
    z = h @ w_in
    q, k, v, u = jnp.split(z, [ATTN_WIDTH, 2 * ATTN_WIDTH, 3 * ATTN_WIDTH], axis=-1)
    q = rms_norm(q.reshape(B, T, N_ATTN_HEADS, HEAD_DIM), q_norm_g)
    k = rms_norm(k.reshape(B, T, N_ATTN_HEADS, HEAD_DIM), k_norm_g)
    v = v.reshape(B, T, N_ATTN_HEADS, HEAD_DIM)
    o_attn, new_k, new_v = attend(q, k, v)
    glu = u[..., :CONV_WIDTH] * jax.nn.sigmoid(u[..., CONV_WIDTH:])
    conv_in = jnp.concatenate([conv_hist.astype(glu.dtype), glu], axis=1)
    dw = lax.conv_general_dilated(conv_in, conv_dw[:, None, :], window_strides=(1,), padding='VALID',
                                  dimension_numbers=('NWC', 'WIO', 'NWC'),
                                  feature_group_count=CONV_WIDTH) + conv_dw_b
    o_conv = jax.nn.silu(layer_norm(dw, conv_ln_g, conv_ln_b)) @ w_pw2
    mix = jnp.concatenate([o_attn.reshape(B, T, ATTN_WIDTH).astype(x.dtype), o_conv], axis=-1) @ w_o
    x = x + g1 * mix
    h2 = rms_norm(x, norm2_g) * (1 + sc2) + sh2
    x = x + g2 * (jnp.square(jax.nn.relu(h2 @ w_ff1)) @ w_ff2)
    return x, new_k, new_v, conv_in[:, -CONV_HIST:]

def setup_inputs(seed: int = 0) -> dict:
    key = jax.random.key(seed)
    ks = jax.random.split(key, 24)
    f32 = jnp.float32
    winc = min(WINDOW_MAX, PAST_LEN)
    nrm = lambda k, shape, s: s * jax.random.normal(k, shape, f32)
    return {
        "x_prompt": nrm(ks[0], (BATCH, SEQ, D_MODEL), 1.0),
        "x_sample": nrm(ks[1], (DEC_BATCH, DEC_SEQ, D_MODEL), 1.0),
        "cache_k": nrm(ks[2], (DEPTH, DEC_BATCH, winc, N_ATTN_HEADS, HEAD_DIM), 1.0),
        "cache_v": nrm(ks[3], (DEPTH, DEC_BATCH, winc, N_ATTN_HEADS, HEAD_DIM), 1.0),
        "state_conv": nrm(ks[4], (DEPTH, DEC_BATCH, CONV_HIST, CONV_WIDTH), 0.5),
        "c_prompt": nrm(ks[5], (BATCH, D_MODEL), 1.0),
        "c_sample": nrm(ks[6], (DEC_BATCH, D_MODEL), 1.0),
        "rel_bias": nrm(ks[7], (NUM_BUCKETS, N_ATTN_HEADS), 0.5),
        "norm1_g": 1.0 + nrm(ks[8], (DEPTH, D_MODEL), 0.02),
        "norm2_g": 1.0 + nrm(ks[9], (DEPTH, D_MODEL), 0.02),
        "w_ada": nrm(ks[10], (DEPTH, D_MODEL, N_MOD * D_MODEL), 0.5 * D_MODEL ** -0.5),
        "b_ada": nrm(ks[11], (DEPTH, N_MOD * D_MODEL), 0.02),
        "w_in": nrm(ks[12], (DEPTH, D_MODEL, IN_WIDTH), D_MODEL ** -0.5),
        "q_norm_g": 1.0 + nrm(ks[13], (DEPTH, HEAD_DIM), 0.02),
        "k_norm_g": 1.0 + nrm(ks[14], (DEPTH, HEAD_DIM), 0.02),
        "conv_dw": nrm(ks[15], (DEPTH, CONV_KERNEL, CONV_WIDTH), CONV_KERNEL ** -0.5),
        "conv_dw_b": nrm(ks[16], (DEPTH, CONV_WIDTH), 0.02),
        "conv_ln_g": 1.0 + nrm(ks[17], (DEPTH, CONV_WIDTH), 0.02),
        "conv_ln_b": nrm(ks[18], (DEPTH, CONV_WIDTH), 0.02),
        "w_pw2": nrm(ks[19], (DEPTH, CONV_WIDTH, CONV_WIDTH), CONV_WIDTH ** -0.5),
        "w_o": nrm(ks[20], (DEPTH, D_MODEL, D_MODEL), D_MODEL ** -0.5),
        "w_ff1": nrm(ks[21], (DEPTH, D_MODEL, D_FF), D_MODEL ** -0.5),
        "w_ff2": nrm(ks[22], (DEPTH, D_FF, D_MODEL), D_FF ** -0.5),
    }

def reference(x_prompt, x_sample, cache_k, cache_v, state_conv, c_prompt, c_sample, rel_bias,
              norm1_g, norm2_g, w_ada, b_ada, w_in, q_norm_g, k_norm_g, conv_dw, conv_dw_b,
              conv_ln_g, conv_ln_b, w_pw2, w_o, w_ff1, w_ff2):
    xp, xs = x_prompt, x_sample
    kp_l, vp_l, cp_l, ks_l, vs_l, cs_l = [], [], [], [], [], []
    for l in range(DEPTH):
        lw = (norm1_g[l], norm2_g[l], w_ada[l], b_ada[l], w_in[l], q_norm_g[l], k_norm_g[l],
              conv_dw[l], conv_dw_b[l], conv_ln_g[l], conv_ln_b[l], w_pw2[l], w_o[l], w_ff1[l], w_ff2[l])
        hist_p = jnp.zeros((xp.shape[0], CONV_HIST, CONV_WIDTH), xp.dtype)
        xp, kp, vp, cp = block(xp, c_prompt, functools.partial(attend_prompt, rel_bias=rel_bias),
                               hist_p, *lw)
        att_s = functools.partial(attend_sample, cache_k_l=cache_k[l], cache_v_l=cache_v[l],
                                  rel_bias=rel_bias)
        xs, ks_, vs_, cs_ = block(xs, c_sample, att_s, state_conv[l], *lw)
        kp_l.append(kp); vp_l.append(vp); cp_l.append(cp)
        ks_l.append(ks_); vs_l.append(vs_); cs_l.append(cs_)
    return (xp, xs, jnp.stack(kp_l), jnp.stack(vp_l), jnp.stack(cp_l),
            jnp.stack(ks_l), jnp.stack(vs_l), jnp.stack(cs_l))


_drawn_inputs = setup_inputs


def setup_inputs(seed=0):
    import zlib

    import numpy as np

    out = dict(_drawn_inputs(seed))
    spreads = {}
    factors = {'rel_bias': 4.233,
     'norm1_g': 2.864,
     'norm2_g': 6.217,
     'q_norm_g': 30.769,
     'k_norm_g': 8.587,
     'conv_dw_b': 8.0,
     'conv_ln_g': 27.521,
     'conv_ln_b': 70.684}
    for name, (base, spread) in spreads.items():
        noise = np.random.default_rng([zlib.crc32(name.encode()), seed]).standard_normal(out[name].shape)
        drawn = base * np.exp(spread * noise) if base else spread * noise
        out[name] = jnp.asarray(drawn.astype(out[name].dtype))
    for name, factor in factors.items():
        out[name] = (out[name] * factor).astype(out[name].dtype)
    return out
```

```python
from contextlib import ExitStack

import numpy as np

import concourse.bass as bass
from concourse import mybir

F32 = mybir.dt.float32
F32R = mybir.dt.float32r
U32 = mybir.dt.uint32
I32 = mybir.dt.int32
ALU = mybir.AluOpType
ACT = mybir.ActivationFunctionType
AX = mybir.AxisListType

P = 128
D = 1024
KT = D // P
SEQ = 2048
NT = SEQ // P
DB, DS = 8, 4
NS = DB * DS
WINC = 2048
H, DH = 8, 64
AW = H * DH
CW = 512
CC = CW // P
TAPS = 31
HIST = TAPS - 1
IN_W = 3 * AW + 2 * CW
FF = 4 * D
NMOD = 6 * D
NB = 128
PATTERNS = ((128, 1), (512, 4), (2048, 16))
BUCKETS = 32
MAXD = 2048
EPS = 1e-6
NEG = -1.0e30
MAGIC = 0x5F3759DF
TOK = SEQ + NS
V_N1, V_N2, V_CB, V_LG, V_LB, V_ALL = 0, 8, 16, 20, 24, 28
M_SH1, M_SC1, M_SH2, M_SC2, M_G2, M_ALL = 0, 8, 16, 24, 32, 40
M_SRC = (0, 1, 3, 4, 5)
SKEYS = 4 * P + 4 * P + DS
RW = 384


def rows_of(i):
    return P if i < NT else NS


def rel_bucket(dist):
    exact = BUCKETS // 2
    df = np.maximum(dist, 1).astype(np.float32)
    scale = np.float32(np.log(MAXD / exact))
    large = exact + (np.log(df / np.float32(exact)) / scale * np.float32(BUCKETS - exact)).astype(np.int32)
    return np.where(dist < exact, dist, np.minimum(large, BUCKETS - 1))


def shape_constants():
    hot_p = np.zeros((BUCKETS + 1, 3, RW), np.float32)
    for p, (_, d) in enumerate(PATTERNS):
        delta = 2 * NB - 1 - np.arange(RW)
        ok = (delta >= 0) & (delta <= NB)
        b = rel_bucket(np.maximum(delta, 0) * d)
        for y in range(RW):
            if ok[y]:
                hot_p[b[y], p, y] = -1.0
            else:
                hot_p[BUCKETS, p, y] = -NEG
    hot_s = np.zeros((DS, BUCKETS, 3, SKEYS), np.float32)
    out_s = np.zeros((DS, 3, SKEYS), np.float32)
    for t in range(DS):
        for col in range(SKEYS):
            if col < 512:
                kind, dist = 0, 512 + t - 4 * (col % 128) - col // 128
            elif col < 1024:
                kind, dist = 1, WINC + t - 16 * (col % 128) - (col - 512) // 128
            else:
                kind, dist = 2, t - (col - 1024)
            for p, (w, d) in enumerate(PATTERNS):
                ok = 0 <= dist <= w and dist % d == 0
                ok = ok and (kind == 2 or (kind == 1) == (p == 2))
                if ok:
                    hot_s[t, int(rel_bucket(np.array(dist))), p, col] = -1.0
                else:
                    out_s[t, p, col] = -NEG
    sel_t = np.zeros((DS, P), np.float32)
    for t in range(DS):
        sel_t[t, t::DS] = 1.0
    own_t = np.repeat(np.eye(DS, dtype=np.float32), BUCKETS, axis=0)
    return {"hot_p": hot_p.reshape(BUCKETS + 1, -1), "hot_s": hot_s.reshape(P, -1),
            "out_s": out_s.reshape(DS, -1), "sel_t": sel_t, "own_t": own_t,
            "mask_h": np.tile(np.repeat(np.eye(H, dtype=np.float32), DS, axis=0), (P // NS, 1))}


def build(nc, I, O):
    scratch = {}

    def dram(name, shape):
        scratch[name] = nc.dram_tensor(name, shape, F32, kind="Internal").ap()
        return scratch[name]

    mod_d = dram("mod_d", (9, NMOD))
    bias_d = dram("bias_d", (H, P, 3 * RW))
    sbias_d = dram("sbias_d", (P, 3 * SKEYS))
    qt_d = dram("qt_d", (P, 4, TOK))
    kt_d = dram("kt_d", (P, 4, TOK))
    acc_d = dram("acc_d", (3, SEQ, AW))
    st_d = dram("st_d", (3, SEQ, 2 * H))
    os_d = dram("os_d", (NS, AW))
    dw_d = dram("dw_d", (P, CC, TOK))
    x1_d = dram("x1_d", (TOK, D))
    h2_d = dram("h2_d", (P, KT, TOK))

    whole = ExitStack()
    with whole:
        stage_sems = []

        def sem(name):
            stage_sems.append(nc.alloc_semaphore(name=name))
            return stage_sems[-1]

        def end_stage():
            nc.clear_and_free_semaphores(list(stage_sems))
            stage_sems.clear()
            nc.all_engine_barrier()

        def keep(name, shape, dt=F32):
            return whole.enter_context(nc.sbuf_tensor(name, shape, dt))

        ident = keep("ident", [P, P])
        modT = keep("modT", [P, M_ALL, 9])
        vecT = keep("vecT", [P, V_ALL])
        tapT = keep("tapT", [P, TAPS * CC])
        gain1 = keep("gain1", [P, KT, 9])
        gain2 = keep("gain2", [P, KT, 9])
        rstd1 = keep("rstd1", [P, NT + 1])
        STORES = ("copied", "v_out0", "v_out1", "k_out0", "k_out1", "tail_out", "y_out00", "y_out01", "y_out10", "y_out11")
        stored = {name: whole.enter_context(nc.semaphore(name)) for name in STORES}
        copied = stored["copied"]

        def copy_cache(eng, n):
            b = n // 2
            for name, out in ((("cache_k", "new_k_sample"), ("cache_v", "new_v_sample"))[n % 2],):
                src = I[name][0, b].rearrange("r h d -> (r h d)")[DS * AW:WINC * AW]
                dst = O[out][0, b].rearrange("r h d -> (r h d)")[0:(WINC - DS) * AW]
                eng.dma_start(dst.rearrange("(a n) -> a n", a=16), src.rearrange("(a n) -> a n", a=16)).then_inc(copied, 16)

        class Chain:

            def __init__(self, eng, s):
                self.eng, self.s, self.n = eng, s, 0

            def __call__(self, ins):
                self.n += 1
                ins.then_inc(self.s, 1)
                self.eng.wait_ge(self.s, self.n)

            def mark(self, ins):
                self.n += 1
                ins.then_inc(self.s, 1)
                return self.n

            def need(self, n):
                if n > 0:
                    self.eng.wait_ge(self.s, n)

        def rsqrt(v, step, y, a, t):
            step(v.tensor_scalar(t.bitcast(U32), a.bitcast(U32), 1, None, ALU.logical_shift_right))
            step(v.tensor_scalar(y.bitcast(I32), t.bitcast(I32), -1.0, float(MAGIC), ALU.mult, ALU.add))
            for _ in range(4):
                step(v.tensor_tensor(t, y, y, ALU.mult))
                step(v.tensor_tensor(t, t, a, ALU.mult))
                step(v.tensor_scalar(t, t, -0.5, 1.5, ALU.mult, ALU.add))
                step(v.tensor_tensor(y, y, t, ALU.mult))

        with ExitStack() as st:
            def sb(name, shape, dt=F32):
                return st.enter_context(nc.sbuf_tensor(name, shape, dt))

            def ps(name, shape, dt=F32):
                return st.enter_context(nc.psum_tensor(name, shape, dt))

            NW = 3
            WC = NMOD // 512
            c_sb = sb("c_sb", [9, D])
            sig_c = sb("sig_c", [9, D])
            silu_c = sb("silu_c", [9, D])
            cT = sb("cT", [P, KT, 9])
            w_ring = sb("w_ring", [P, NW, KT, 512])
            b_rows = sb("b_rows", [9, NMOD])
            mod = sb("mod", [9, NMOD])
            vecs = sb("vecs", [V_ALL, P])
            taps = sb("taps", [TAPS * CC, P])
            x_st = sb("x_st", [P, 2, D])
            x_sq = sb("x_sq", [P, D])
            ssq = sb("ssq", [P, NT + 1])
            rs_t = sb("rs_t", [P, NT + 1])
            rel33 = sb("rel33", [BUCKETS + 1, H])
            relB = sb("relB", [BUCKETS + 1, H, P])
            relS = sb("relS", [P, H])
            ownT = sb("ownT", [P, DS])
            selT = sb("selT", [DS, P])
            pairE = sb("pairE", [P, 4, H, DS])
            hotP = sb("hotP", [BUCKETS + 1, 3 * RW])
            hotS = sb("hotS", [P, 3 * SKEYS])
            outS = sb("outS", [DS, 3 * SKEYS])
            biasB = sb("biasB", [P, 2, 3 * RW])
            biasS = sb("biasS", [P, 3 * SKEYS])
            cT_ps = ps("cT_ps", [P, 512])
            mod_ps = [ps(f"mod_ps{i}", [P, 512]) for i in range(2)]
            vec_ps = ps("vec_ps", [P, 512])
            tb_ps = [ps(f"tb_ps{i}", [P, 512]) for i in range(2)]
            modT_ps = ps("modT_ps", [P, 512])
            id_zero, id_done = sem("id_zero"), sem("id_done")
            c_in, sig_done, silu_done, cT_pe, cT_done = sem("c_in"), sem("sig_done"), sem("silu_done"), sem("cT_pe"), sem("cT_done")
            w_in_ = [sem(f"wada_in{i}") for i in range(NW)]
            small_in, mod_pe, mod_done = sem("small_in"), sem("mod_pe"), sem("mod_done")
            vec_pe, vec_done, modT_pe, modT_done = sem("vec_pe"), sem("vec_done"), sem("modT_pe"), sem("modT_done")
            xs_in = [sem("xs_in0"), sem("xs_in1")]
            sq_done = sem("sq_done")
            rel_ready, tb_pe, tb_done, mod_out, v0 = sem("rel_ready"), sem("tb_pe"), sem("tb_done"), sem("mod_out"), sem("v0")
            tb_out = [sem("tb_out0"), sem("tb_out1")]
            TBN = 3 * H + 9
            SMALL = 15

            with nc.Block() as block:
                @block.gpsimd
                def _(pool):
                    pool.memset(ident[:], 0.0).then_inc(id_zero, 1)
                    pool.wait_ge(id_zero, 1)
                    pool.affine_select(out=ident[:], in_=ident[:], compare_op=ALU.not_equal, fill=1.0, base=0,
                                       pattern=[[-1, P]], channel_multiplier=1).then_inc(id_done, 1)
                    copy_cache(pool, 0)
                    pool.wait_ge(id_done, 1)

                @block.sync
                def _(sp):
                    sp.dma_start(c_sb[8:9, :], I["c_prompt"]).then_inc(c_in, 16)
                    sp.dma_start(c_sb[0:8, :], I["c_sample"]).then_inc(c_in, 16)
                    w_view = I["w_ada"][0].rearrange("(k p) n -> p k n", p=P)
                    for n in range(WC):
                        if n >= NW:
                            sp.wait_ge(mod_pe, n - NW + 1)
                        sp.dma_start(w_ring[:, n % NW], w_view[:, :, n * 512:(n + 1) * 512]).then_inc(w_in_[n % NW], 16)
                    sp.wait_ge(mod_done, WC)
                    sp.dma_start(mod_d, mod[:]).then_inc(mod_out, 16)
                    sp.wait_ge(mod_out, 16)

                @block.scalar
                def _(act):
                    small = [(vecs[V_N1:V_N1 + 8, :], I["norm1_g"][0].rearrange("(k p) -> k p", p=P)),
                             (vecs[V_N2:V_N2 + 8, :], I["norm2_g"][0].rearrange("(k p) -> k p", p=P)),
                             (vecs[V_CB:V_CB + 4, :], I["conv_dw_b"][0].rearrange("(k p) -> k p", p=P)),
                             (vecs[V_LG:V_LG + 4, :], I["conv_ln_g"][0].rearrange("(k p) -> k p", p=P)),
                             (vecs[V_LB:V_LB + 4, :], I["conv_ln_b"][0].rearrange("(k p) -> k p", p=P)),
                             (taps[:], I["conv_dw"][0].rearrange("j (k p) -> (j k) p", p=P)),
                             (rel33[0:BUCKETS, :], I["rel_bias"]),
                             (hotP[:], I["hot_p"]), (hotS[:], I["hot_s"]), (outS[:], I["out_s"]),
                             (ownT[:], I["own_t"]), (selT[:], I["sel_t"])]
                    for t in range(2):
                        small.append((relS[64 * t:64 * t + 32, :], I["rel_bias"]))
                        small.append((relS[64 * t + 32:64 * t + 64, :], I["rel_bias"]))
                    small.append((b_rows[:], I["b_ada"].to_broadcast([9, NMOD])))
                    for dst, src in small:
                        act.dma_start(dst, src).then_inc(small_in, 16)
                    assert len(small) == SMALL + 2
                    act.wait_ge(c_in, 32)
                    act.activation(sig_c[:], c_sb[:], ACT.Sigmoid).then_inc(sig_done, 1)
                    for i in range(NT + 1):
                        n = rows_of(i)
                        if i >= 2:
                            act.wait_ge(sq_done, i - 1)
                        src = I["x_prompt"][0, i * P:(i + 1) * P, :] if i < NT else I["x_sample"].rearrange("b t d -> (b t) d")
                        act.dma_start(x_st[0:n, i % 2], src).then_inc(xs_in[i % 2], 16)
                        if i >= 1:
                            m = rows_of(i - 1)
                            act.wait_ge(xs_in[(i - 1) % 2], 16 * ((i - 1) // 2 + 1))
                            if i >= 2:
                                act.wait_ge(sq_done, i - 1)
                            else:
                                act.wait_ge(v0, 1)
                            act.activation(x_sq[0:m], x_st[0:m, (i - 1) % 2], ACT.Square,
                                           accum_out=ssq[0:m, i - 1:i]).then_inc(sq_done, 1)
                    act.wait_ge(xs_in[0], 16 * 9)
                    act.wait_ge(sq_done, NT)
                    act.activation(x_sq[0:NS], x_st[0:NS, 0], ACT.Square, accum_out=ssq[0:NS, NT:NT + 1]).then_inc(sq_done, 1)
                    for h in range(H):
                        act.wait_ge(tb_done, 3 * h + 3)
                        act.dma_start(bias_d[h], biasB[:, h % 2]).then_inc(tb_out[h % 2], 16)
                    act.wait_ge(tb_done, TBN)
                    act.dma_start(sbias_d, biasS[:]).then_inc(tb_out[0], 16)
                    act.wait_ge(tb_out[0], 16 * (H // 2 + 1))
                    act.wait_ge(tb_out[1], 16 * (H // 2))

                @block.tensor
                def _(pe):
                    pe.wait_ge(id_done, 1)
                    pe.wait_ge(silu_done, 1)
                    for k in range(KT):
                        mm = pe.transpose(cT_ps[:, k * 9:(k + 1) * 9], silu_c[:, k * P:(k + 1) * P], ident[0:9, 0:9])
                    mm.then_inc(cT_pe, 1)
                    pe.wait_ge(small_in, 16 * (SMALL + 2))
                    pe.transpose(vec_ps[:, 0:V_ALL], vecs[:], ident[0:V_ALL, 0:V_ALL])
                    pe.transpose(vec_ps[:, 128:128 + TAPS * CC], taps[:], ident[0:TAPS * CC, 0:TAPS * CC]).then_inc(vec_pe, 1)
                    pe.wait_ge(cT_done, 1)

                    def tables(g):
                        if g >= 2:
                            pe.wait_ge(tb_done, g - 1)
                        pe.wait_ge(rel_ready, 1)
                        if g < 3 * H:
                            h, p = divmod(g, 3)
                            pe.matmul(tb_ps[g % 2][:, 0:RW], relB[:, h, :], hotP[:, p * RW:(p + 1) * RW],
                                      start=True, stop=True).then_inc(tb_pe, 1)
                        else:
                            lo = (g - 3 * H) * 344
                            hi = min(lo + 344, 3 * SKEYS)
                            pe.matmul(tb_ps[g % 2][:, 0:hi - lo], pairE[:].rearrange("p b h t -> p (b h t)"), hotS[:, lo:hi], start=True, stop=False)
                            pe.matmul(tb_ps[g % 2][:, 0:hi - lo], selT[:], outS[:, lo:hi],
                                      start=False, stop=True).then_inc(tb_pe, 1)

                    g = 0
                    for n in range(WC):
                        pe.wait_ge(w_in_[n % NW], 16 * (n // NW + 1))
                        if n >= 2:
                            pe.wait_ge(mod_done, n - 1)
                        for k in range(KT):
                            mm = pe.matmul(mod_ps[n % 2][0:9, :], cT[:, k, :], w_ring[:, n % NW, k, :], start=k == 0, stop=k == KT - 1)
                        mm.then_inc(mod_pe, 1)
                        for _ in range(3):
                            if g < TBN:
                                tables(g)
                                g += 1
                    while g < TBN:
                        tables(g)
                        g += 1
                    pe.wait_ge(mod_done, WC)
                    for j in range(M_ALL):
                        c0 = M_SRC[j // 8] * D + (j % 8) * P
                        mm = pe.transpose(modT_ps[:, j * 9:(j + 1) * 9], mod[:, c0:c0 + P], ident[0:9, 0:9])
                    mm.then_inc(modT_pe, 1)

                @block.vector
                def _(v):
                    step = Chain(v, v0)
                    step(v.memset(ssq[:], 1.0))
                    v.wait_ge(small_in, 16 * (SMALL + 2))
                    step(v.memset(rel33[BUCKETS:BUCKETS + 1, :], 1.0))
                    v.tensor_copy(relB[:], rel33[:].unsqueeze(2).to_broadcast([BUCKETS + 1, H, P]))
                    for t in range(DS):
                        ins = v.tensor_scalar(pairE[:, :, :, t], relS[:].unsqueeze(1).to_broadcast([P, 4, H]), ownT[:, t:t + 1], None, ALU.mult)
                    step(ins)
                    v.sem_inc(rel_ready, 1)
                    v.wait_ge(sig_done, 1)
                    v.tensor_tensor(silu_c[:], c_sb[:], sig_c[:], ALU.mult).then_inc(silu_done, 1)
                    v.wait_ge(cT_pe, 1)
                    v.tensor_copy(cT[:].rearrange("p k b -> p (k b)"), cT_ps[:, 0:KT * 9]).then_inc(cT_done, 1)
                    v.wait_ge(vec_pe, 1)
                    v.tensor_copy(vecT[:], vec_ps[:, 0:V_ALL])
                    step(v.tensor_copy(tapT[:], vec_ps[:, 128:128 + TAPS * CC]))

                    def table_copy(g):
                        v.wait_ge(tb_pe, g + 1)
                        if g < 3 * H:
                            h, p = divmod(g, 3)
                            if h >= 2:
                                v.wait_ge(tb_out[h % 2], 16 * (h // 2))
                            v.tensor_copy(biasB[:, h % 2, p * RW:(p + 1) * RW], tb_ps[g % 2][:, 0:RW]).then_inc(tb_done, 1)
                        else:
                            lo = (g - 3 * H) * 344
                            hi = min(lo + 344, 3 * SKEYS)
                            v.tensor_copy(biasS[:, lo:hi], tb_ps[g % 2][:, 0:hi - lo]).then_inc(tb_done, 1)

                    g = 0
                    for n in range(WC):
                        v.wait_ge(mod_pe, n + 1)
                        v.tensor_tensor(mod[:, n * 512:(n + 1) * 512], mod_ps[n % 2][0:9, :],
                                        b_rows[:, n * 512:(n + 1) * 512], ALU.add).then_inc(mod_done, 1)
                        for _ in range(3):
                            if g < TBN:
                                table_copy(g)
                                g += 1
                    while g < TBN:
                        table_copy(g)
                        g += 1
                    v.wait_ge(sq_done, NT + 1)
                    step(v.tensor_scalar(ssq[:], ssq[:], 1.0 / D, EPS, ALU.mult, ALU.add))
                    rsqrt(v, step, rstd1[:], ssq[:], rs_t[:])
                    v.wait_ge(modT_pe, 1)
                    step(v.tensor_copy(modT[:].rearrange("p j b -> p (j b)"), modT_ps[:, 0:M_ALL * 9]))
                    for gain, m0, g0 in ((gain1, M_SC1, V_N1), (gain2, M_SC2, V_N2)):
                        step(v.scalar_tensor_tensor(out=gain[:], in0=modT[:, m0:m0 + 8, :], scalar=1.0,
                                                    in1=vecT[:, g0:g0 + 8].unsqueeze(2).to_broadcast([P, KT, 9]),
                                                    op0=ALU.add, op1=ALU.mult))

        end_stage()

        def projection(tag, col0, ncols, body):
            st = ExitStack()
            with st:
                def sb(name, shape, dt=F32):
                    return st.enter_context(nc.sbuf_tensor(tag + name, shape, dt))

                def ps(name, shape, dt=F32):
                    return st.enter_context(nc.psum_tensor(tag + name, shape, dt))

                def sm(name):
                    return sem(tag + name)

                NC = ncols // 512
                w_raw = sb("w_raw", [P, 2, ncols])
                w_hi = sb("w_hi", [P, KT, ncols], F32R)
                w_lo = sb("w_lo", [P, KT, ncols], F32R)
                x_in = sb("x_in", [P, 2, D])
                x_nrm = sb("x_nrm", [P, D])
                h_full = sb("h_full", [P, KT, P])
                h_hi = sb("h_hi", [P, 2, KT, P], F32R)
                h_lo = sb("h_lo", [P, 2, KT, P], F32R)
                xt_ps = ps("xt_ps", [P, KT, P])
                z_ps = [ps(f"z_ps{i}", [P, 512]) for i in range(4)]
                w_ld = [sm("w_ld0"), sm("w_ld1")]
                w_hid, w_lod = sm("w_hi_done"), sm("w_lo_done")
                x_ld = [sm("x_ld0"), sm("x_ld1")]
                x_nrmd, xt_pe, h_done, hi_done, lo_done = sm("x_nrm_done"), sm("xt_pe"), sm("h_done"), sm("hi_done"), sm("lo_done")
                z_pe, hv = sm("z_pe"), sm("hv")

                def load_w(sp):
                    for k in range(KT):
                        if k >= 2:
                            sp.wait_ge(w_lod, k - 1)
                        sp.dma_start(w_raw[:, k % 2], I["w_in"][0, k * P:(k + 1) * P, col0:col0 + ncols]).then_inc(w_ld[k % 2], 16)

                def load_x(sp, i):
                    if i >= 2:
                        sp.wait_ge(x_nrmd, i - 1)
                    src = I["x_prompt"][0, i * P:(i + 1) * P, :] if i < NT else I["x_sample"].rearrange("b t d -> (b t) d")
                    sp.dma_start(x_in[0:rows_of(i), i % 2], src).then_inc(x_ld[i % 2], 16)

                def split_w_hi(act):
                    for k in range(KT):
                        act.wait_ge(w_ld[k % 2], 16 * (k // 2 + 1))
                        act.activation(w_hi[:, k], w_raw[:, k % 2], ACT.Copy).then_inc(w_hid, 1)

                def split_w_lo(v):
                    for k in range(KT):
                        v.wait_ge(w_hid, k + 1)
                        v.tensor_tensor(w_lo[:, k], w_raw[:, k % 2], w_hi[:, k].bitcast(F32), ALU.subtract).then_inc(w_lod, 1)

                def norm_x(pool, i):
                    n = rows_of(i)
                    pool.wait_ge(x_ld[i % 2], 16 * (i // 2 + 1))
                    if i >= 1:
                        pool.wait_ge(xt_pe, i)
                    pool.tensor_scalar(x_nrm[0:n], x_in[0:n, i % 2], rstd1[0:n, i:i + 1], None, ALU.mult).then_inc(x_nrmd, 1)

                def turn_x(pe, i):
                    n = rows_of(i)
                    pe.wait_ge(x_nrmd, i + 1)
                    if i >= 1:
                        pe.wait_ge(h_done, i)
                    for k in range(KT):
                        mm = pe.transpose(xt_ps[:, k, 0:n], x_nrm[0:n, k * P:(k + 1) * P], ident[0:n, 0:n])
                    mm.then_inc(xt_pe, 1)

                def modulate(act, i):
                    act.wait_ge(xt_pe, i + 1)
                    if i >= 1:
                        act.wait_ge(lo_done, i)
                    for k in range(KT):
                        ins = act.activation(h_full[:, k, :], xt_ps[:, k, :], ACT.Identity,
                                             bias=modT[:, M_SH1 + k, 8:9], scale=gain1[:, k, 8:9])
                    ins.then_inc(h_done, 1)

                def modulate_sample(v, step):
                    v.wait_ge(xt_pe, NT + 1)
                    v.wait_ge(lo_done, NT)
                    for k in range(KT):
                        view = h_full[:, k, 0:NS].rearrange("p (b t) -> p b t", t=DS)
                        step(v.tensor_tensor(view, xt_ps[:, k, 0:NS].rearrange("p (b t) -> p b t", t=DS),
                                             gain1[:, k, 0:DB].unsqueeze(2).to_broadcast([P, DB, DS]), ALU.mult))
                        ins = v.tensor_tensor(view, view, modT[:, M_SH1 + k, 0:DB].unsqueeze(2).to_broadcast([P, DB, DS]), ALU.add)
                    ins.then_inc(h_done, 1)

                def split_hi(act, i):
                    n = rows_of(i)
                    act.wait_ge(h_done, i + 1)
                    if i >= 2:
                        act.wait_ge(z_pe, NC * (i - 1))
                    act.activation(h_hi[:, i % 2, :, 0:n], h_full[:, :, 0:n], ACT.Copy).then_inc(hi_done, 1)

                def split_lo(pool, i):
                    n = rows_of(i)
                    pool.wait_ge(hi_done, i + 1)
                    if i >= 2:
                        pool.wait_ge(z_pe, NC * (i - 1))
                    pool.tensor_tensor(h_lo[:, i % 2, :, 0:n], h_full[:, :, 0:n], h_hi[:, i % 2, :, 0:n].bitcast(F32),
                                       ALU.subtract).then_inc(lo_done, 1)

                def products(pe, i, bank_free):
                    n = rows_of(i)
                    pe.wait_ge(lo_done, i + 1)
                    for c in range(NC):
                        g = NC * i + c
                        if g >= 4:
                            bank_free(g - 4)
                        z = z_ps[g % 4][0:n, :]
                        for k in range(KT):
                            if i == 0 and c == 0:
                                pe.wait_ge(w_lod, k + 1)
                            hi, lo = h_hi[:, i % 2, k, 0:n], h_lo[:, i % 2, k, 0:n]
                            cols = slice(c * 512, (c + 1) * 512)
                            pe.matmul(z, hi, w_hi[:, k, cols], start=k == 0, stop=False)
                            pe.matmul(z, hi, w_lo[:, k, cols], start=False, stop=False)
                            mm = pe.matmul(z, lo, w_hi[:, k, cols], start=False, stop=k == KT - 1)
                        mm.then_inc(z_pe, 1)

                body(dict(sb=sb, ps=ps, sm=sm, z_ps=z_ps, z_pe=z_pe, hv=hv, load_w=load_w, load_x=load_x,
                                     split_w_hi=split_w_hi, split_w_lo=split_w_lo, norm_x=norm_x, turn_x=turn_x,
                                     modulate=modulate, modulate_sample=modulate_sample, split_hi=split_hi,
                                     split_lo=split_lo, products=products))

        conv = ExitStack()
        with conv:
            gluT = conv.enter_context(nc.sbuf_tensor("gluT", [P, CC, HIST + SEQ], F32))
            gluS = conv.enter_context(nc.sbuf_tensor("gluS", [P, CC, DB, HIST + DS], F32))

            def values_and_gates(f):
                sm = f["sm"]
                v_sb = f["sb"]("v_sb", [P, 2, AW])
                gate = f["sb"]("gate", [P, 2, CW])
                glu = f["sb"]("glu", [P, 2, CW])
                hist = f["sb"]("hist", [120, 2, CW])
                g_ps = f["ps"]("g_ps", [P, CC, P])
                v_done, gate_done, glu_done = sm("v_done"), sm("gate_done"), sm("glu_done")
                g_pe, g_out, v_out = sm("g_pe"), sm("g_out"), [stored["v_out0"], stored["v_out1"]]
                tail_out, hist_in, hist_pe, hist_cp = stored["tail_out"], sm("hist_in"), sm("hist_pe"), sm("hist_cp")
                z_ps, z_pe = f["z_ps"], f["z_pe"]
                with nc.Block() as block:
                    @block.sync
                    def _(sp):
                        f["load_x"](sp, 0)
                        f["load_x"](sp, 1)
                        sp.dma_start(hist[:], I["state_conv"][0].rearrange("(a b) t c -> (b t) a c", a=2)).then_inc(hist_in, 16)
                        f["load_w"](sp)
                        sp.dma_start(O["new_conv_sample"][0, :, 0:HIST - DS, :], I["state_conv"][0, :, DS:HIST, :]).then_inc(tail_out, 16)
                        for i in range(NT + 1):
                            if i + 2 <= NT:
                                f["load_x"](sp, i + 2)
                            sp.wait_ge(v_done, i + 1)
                            if i < NT:
                                sp.dma_start(O["new_v_prompt"][0, 0, i * P:(i + 1) * P].rearrange("t h d -> t (h d)"),
                                             v_sb[:, i % 2]).then_inc(v_out[i % 2], 16)
                            else:
                                for b in range(DB):
                                    sp.dma_start(O["new_v_sample"][0, b, WINC - DS:WINC].rearrange("t h d -> t (h d)"),
                                                 v_sb[DS * b:DS * b + DS, i % 2]).then_inc(v_out[i % 2], 16)
                            if i == NT - 1:
                                sp.wait_ge(glu_done, NT)
                                sp.dma_start(O["new_conv_prompt"][0, 0], glu[P - HIST:P, i % 2]).then_inc(tail_out, 16)
                        sp.wait_ge(glu_done, NT + 1)
                        for b in range(DB):
                            sp.dma_start(O["new_conv_sample"][0, b, HIST - DS:HIST, :],
                                         glu[DS * b:DS * b + DS, NT % 2]).then_inc(tail_out, 16)
                        sp.wait_ge(tail_out, 16 * (2 + DB))
                        sp.wait_ge(v_out[0], 16 * (8 + DB))
                        sp.wait_ge(v_out[1], 16 * 8)

                    @block.gpsimd
                    def _(pool):
                        copy_cache(pool, 1)
                        copy_cache(pool, 2)
                        f["norm_x"](pool, 0)
                        for i in range(NT + 1):
                            f["split_lo"](pool, i)
                            if i < NT:
                                f["norm_x"](pool, i + 1)

                    @block.scalar
                    def _(act):
                        f["split_w_hi"](act)
                        f["modulate"](act, 0)
                        f["split_hi"](act, 0)
                        for i in range(NT + 1):
                            n = rows_of(i)
                            if i + 1 < NT:
                                f["modulate"](act, i + 1)
                            if i + 1 <= NT:
                                f["split_hi"](act, i + 1)
                            if i >= 2:
                                act.wait_ge(v_out[i % 2], 16 * (i // 2))
                            act.wait_ge(z_pe, 3 * i + 1)
                            act.activation(v_sb[0:n, i % 2], z_ps[(3 * i) % 4][0:n], ACT.Copy).then_inc(v_done, 1)
                            act.wait_ge(z_pe, 3 * i + 3)
                            if i >= 2:
                                act.wait_ge(glu_done, i - 1)
                            act.activation(gate[0:n, i % 2], z_ps[(3 * i + 2) % 4][0:n], ACT.Sigmoid).then_inc(gate_done, 1)

                    @block.vector
                    def _(v):
                        step = Chain(v, f["hv"])
                        f["split_w_lo"](v)
                        v.memset(gluT[:, :, 0:HIST], 0.0)
                        for a in range(2):
                            v.wait_ge(hist_pe, a + 1)
                            for c in range(CC):
                                ins = v.tensor_copy(gluS[:, c, 4 * a:4 * a + 4, 0:HIST],
                                                    g_ps[:, c, 0:120].rearrange("p (b t) -> p b t", t=HIST))
                            ins.then_inc(hist_cp, 1)
                        for i in range(NT + 1):
                            n = rows_of(i)
                            if i == NT - 1:
                                f["modulate_sample"](v, step)
                            v.wait_ge(gate_done, i + 1)
                            v.wait_ge(v_done, i + 1)
                            if i >= 2:
                                v.wait_ge(g_pe, i - 1)
                            if i == NT:
                                v.wait_ge(g_pe, NT)
                            v.tensor_tensor(glu[0:n, i % 2], z_ps[(3 * i + 1) % 4][0:n], gate[0:n, i % 2], ALU.mult).then_inc(glu_done, 1)
                            v.wait_ge(g_pe, i + 1)
                            if i < NT:
                                v.tensor_copy(gluT[:, :, HIST + i * P:HIST + (i + 1) * P], g_ps[:]).then_inc(g_out, 1)
                            else:
                                for c in range(CC):
                                    ins = v.tensor_copy(gluS[:, c, :, HIST:HIST + DS], g_ps[:, c, 0:NS].rearrange("p (b t) -> p b t", t=DS))
                                ins.then_inc(g_out, 1)

                    @block.tensor
                    def _(pe):
                        def turn_glu(i):
                            n = rows_of(i)
                            pe.wait_ge(glu_done, i + 1)
                            if i >= 1:
                                pe.wait_ge(g_out, i)
                            for c in range(CC):
                                mm = pe.transpose(g_ps[:, c, 0:n], glu[0:n, i % 2, c * P:(c + 1) * P], ident[0:n, 0:n])
                            mm.then_inc(g_pe, 1)

                        f["turn_x"](pe, 0)
                        pe.wait_ge(hist_in, 16)
                        for a in range(2):
                            if a == 1:
                                pe.wait_ge(hist_cp, 1)
                            for c in range(CC):
                                mm = pe.transpose(g_ps[:, c, 0:120], hist[:, a, c * P:(c + 1) * P], ident[0:120, 0:120])
                            mm.then_inc(hist_pe, 1)
                        pe.wait_ge(hist_cp, 2)
                        for i in range(NT + 1):
                            if i < NT:
                                f["turn_x"](pe, i + 1)
                            f["products"](pe, i, lambda g: pe.wait_ge(glu_done, g // 3 + 1))
                            if i >= 1:
                                turn_glu(i - 1)
                        turn_glu(NT)

            projection("vu_", 2 * AW, AW + 2 * CW, values_and_gates)
            end_stage()

            def queries_and_keys(f):
                sm = f["sm"]
                raw = f["sb"]("raw", [P, 2, 2 * AW])
                sqr = f["sb"]("sqr", [P, 2 * AW])
                nrm = f["sb"]("nrm", [P, 2, 2 * AW])
                gains = f["sb"]("gains", [P, 2, DH])
                ssq = f["sb"]("ssq", [P, 2 * H])
                rsq = f["sb"]("rsq", [P, 2, 2 * H])
                tmp = f["sb"]("tmp", [P, 2 * H])
                qkT = f["sb"]("qkT", [P, 2, 2, 4, P])
                t_ps = f["ps"]("t_ps", [P, 2, 4, P])
                dwT = f["sb"]("dwT", [P, SEQ])
                dwS = f["sb"]("dwS", [P, CC, NS])
                gain_in, gain_set, raw_done, rs_done = sm("gain_in"), sm("gain_set"), sm("raw_done"), sm("rs_done")
                nrm_half, nrm_done, t_pe, t_done = sm("nrm_half"), sm("nrm_done"), sm("t_pe"), sm("t_done")
                k_out, t_out = [stored["k_out0"], stored["k_out1"]], [sm("t_out0"), sm("t_out1")]
                dw_done, dw_out = sm("dw_done"), sm("dw_out")
                z_ps, z_pe = f["z_ps"], f["z_pe"]
                with nc.Block() as block:
                    @block.sync
                    def _(sp):
                        f["load_x"](sp, 0)
                        f["load_x"](sp, 1)
                        sp.dma_start(gains[:, 0, :], I["q_norm_g"].to_broadcast([P, DH])).then_inc(gain_in, 16)
                        sp.dma_start(gains[:, 1, :], I["k_norm_g"].to_broadcast([P, DH])).then_inc(gain_in, 16)
                        f["load_w"](sp)
                        dw_sent = 0
                        for i in range(NT + 1):
                            n = rows_of(i)
                            if i + 2 <= NT:
                                f["load_x"](sp, i + 2)
                            sp.wait_ge(nrm_done, i + 1)
                            if i < NT:
                                sp.dma_start(O["new_k_prompt"][0, 0, i * P:(i + 1) * P].rearrange("t h d -> t (h d)"),
                                             nrm[:, i % 2, AW:]).then_inc(k_out[i % 2], 16)
                            else:
                                for b in range(DB):
                                    sp.dma_start(O["new_k_sample"][0, b, WINC - DS:WINC].rearrange("t h d -> t (h d)"),
                                                 nrm[DS * b:DS * b + DS, i % 2, AW:]).then_inc(k_out[i % 2], 16)
                            sp.wait_ge(t_done, i + 1)
                            sp.dma_start(qt_d[:, :, i * P:i * P + n], qkT[:, i % 2, 0, :, 0:n]).then_inc(t_out[i % 2], 16)
                            sp.dma_start(kt_d[:, :, i * P:i * P + n], qkT[:, i % 2, 1, :, 0:n]).then_inc(t_out[i % 2], 16)
                            if i % 4 == 3:
                                c = i // 4
                                sp.wait_ge(dw_done, c + 1)
                                sp.dma_start(dw_d[:, c, 0:SEQ], dwT[:]).then_inc(dw_out, 16)
                        sp.wait_ge(dw_done, CC + 1)
                        sp.dma_start(dw_d[:, :, SEQ:TOK], dwS[:]).then_inc(dw_out, 16)
                        sp.wait_ge(dw_out, 16 * (CC + 1))
                        sp.wait_ge(k_out[0], 16 * (8 + DB))
                        sp.wait_ge(k_out[1], 16 * 8)
                        sp.wait_ge(t_out[0], 32 * 9)
                        sp.wait_ge(t_out[1], 32 * 8)

                    @block.gpsimd
                    def _(pool):
                        copy_cache(pool, 3)
                        copy_cache(pool, 4)
                        copy_cache(pool, 5)
                        f["norm_x"](pool, 0)
                        heads = lambda ap: ap.rearrange("p (s h d) -> p s h d", s=2, d=DH)

                        def norm_qk(i):
                            n = rows_of(i)
                            pool.wait_ge(rs_done, i + 1)
                            if i == 0:
                                pool.wait_ge(gain_set, 1)
                            if i >= 2:
                                pool.wait_ge(t_pe, 2 * (i - 1))
                                pool.wait_ge(k_out[i % 2], 16 * (i // 2))
                            out = nrm[0:n, i % 2].rearrange("p (h d) -> p h d", d=DH)
                            pool.tensor_tensor(out, raw[0:n, i % 2].rearrange("p (h d) -> p h d", d=DH),
                                               rsq[0:n, i % 2].unsqueeze(2).to_broadcast([n, 2 * H, DH]), ALU.mult).then_inc(nrm_half, 1)
                            pool.wait_ge(nrm_half, i + 1)
                            pool.tensor_tensor(heads(nrm[0:n, i % 2]), heads(nrm[0:n, i % 2]),
                                               gains[0:n].unsqueeze(2).to_broadcast([n, 2, H, DH]), ALU.mult).then_inc(nrm_done, 1)

                        for i in range(NT + 1):
                            f["split_lo"](pool, i)
                            if i < NT:
                                f["norm_x"](pool, i + 1)
                            if i >= 1:
                                norm_qk(i - 1)
                        norm_qk(NT)

                    @block.scalar
                    def _(act):
                        def turned(i):
                            n = rows_of(i)
                            if i >= 2:
                                act.wait_ge(t_out[i % 2], 32 * (i // 2))
                            for s in range(2):
                                act.wait_ge(t_pe, 2 * i + s + 1)
                                ins = act.activation(qkT[:, i % 2, s, :, 0:n], t_ps[:, s, :, 0:n], ACT.Copy)
                            ins.then_inc(t_done, 1)

                        f["split_w_hi"](act)
                        f["modulate"](act, 0)
                        f["split_hi"](act, 0)
                        for i in range(NT + 1):
                            n = rows_of(i)
                            if i + 1 < NT:
                                f["modulate"](act, i + 1)
                            if i + 1 <= NT:
                                f["split_hi"](act, i + 1)
                            if i >= 2:
                                act.wait_ge(nrm_half, i - 1)
                            for s in range(2):
                                act.wait_ge(z_pe, 2 * i + s + 1)
                                ins = act.activation(raw[0:n, i % 2, s * AW:(s + 1) * AW], z_ps[(2 * i + s) % 4][0:n], ACT.Copy)
                            ins.then_inc(raw_done, 1)
                            if i >= 1:
                                turned(i - 1)
                        turned(NT)

                    @block.vector
                    def _(v):
                        step = Chain(v, f["hv"])
                        f["split_w_lo"](v)
                        v.wait_ge(gain_in, 32)
                        v.tensor_scalar(gains[:, 0, :], gains[:, 0, :], -float(DH) ** -0.5, None, ALU.mult).then_inc(gain_set, 1)

                        def head_norms(i):
                            n = rows_of(i)
                            v.wait_ge(raw_done, i + 1)
                            if i >= 2:
                                v.wait_ge(nrm_half, i - 1)
                            step(v.tensor_tensor(sqr[0:n], raw[0:n, i % 2], raw[0:n, i % 2], ALU.mult))
                            step(v.tensor_reduce(ssq[0:n], sqr[0:n].rearrange("p (h d) -> p h d", d=DH), AX.X, ALU.add))
                            step(v.tensor_scalar(ssq[0:n], ssq[0:n], 1.0 / DH, EPS, ALU.mult, ALU.add))
                            rsqrt(v, step, rsq[0:n, i % 2], ssq[0:n], tmp[0:n])
                            v.sem_inc(rs_done, 1)

                        PIECES = 4
                        PW = SEQ // PIECES

                        def conv_taps(c, taps):
                            for j in taps:
                                w = tapT[:, j * CC + c:j * CC + c + 1]
                                for s in range(PIECES):
                                    x = gluT[:, c, j + s * PW:j + s * PW + PW]
                                    y = dwT[:, s * PW:(s + 1) * PW]
                                    if j == 0:
                                        if c >= 1:
                                            v.wait_ge(dw_out, 16 * c)
                                        ins = v.tensor_scalar(y, x, w, vecT[:, V_CB + c:V_CB + c + 1], ALU.mult, ALU.add)
                                    else:
                                        v.wait_ge(f["hv"], step.n - PIECES + 1)
                                        ins = v.scalar_tensor_tensor(out=y, in0=x, scalar=w, in1=y, op0=ALU.mult, op1=ALU.add)
                                    step.mark(ins)
                            if taps[-1] == TAPS - 1:
                                v.wait_ge(f["hv"], step.n)
                                v.sem_inc(dw_done, 1)

                        for i in range(NT):
                            if i == NT - 1:
                                f["modulate_sample"](v, step)
                            taps = list(range(8 * (i % 4), min(8 * (i % 4) + 8, TAPS)))
                            conv_taps(i // 4, taps)
                            head_norms(i)
                        for c in range(CC):
                            y = dwS[:, c, :].rearrange("p (b t) -> p b t", t=DS)
                            for j in range(TAPS):
                                x = gluS[:, c, :, j:j + DS]
                                w = tapT[:, j * CC + c:j * CC + c + 1]
                                if j == 0:
                                    step(v.tensor_scalar(y, x, w, vecT[:, V_CB + c:V_CB + c + 1], ALU.mult, ALU.add))
                                else:
                                    step(v.scalar_tensor_tensor(out=y, in0=x, scalar=w, in1=y, op0=ALU.mult, op1=ALU.add))
                        v.sem_inc(dw_done, 1)
                        head_norms(NT)

                    @block.tensor
                    def _(pe):
                        def turn_qk(i):
                            n = rows_of(i)
                            pe.wait_ge(nrm_done, i + 1)
                            if i >= 1:
                                pe.wait_ge(t_done, i)
                            for s in range(2):
                                for c in range(4):
                                    mm = pe.transpose(t_ps[:, s, c, 0:n], nrm[0:n, i % 2, (4 * s + c) * P:(4 * s + c + 1) * P], ident[0:n, 0:n])
                                mm.then_inc(t_pe, 1)

                        f["turn_x"](pe, 0)
                        for i in range(NT + 1):
                            if i < NT:
                                f["turn_x"](pe, i + 1)
                            f["products"](pe, i, lambda g: pe.wait_ge(raw_done, g // 2 + 1))
                            if i >= 1:
                                turn_qk(i - 1)
                        turn_qk(NT)

            projection("qk_", 0, 2 * AW, queries_and_keys)
            end_stage()

        with ExitStack() as st:
            def sb(name, shape, dt=F32):
                return st.enter_context(nc.sbuf_tensor("pa_" + name, shape, dt))

            def ps(name, shape, dt=F32):
                return st.enter_context(nc.psum_tensor("pa_" + name, shape, dt))

            def sm(name):
                return sem("pa_" + name)

            PAIRS = H // 2
            bias = sb("bias", [P, H, 3, 2 * NB])
            qT = sb("qT", [P, 2, SEQ])
            kT = sb("kT", [P, 2, SEQ])
            vp = sb("vp", [P, 2, 3, NT, P])
            score = sb("score", [P, 3, 2 * NB])
            prob = sb("prob", [P, 3, 2 * NB])
            probT = sb("probT", [P, 3, 2 * NB])
            o_sb = sb("o_sb", [P, 2, NT, P])
            stat = sb("stat", [P, 3, NT, 2, H])
            s_ps = [ps(f"s_ps{i}", [P, 512]) for i in range(3)]
            t_ps = [ps(f"t_ps{i}", [P, 512]) for i in range(3)]
            o_ps = [ps(f"o_ps{i}", [P, 512]) for i in range(2)]
            bias_in, pair_in = sm("bias_in"), [sm("pair_in0"), sm("pair_in1")]
            s_pe, s_done, e_done, t_pe, t_done, o_done = (sm(x) for x in ("s_pe", "s_done", "e_done", "t_pe", "t_done", "o_done"))
            o_seen = sm("o_seen")
            o_out, st_out = [sm("o_out0"), sm("o_out1")], sm("st_out")
            items = [(hp, p, t, hh) for hp in range(PAIRS) for p in range(3) for t in range(NT) for hh in range(2)]
            N = len(items)

            def blocks(p):
                d = PATTERNS[p][1]
                return d, NT // d

            def tokens(p, t, prev):
                d, nb = blocks(p)
                r, n = divmod(t, nb)
                first, count = (n - prev) * NB * d + r, (1 + prev) * NB
                return slice(first, first + (count - 1) * d + 1, d)

            def has_prev(p, t):
                return int(t % blocks(p)[1] > 0)

            def by_block(dram_rows, p, src):
                d, nb = blocks(p)
                view = dram_rows.rearrange("(n i r) c -> r i n c", i=NB, r=d)
                for r in range(d) if nb > 1 else [None]:
                    if r is None:
                        yield dram_rows.rearrange("(i r) c -> i r c", r=d), src
                    else:
                        yield view[r], src[:, r * nb:(r + 1) * nb, :]

            out_n = {q: (1, 4, 1)[q % 3] for q in range(3 * PAIRS)}

            def out_count(q):
                return 16 * sum(out_n[x] for x in range(q % 2, q + 1, 2))

            with nc.Block() as block:
                @block.sync
                def _(sp):
                    def load_pair(hp):
                        if hp >= 2:
                            sp.wait_ge(o_seen, (hp - 1) * 6 * NT)
                        b = hp % 2
                        sp.dma_start(qT[:, b], qt_d[:, hp, 0:SEQ]).then_inc(pair_in[b], 16)
                        sp.dma_start(kT[:, b], kt_d[:, hp, 0:SEQ]).then_inc(pair_in[b], 16)
                        rows = O["new_v_prompt"][0, 0].rearrange("t h d -> t (h d)")[:, hp * P:(hp + 1) * P]
                        for p in range(3):
                            for src, dst in by_block(rows, p, vp[:, b, p]):
                                sp.dma_start(dst, src).then_inc(pair_in[b], 16)

                    load_pair(0)
                    for h in range(H):
                        skew = bass.AP(bias_d.tensor, h * P * 3 * RW + NB - 1, [[3 * RW - 1, P], [RW, 3], [1, 2 * NB]])
                        sp.dma_start(bias[:, h], skew).then_inc(bias_in, 16)
                    load_pair(1)
                    for q in range(3 * PAIRS):
                        hp, p = divmod(q, 3)
                        if p == 0 and 1 <= hp < PAIRS - 1:
                            load_pair(hp + 1)
                        sp.wait_ge(o_done, (q + 1) * NT)
                        for dst, src in by_block(acc_d[p][:, hp * P:(hp + 1) * P], p, o_sb[:, q % 2]):
                            sp.dma_start(dst, src).then_inc(o_out[q % 2], 16)
                    sp.wait_ge(s_done, N)
                    sp.wait_ge(e_done, N)
                    for p in range(3):
                        for dst, src in by_block(st_d[p], p, stat[:, p].rearrange("i t s h -> i t (s h)")):
                            sp.dma_start(dst, src).then_inc(st_out, 16)
                    sp.wait_ge(st_out, 16 * 6)
                    sp.wait_ge(o_out[0], out_count(3 * PAIRS - 2))
                    sp.wait_ge(o_out[1], out_count(3 * PAIRS - 1))

                @block.gpsimd
                def _(pool):
                    for n in range(6, 9):
                        copy_cache(pool, n)

                @block.tensor
                def _(pe):
                    def scores(w):
                        hp, p, t, hh = items[w]
                        b, part, prev = hp % 2, slice(hh * DH, hh * DH + DH), has_prev(p, t)
                        if w % (6 * NT) == 0:
                            pe.wait_ge(pair_in[b], 16 * 8 * (hp // 2 + 1))
                        if w >= 3:
                            pe.wait_ge(s_done, w - 2)
                        pe.matmul(s_ps[w % 3][:, 0:(1 + prev) * NB], qT[part, b, tokens(p, t, 0)], kT[part, b, tokens(p, t, prev)],
                                  start=True, stop=True).then_inc(s_pe, 1)

                    def turn(w):
                        prev = has_prev(*items[w][1:3])
                        pe.wait_ge(e_done, w + 1)
                        if w >= 3:
                            pe.wait_ge(t_done, w - 2)
                        for j in range(1 + prev):
                            mm = pe.transpose(t_ps[w % 3][:, j * NB:(j + 1) * NB], prob[:, w % 3, j * NB:(j + 1) * NB], ident[:])
                        mm.then_inc(t_pe, 1)

                    def weigh(w):
                        hp, p, t, hh = items[w]
                        prev = has_prev(p, t)
                        u = w // 2
                        pe.wait_ge(t_done, w + 1)
                        if hh == 0 and u >= 2:
                            pe.wait_ge(o_done, u - 1)
                        for j in range(1 + prev):
                            mm = pe.matmul(o_ps[u % 2][:, hh * DH:(hh + 1) * DH], probT[:, w % 3, j * NB:(j + 1) * NB],
                                           vp[:, hp % 2, p, t - prev + j, hh * DH:(hh + 1) * DH], start=j == 0, stop=j == prev)
                        mm.then_inc(o_seen, 1)

                    for w in range(N + 3):
                        if w < N:
                            scores(w)
                        if 2 <= w < N + 2:
                            turn(w - 2)
                        if w >= 3:
                            weigh(w - 3)

                @block.vector
                def _(v):
                    v.wait_ge(bias_in, 16 * H)
                    for w in range(N + 3):
                        if w < N:
                            hp, p, t, hh = items[w]
                            h, prev = 2 * hp + hh, has_prev(p, t)
                            v.wait_ge(s_pe, w + 1)
                            if w >= 3:
                                v.wait_ge(e_done, w - 2)
                            cols = slice(0, (1 + prev) * NB)
                            v.tensor_tensor_reduce(score[:, w % 3, cols], s_ps[w % 3][:, cols], bias[:, h, p, (1 - prev) * NB:2 * NB],
                                                   1.0, -NEG, ALU.add, ALU.min, stat[:, p, t, 0, h:h + 1]).then_inc(s_done, 1)
                        if 2 <= w < N + 2 and (w - 2) % 4 != 3:
                            u = w - 2
                            v.wait_ge(t_pe, u + 1)
                            cols = slice(0, (1 + has_prev(*items[u][1:3])) * NB)
                            if u >= 3:
                                v.wait_ge(o_seen, u - 2)
                            v.wait_ge(t_done, u)
                            v.tensor_copy(probT[:, u % 3, cols], t_ps[u % 3][:, cols]).then_inc(t_done, 1)
                        if w >= 3 and items[w - 3][3] == 1:
                            u = (w - 3) // 2
                            q = u // NT
                            v.wait_ge(o_seen, 2 * u + 2)
                            if u % NT == 0 and q >= 2:
                                v.wait_ge(o_out[q % 2], out_count(q - 2))
                            v.tensor_copy(o_sb[:, q % 2, u % NT], o_ps[u % 2][:, 0:P]).then_inc(o_done, 1)

                @block.scalar
                def _(act):
                    for w in range(N + 2):
                        if w < N:
                            hp, p, t, hh = items[w]
                            h = 2 * hp + hh
                            cols = slice(0, (1 + has_prev(p, t)) * NB)
                            act.wait_ge(s_done, w + 1)
                            if w >= 3:
                                act.wait_ge(t_pe, w - 2)
                            act.activation(prob[:, w % 3, cols], score[:, w % 3, cols], ACT.Exp, bias=stat[:, p, t, 0, h:h + 1],
                                           scale=-1.0, accum_out=stat[:, p, t, 1, h:h + 1]).then_inc(e_done, 1)
                        if w >= 2 and (w - 2) % 4 == 3:
                            u = w - 2
                            act.wait_ge(t_pe, u + 1)
                            cols = slice(0, (1 + has_prev(*items[u][1:3])) * NB)
                            act.wait_ge(o_seen, u - 2)
                            act.wait_ge(t_done, u)
                            act.activation(probT[:, u % 3, cols], t_ps[u % 3][:, cols], ACT.Copy).then_inc(t_done, 1)

        end_stage()

        with ExitStack() as st:
            def sb(name, shape, dt=F32):
                return st.enter_context(nc.sbuf_tensor("sa_" + name, shape, dt))

            def ps(name, shape, dt=F32):
                return st.enter_context(nc.psum_tensor("sa_" + name, shape, dt))

            def sm(name):
                return sem("sa_" + name)

            G = 4
            qs = sb("qs", [P, 4, NS])
            ks = sb("ks", [P, 4, NS])
            qblk = sb("qblk", [P, DB, 4, NS])
            kn = sb("kn", [P, 2, 2, 4, AW])
            kTt = sb("kTt", [P, 2, 4, 4, P])
            vn = sb("vn", [P, G, 2, 4, AW])
            vnew = sb("vnew", [DS, DB, AW])
            sbias = sb("sbias", [P, 3, SKEYS])
            score = sb("score", [P, SKEYS])
            prob = sb("prob", [P, 3, SKEYS])
            mins = sb("mins", [P, 8])
            mask = sb("mask", [P, H])
            probT = sb("probT", [P, 8, P])
            probN = sb("probN", [DS, P])
            o_m = sb("o_m", [P, AW])
            o_r = sb("o_r", [P, 2, DH])
            k_ps = [ps(f"k_ps{i}", [P, 4, P]) for i in range(2)]
            s_ps = ps("s_ps", [P, 3, 512])
            p_ps = [ps(f"p_ps{i}", [P, 512]) for i in range(2)]
            o_ps = ps("o_ps", [P, 512])
            small_in, blk_zero, blk_done = sm("small_in"), sm("blk_zero"), sm("blk_done")
            k_in, v_in = [sm("k_in0"), sm("k_in1")], sm("v_in")
            k_pe, k_cp, s_pe, soft, p_pe, p_cp, o_pe, o_done, o_out, sv = (sm(x) for x in ("k_pe", "k_cp", "s_pe", "soft", "p_pe", "p_cp", "o_pe", "o_done", "o_out", "sv"))
            s_read, s_min, s_exp = sm("s_read"), sm("s_min"), sm("s_exp")
            units = [(b, a) for b in range(DB) for a in range(2)]

            def rows(cache, b, a):
                r = cache[0, b].rearrange("r h d -> r (h d)")
                if a == 0:
                    return r[WINC - 512:WINC].rearrange("(p j) c -> p j c", j=4)
                return r.rearrange("(p j) c -> p j c", j=16)[:, 0:DS, :]

            with nc.Block() as block:
                @block.sync
                def _(sp):
                    sp.dma_start(qs[:], qt_d[:, :, SEQ:TOK]).then_inc(small_in, 16)
                    sp.dma_start(ks[:], kt_d[:, :, SEQ:TOK]).then_inc(small_in, 16)
                    sp.dma_start(mask[:], I["mask_h"]).then_inc(small_in, 16)

                    def load_k(n):
                        b, a = units[n]
                        if n >= 4:
                            sp.wait_ge(k_pe, 4 * (n - 3))
                        sp.dma_start(kn[:, (n // 2) % 2, a], rows(I["cache_k"], b, a)).then_inc(k_in[(n // 2) % 2], 16)

                    for n in range(4):
                        load_k(n)
                    sp.dma_start(vnew[:], O["new_v_sample"][0, :, WINC - DS:WINC].rearrange("b t h d -> t b (h d)")).then_inc(small_in, 16)
                    sp.dma_start(sbias[:].rearrange("p a c -> p (a c)"), sbias_d).then_inc(small_in, 16)
                    for g in range(DB // G):
                        for b in range(G * g, G * g + G):
                            if b % G == 0 and g >= 1:
                                sp.wait_ge(o_pe, g)
                            for a in range(2):
                                sp.dma_start(vn[:, b % G, a], rows(I["cache_v"], b, a)).then_inc(v_in, 16)
                            for n in (2 * b + 4, 2 * b + 5):
                                if n < 2 * DB:
                                    load_k(n)
                    for g in range(DB // G):
                        sp.wait_ge(o_done, g + 1)
                        for j in range(G):
                            b = G * g + j
                            sp.dma_start(os_d[DS * b:DS * b + DS].rearrange("t (h d) -> h t d", d=DH),
                                         o_r[32 * j:32 * j + 32, g % 2]).then_inc(o_out, 16)
                    sp.wait_ge(o_out, 16 * DB)

                @block.gpsimd
                def _(pool):
                    pool.memset(qblk[:], 0.0).then_inc(blk_zero, 1)
                    pool.wait_ge(blk_zero, 1)
                    pool.wait_ge(small_in, 16 * 5)
                    for c in range(4):
                        for hh in range(2):
                            part = slice(hh * DH, hh * DH + DH)
                            col = DS * (2 * c + hh)
                            ins = pool.tensor_copy(qblk[part, :, c, col:col + DS], qs[part, c, :].rearrange("p (b t) -> p b t", t=DS))
                    ins.then_inc(blk_done, 1)
                    for n in range(9, 10):
                        copy_cache(pool, n)

                @block.tensor
                def _(pe):
                    def turn(n, c):
                        b, a = units[n]
                        if c == 0:
                            pe.wait_ge(k_in[(n // 2) % 2], 16 * (2 * (n // 4) + 2))
                        g = 4 * n + c
                        if g >= 2:
                            pe.wait_ge(k_cp, g - 1)
                        for j in range(4):
                            mm = pe.transpose(k_ps[g % 2][:, j, :], kn[:, (n // 2) % 2, a, j, c * P:(c + 1) * P], ident[:])
                        mm.then_inc(k_pe, 1)

                    def scores(n):
                        b, a = units[n]
                        part = slice(32 * (b % G), 32 * (b % G) + 32)
                        pe.wait_ge(k_cp, 4 * n + 4)
                        if n == 0:
                            pe.wait_ge(blk_done, 1)
                        if b % G == 0 and a == 0 and b >= G:
                            pe.wait_ge(s_read, b // G)
                        for c in range(4):
                            mm = pe.matmul(s_ps[part, a, :], qblk[:, b, c, :], kTt[:, n % 2, c].rearrange("p j k -> p (j k)"), start=c == 0, stop=c == 3)
                        if a == 1:
                            for c in range(4):
                                mm = pe.matmul(s_ps[part, 2, 0:DS], qblk[:, b, c, :], ks[:, c, DS * b:DS * b + DS], start=c == 0, stop=c == 3)
                        mm.then_inc(s_pe, 1)

                    def values(g):
                        pe.wait_ge(soft, g + 1)
                        for j in range(3):
                            u = 3 * g + j
                            if u >= 2:
                                pe.wait_ge(p_cp, u - 1)
                            if j < 2:
                                for m in range(4):
                                    mm = pe.transpose(p_ps[u % 2][:, m * P:(m + 1) * P], prob[:, 0, (4 * j + m) * P:(4 * j + m + 1) * P], ident[:])
                            else:
                                mm = pe.transpose(p_ps[u % 2][0:DS, 0:P], prob[:, 0, 8 * P:8 * P + DS], ident[:])
                            mm.then_inc(p_pe, 1)
                        pe.wait_ge(p_cp, 3 * g + 3)
                        pe.wait_ge(v_in, 16 * 2 * G * (g + 1))
                        if g >= 1:
                            pe.wait_ge(o_done, g)
                        for j in range(G):
                            part = slice(32 * j, 32 * j + 32)
                            for m in range(8):
                                pe.matmul(o_ps[part, :], probT[:, m, part], vn[:, j, m // 4, m % 4, :], start=m == 0, stop=False)
                            mm = pe.matmul(o_ps[part, :], probN[:, part], vnew[:, G * g + j, :], start=False, stop=True)
                        mm.then_inc(o_pe, 1)

                    for n in range(2 * DB):
                        for c in range(4):
                            turn(n, c)
                        if n >= 1:
                            scores(n - 1)
                        if n == 2 * G + 2:
                            values(0)
                    scores(2 * DB - 1)
                    values(1)

                @block.vector
                def _(v):
                    step = Chain(v, sv)

                    def k_copy(g):
                        n, c = divmod(g, 4)
                        v.wait_ge(k_pe, g + 1)
                        if n >= 2:
                            v.wait_ge(s_pe, n - 1)
                        v.tensor_copy(kTt[:, n % 2, c], k_ps[g % 2][:]).then_inc(k_cp, 1)

                    def soften(g):
                        v.wait_ge(s_pe, 2 * G * (g + 1))
                        if g == 0:
                            v.wait_ge(small_in, 16 * 5)
                        v.tensor_copy(score[:, 0:8 * P], s_ps[:, 0:2, :].rearrange("p a k -> p (a k)"))
                        step(v.tensor_copy(score[:, 8 * P:SKEYS], s_ps[:, 2, 0:DS]))
                        v.sem_inc(s_read, 1)
                        if g >= 1:
                            v.wait_ge(o_pe, g)
                        for p in range(3):
                            ins = v.tensor_tensor_reduce(prob[:, p], score[:], sbias[:, p], 1.0, -NEG, ALU.add, ALU.min, mins[:, p:p + 1])
                        step(ins)
                        step(v.tensor_reduce(mins[:, 3:4], mins[:, 0:3], AX.X, ALU.min))
                        v.sem_inc(s_min, 1)
                        v.wait_ge(s_exp, g + 1)
                        step(v.tensor_reduce(mins[:, 7:8], mins[:, 4:7], AX.X, ALU.add))
                        step(v.reciprocal(mins[:, 7:8], mins[:, 7:8]))
                        step(v.tensor_tensor(prob[:, 0], prob[:, 0], prob[:, 1], ALU.add))
                        step(v.tensor_tensor(prob[:, 0], prob[:, 0], prob[:, 2], ALU.add))
                        v.tensor_scalar(prob[:, 0], prob[:, 0], mins[:, 7:8], None, ALU.mult).then_inc(soft, 1)

                    def p_copy(g):
                        for j in range(3):
                            u = 3 * g + j
                            v.wait_ge(p_pe, u + 1)
                            if j == 0 and g >= 1:
                                v.wait_ge(o_pe, g)
                            if j < 2:
                                v.tensor_copy(probT[:, 4 * j:4 * j + 4].rearrange("p m k -> p (m k)"), p_ps[u % 2][:]).then_inc(p_cp, 1)
                            else:
                                v.tensor_copy(probN[:], p_ps[u % 2][0:DS, 0:P]).then_inc(p_cp, 1)

                    def gather(g):
                        v.wait_ge(o_pe, g + 1)
                        step(v.tensor_tensor(o_m[:].rearrange("p (h d) -> p h d", d=DH), o_ps[:].rearrange("p (h d) -> p h d", d=DH),
                                             mask[:].unsqueeze(2).to_broadcast([P, H, DH]), ALU.mult))
                        v.tensor_reduce(o_r[:, g % 2], o_m[:].rearrange("p (h d) -> p d h", d=DH), AX.X, ALU.add).then_inc(o_done, 1)

                    for n in range(2 * DB):
                        for c in range(4):
                            k_copy(4 * n + c)
                        if n == 2 * G:
                            soften(0)
                        if n == 2 * G + 2:
                            p_copy(0)
                            gather(0)
                    soften(1)
                    p_copy(1)
                    gather(1)

                @block.scalar
                def _(act):
                    for g in range(DB // G):
                        act.wait_ge(s_min, g + 1)
                        for p in range(3):
                            ins = act.activation(prob[:, p], prob[:, p], ACT.Exp, bias=mins[:, 3:4], scale=-1.0, accum_out=mins[:, 4 + p:5 + p])
                        ins.then_inc(s_exp, 1)
        end_stage()

        with ExitStack() as st:
            def sb(name, shape, dt=F32):
                return st.enter_context(nc.sbuf_tensor("mx_" + name, shape, dt))

            def ps(name, shape, dt=F32):
                return st.enter_context(nc.psum_tensor("mx_" + name, shape, dt))

            def sm(name):
                return sem("mx_" + name)

            wo_hi = sb("wo_hi", [P, KT, D], F32R)
            wo_lo = sb("wo_lo", [P, KT, D], F32R)
            wp_hi = sb("wp_hi", [P, CC, CW], F32R)
            wp_lo = sb("wp_lo", [P, CC, CW], F32R)
            w_raw = sb("w_raw", [P, 2, D])
            gate_p = sb("gate_p", [P, D])
            gate_s = sb("gate_s", [NS, D])
            stat = sb("stat", [P, NT, 3, 2, H])
            least = sb("least", [P, NT, H])
            fac = sb("fac", [P, NT, 3, H])
            total = sb("total", [P, NT, H])
            acc = sb("acc", [P, 2, 3, AW])
            o_n = sb("o_n", [P, AW])
            dwt = sb("dwt", [P, 2, CC, P])
            x_in = sb("x_in", [P, 2, D])
            bn = sb("bn", [P, 6])
            mv = sb("mv", [P, 2])
            ln = sb("ln", [P, 4])
            y_n = sb("y_n", [P, CW])
            y_a = sb("y_a", [P, CC, P])
            y_g = sb("y_g", [P, CC, P])
            y_hi = sb("y_hi", [P, CC, P], F32R)
            y_lo = sb("y_lo", [P, CC, P], F32R)
            m_hi = sb("m_hi", [P, 2, KT, P], F32R)
            m_lo = sb("m_lo", [P, 2, KT, P], F32R)
            upd = sb("upd", [P, D])
            x1 = sb("x1", [P, 2, D])
            x1_sq = sb("x1_sq", [P, D])
            rs2 = sb("rs2", [P, 4])
            x1n = sb("x1n", [P, D])
            h2 = sb("h2", [P, 2, KT, P])
            dw_ps = ps("dw_ps", [P, CW])
            y_ps = ps("y_ps", [P, CC, P])
            c_ps = ps("c_ps", [P, CC, P])
            a_ps = ps("a_ps", [P, 4, P])
            z_ps = [ps(f"z_ps{i}", [P, 512]) for i in range(2)]
            h_ps = ps("h_ps", [P, KT, P])
            sems = ("fac_x w_hid w_lod gate_in stat_in fac_e fac_d dw_pe yn_d y_pe ya_d yg_d yf_d yhi_d ylo_d c_pe a_pe o_half o_d mhi_d mlo_d "
                    "z_pe upd_d x1_d_ sq_d rs2_d x1n_d h_pe h2_d_ mv_ x1q").split()
            S = {x: sm(x) for x in sems}
            w_ld, acc_in, dw_in, x_in_s = ([sm(f"{x}{i}") for i in range(2)] for x in ("w_ld", "acc_in", "dw_in", "x_in"))
            x1_out, h2_out = ([sm(f"{x}{i}") for i in range(2)] for x in ("x1_out", "h2_out"))
            WN = KT + 2

            def w_piece(n):
                if n < KT:
                    return I["w_o"][0, n * P:(n + 1) * P, :], w_raw[:, n % 2], wo_hi[:, n], wo_lo[:, n]
                m = 2 * (n - KT)
                flat = lambda ap: ap.rearrange("p k c -> p (k c)")
                return (I["w_pw2"][0, m * P:(m + 2) * P, :].rearrange("(k p) c -> p k c", p=P), w_raw[:, n % 2].rearrange("p (k c) -> p k c", k=2),
                        wp_hi[:, m:m + 2], wp_lo[:, m:m + 2])

            def like(n, ap):
                return ap if n < KT else ap.rearrange("p (k c) -> p k c", k=2)

            with nc.Block() as block:
                @block.sync
                def _(sp):
                    def loads(i):
                        n = rows_of(i)
                        t = slice(i * P, i * P + n)
                        if i >= 2:
                            sp.wait_ge(S["o_d"], i - 1)
                            sp.wait_ge(S["dw_pe"], i - 1)
                            sp.wait_ge(S["x1_d_"], i - 1)
                        if i < NT:
                            sp.dma_start(acc[:, i % 2], acc_d[:, t].rearrange("a t c -> t a c")).then_inc(acc_in[i % 2], 16)
                        else:
                            sp.dma_start(acc[0:n, i % 2, 0], os_d).then_inc(acc_in[i % 2], 16)
                        sp.dma_start(dwt[:, i % 2, :, 0:n], dw_d[:, :, t]).then_inc(dw_in[i % 2], 16)
                        src = I["x_prompt"][0, t, :] if i < NT else I["x_sample"].rearrange("b t d -> (b t) d")
                        sp.dma_start(x_in[0:n, i % 2], src).then_inc(x_in_s[i % 2], 16)

                    for a in range(3):
                        sp.dma_start(stat[:, :, a].rearrange("p i s h -> p i (s h)"), st_d[a].rearrange("(i p) c -> p i c", p=P)).then_inc(S["stat_in"], 16)
                    loads(0)
                    for n in range(WN):
                        if n >= 2:
                            sp.wait_ge(S["w_lod"], n - 1)
                        src, raw = w_piece((n + KT) % WN)[0:2]
                        sp.dma_start(like((n + KT) % WN, w_raw[:, n % 2]), src).then_inc(w_ld[n % 2], 16)
                        if n == 1:
                            loads(1)
                            sp.dma_start(gate_p[:], mod_d[8:9, 2 * D:3 * D].to_broadcast([P, D])).then_inc(S["gate_in"], 16)
                            sp.dma_start(gate_s[:], bass.AP(mod_d.tensor, 2 * D, [[NMOD, DB], [0, DS], [1, D]])).then_inc(S["gate_in"], 16)
                    for i in range(NT + 1):
                        if i + 2 <= NT:
                            loads(i + 2)
                        n = rows_of(i)
                        sp.wait_ge(S["x1_d_"], i + 1)
                        sp.dma_start(x1_d[i * P:i * P + n], x1[0:n, i % 2]).then_inc(x1_out[i % 2], 16)
                        sp.wait_ge(S["h2_d_"], i + 1)
                        sp.dma_start(h2_d[:, :, i * P:i * P + n], h2[:, i % 2, :, 0:n]).then_inc(h2_out[i % 2], 16)
                    for s in (x1_out, h2_out):
                        sp.wait_ge(s[0], 16 * 9)
                        sp.wait_ge(s[1], 16 * 8)

                @block.gpsimd
                def _(pool):
                    for n in range(10, 12):
                        copy_cache(pool, n)

                    def merge(i):
                        n = rows_of(i)
                        if i < NT:
                            if i == 0:
                                pool.wait_ge(S["fac_d"], 1)
                            pool.wait_ge(acc_in[i % 2], 16 * (i // 2 + 1))
                            view = acc[:, i % 2].rearrange("p a (h d) -> p (a h) d", d=DH)
                            pool.tensor_tensor(view, view, fac[:, i].rearrange("p a h -> p (a h)").unsqueeze(2).to_broadcast([P, 3 * H, DH]),
                                               ALU.mult).then_inc(S["o_half"], 1)
                            pool.wait_ge(S["o_half"], 2 * i + 1)
                            pool.tensor_tensor(acc[:, i % 2, 0], acc[:, i % 2, 0], acc[:, i % 2, 1], ALU.add).then_inc(S["o_half"], 1)
                            pool.wait_ge(S["o_half"], 2 * i + 2)
                            if i >= 1:
                                pool.wait_ge(S["a_pe"], i)
                            pool.tensor_tensor(o_n[:], acc[:, i % 2, 0], acc[:, i % 2, 2], ALU.add).then_inc(S["o_d"], 1)
                        else:
                            pool.wait_ge(acc_in[i % 2], 16 * (i // 2 + 1))
                            pool.wait_ge(S["a_pe"], i)
                            pool.tensor_copy(o_n[0:n], acc[0:n, i % 2, 0]).then_inc(S["o_d"], 1)

                    def split_y(i):
                        n = rows_of(i)
                        pool.wait_ge(S["yhi_d"], i + 1)
                        if i >= 1:
                            pool.wait_ge(S["c_pe"], i)
                        pool.tensor_tensor(y_lo[:, :, 0:n], y_a[:, :, 0:n], y_hi[:, :, 0:n].bitcast(F32), ALU.subtract).then_inc(S["ylo_d"], 1)

                    def residual(i):
                        n = rows_of(i)
                        pool.wait_ge(S["upd_d"], i + 1)
                        pool.wait_ge(x_in_s[i % 2], 16 * (i // 2 + 1))
                        if i >= 2:
                            pool.wait_ge(x1_out[i % 2], 16 * (i // 2))
                            pool.wait_ge(S["x1n_d"], i - 1)
                        pool.tensor_tensor(x1[0:n, i % 2], upd[0:n], x_in[0:n, i % 2], ALU.add).then_inc(S["x1_d_"], 1)

                    def norm2(i):
                        n = rows_of(i)
                        pool.wait_ge(S["rs2_d"], i + 1)
                        if i >= 1:
                            pool.wait_ge(S["h_pe"], i)
                        pool.tensor_scalar(x1n[0:n], x1[0:n, i % 2], rs2[0:n, 0:1], None, ALU.mult).then_inc(S["x1n_d"], 1)

                    merge(0)
                    split_y(0)
                    for i in range(NT + 1):
                        if i < NT:
                            merge(i + 1)
                            split_y(i + 1)
                        residual(i)
                        norm2(i)

                @block.scalar
                def _(act):
                    for n in range(WN):
                        if n == 2:
                            act.wait_ge(S["fac_e"], 1)
                            act.activation(fac[:], fac[:], ACT.Exp).then_inc(S["fac_x"], 1)
                        m = (n + KT) % WN
                        act.wait_ge(w_ld[n % 2], 16 * (n // 2 + 1))
                        act.activation(w_piece(m)[2], like(m, w_raw[:, n % 2]), ACT.Copy).then_inc(S["w_hid"], 1)

                    def swish(i):
                        n = rows_of(i)
                        act.wait_ge(S["y_pe"], i + 1)
                        if i >= 1:
                            act.wait_ge(S["ylo_d"], i)
                        for c in range(CC):
                            g, b = vecT[:, V_LG + c:V_LG + c + 1], vecT[:, V_LB + c:V_LB + c + 1]
                            act.activation(y_a[:, c, 0:n], y_ps[:, c, 0:n], ACT.Identity, bias=b, scale=g)
                            ins = act.activation(y_g[:, c, 0:n], y_ps[:, c, 0:n], ACT.Sigmoid, bias=b, scale=g)
                        ins.then_inc(S["yg_d"], 1)
                        act.wait_ge(S["yf_d"], i + 1)
                        if i >= 1:
                            act.wait_ge(S["c_pe"], i)
                        act.activation(y_hi[:, :, 0:n], y_a[:, :, 0:n], ACT.Copy).then_inc(S["yhi_d"], 1)

                    def split_mix(i):
                        n = rows_of(i)
                        act.wait_ge(S["a_pe"], i + 1)
                        if i >= 2:
                            act.wait_ge(S["z_pe"], 2 * (i - 1))
                        act.activation(m_hi[:, i % 2, 0:4, 0:n], a_ps[:, :, 0:n], ACT.Copy).then_inc(S["mhi_d"], 1)
                        act.wait_ge(S["c_pe"], i + 1)
                        act.activation(m_hi[:, i % 2, 4:8, 0:n], c_ps[:, :, 0:n], ACT.Copy).then_inc(S["mhi_d"], 1)

                    def square(i):
                        n = rows_of(i)
                        act.wait_ge(S["x1_d_"], i + 1)
                        if i >= 1:
                            act.wait_ge(S["rs2_d"], i)
                            act.wait_ge(S["x1q"], i)
                        act.activation(x1_sq[0:n], x1[0:n, i % 2], ACT.Square, accum_out=rs2[0:n, 1:2]).then_inc(S["x1q"], 1)

                    def modulate(i):
                        act.wait_ge(S["h_pe"], i + 1)
                        if i >= 2:
                            act.wait_ge(h2_out[i % 2], 16 * (i // 2))
                        for k in range(KT):
                            ins = act.activation(h2[:, i % 2, k], h_ps[:, k], ACT.Identity, bias=modT[:, M_SH2 + k, 8:9], scale=gain2[:, k, 8:9])
                        ins.then_inc(S["h2_d_"], 1)

                    swish(0)
                    split_mix(0)
                    for i in range(NT + 1):
                        if i < NT:
                            swish(i + 1)
                        if 1 <= i:
                            modulate(i - 1)
                        if i < NT:
                            split_mix(i + 1)
                        square(i)

                @block.vector
                def _(v):
                    step = Chain(v, S["mv_"])

                    def split_w(n):
                        m = (n + KT) % WN
                        v.wait_ge(S["w_hid"], n + 1)
                        v.tensor_tensor(w_piece(m)[3], like(m, w_raw[:, n % 2]), w_piece(m)[2].bitcast(F32), ALU.subtract).then_inc(S["w_lod"], 1)

                    def layer_norm(i):
                        n = rows_of(i)
                        v.wait_ge(S["dw_pe"], i + 1)
                        step(v.bn_stats(bn[0:n], dw_ps[0:n]))
                        step(v.bn_aggr(mv[0:n], bn[0:n]))
                        step(v.tensor_scalar(ln[0:n, 0:1], mv[0:n, 1:2], EPS, None, ALU.add))
                        rsqrt(v, step, ln[0:n, 1:2], ln[0:n, 0:1], ln[0:n, 2:3])
                        if i >= 1:
                            v.wait_ge(S["y_pe"], i)
                        v.tensor_scalar(y_n[0:n], dw_ps[0:n], mv[0:n, 0:1], ln[0:n, 1:2], ALU.subtract, ALU.mult).then_inc(S["yn_d"], 1)

                    def gate_y(i):
                        n = rows_of(i)
                        v.wait_ge(S["yg_d"], i + 1)
                        v.tensor_tensor(y_a[:, :, 0:n], y_a[:, :, 0:n], y_g[:, :, 0:n], ALU.mult).then_inc(S["yf_d"], 1)

                    def split_mix(i):
                        n = rows_of(i)
                        v.wait_ge(S["mhi_d"], 2 * i + 1)
                        v.tensor_tensor(m_lo[:, i % 2, 0:4, 0:n], a_ps[:, :, 0:n], m_hi[:, i % 2, 0:4, 0:n].bitcast(F32), ALU.subtract).then_inc(S["mlo_d"], 1)
                        v.wait_ge(S["mhi_d"], 2 * i + 2)
                        v.tensor_tensor(m_lo[:, i % 2, 4:8, 0:n], c_ps[:, :, 0:n], m_hi[:, i % 2, 4:8, 0:n].bitcast(F32), ALU.subtract).then_inc(S["mlo_d"], 1)

                    def update(i):
                        n = rows_of(i)
                        gate = gate_p if i < NT else gate_s
                        if i >= 1:
                            v.wait_ge(S["x1_d_"], i)
                        if i == 0:
                            v.wait_ge(S["gate_in"], 32)
                        for c in range(2):
                            v.wait_ge(S["z_pe"], 2 * i + c + 1)
                            ins = v.tensor_tensor(upd[0:n, c * 512:(c + 1) * 512], z_ps[c][0:n], gate[0:n, c * 512:(c + 1) * 512], ALU.mult)
                        ins.then_inc(S["upd_d"], 1)

                    def second_norm(i):
                        n = rows_of(i)
                        v.wait_ge(S["x1q"], i + 1)
                        if i >= 1:
                            v.wait_ge(S["x1n_d"], i)
                        step(v.tensor_scalar(rs2[0:n, 2:3], rs2[0:n, 1:2], 1.0 / D, EPS, ALU.mult, ALU.add))
                        rsqrt(v, step, rs2[0:n, 0:1], rs2[0:n, 2:3], rs2[0:n, 3:4])
                        v.sem_inc(S["rs2_d"], 1)

                    split_w(0)
                    split_w(1)
                    v.wait_ge(S["stat_in"], 48)
                    step(v.tensor_tensor(least[:], stat[:, :, 0, 0], stat[:, :, 1, 0], ALU.min))
                    step(v.tensor_tensor(least[:], least[:], stat[:, :, 2, 0], ALU.min))
                    for a in range(3):
                        step(v.tensor_tensor(fac[:, :, a], least[:], stat[:, :, a, 0], ALU.subtract))
                    v.sem_inc(S["fac_e"], 1)
                    v.wait_ge(S["fac_x"], 1)
                    step(v.tensor_tensor(total[:], fac[:, :, 0], stat[:, :, 0, 1], ALU.mult))
                    for a in (1, 2):
                        step(v.tensor_tensor(least[:], fac[:, :, a], stat[:, :, a, 1], ALU.mult))
                        step(v.tensor_tensor(total[:], total[:], least[:], ALU.add))
                    step(v.reciprocal(total[:], total[:]))
                    for a in range(3):
                        step(v.tensor_tensor(fac[:, :, a], fac[:, :, a], total[:], ALU.mult))
                    v.sem_inc(S["fac_d"], 1)
                    layer_norm(0)
                    for n in range(2, WN):
                        split_w(n)
                    gate_y(0)
                    split_mix(0)
                    for i in range(NT + 1):
                        if i < NT:
                            layer_norm(i + 1)
                            gate_y(i + 1)
                        update(i)
                        if i < NT:
                            split_mix(i + 1)
                        second_norm(i)
                    v.wait_ge(S["h_pe"], NT + 1)
                    v.wait_ge(h2_out[NT % 2], 16 * (NT // 2))
                    for k in range(KT):
                        view = h2[:, NT % 2, k, 0:NS].rearrange("p (b t) -> p b t", t=DS)
                        step(v.tensor_tensor(view, h_ps[:, k, 0:NS].rearrange("p (b t) -> p b t", t=DS),
                                             gain2[:, k, 0:DB].unsqueeze(2).to_broadcast([P, DB, DS]), ALU.mult))
                        ins = v.tensor_tensor(view, view, modT[:, M_SH2 + k, 0:DB].unsqueeze(2).to_broadcast([P, DB, DS]), ALU.add)
                    ins.then_inc(S["h2_d_"], 1)

                @block.tensor
                def _(pe):
                    def turn_dw(i):
                        n = rows_of(i)
                        pe.wait_ge(dw_in[i % 2], 16 * (i // 2 + 1))
                        if i >= 1:
                            pe.wait_ge(S["yn_d"], i)
                        for c in range(CC):
                            mm = pe.transpose(dw_ps[0:n, c * P:(c + 1) * P], dwt[:, i % 2, c, 0:n], ident[:])
                        mm.then_inc(S["dw_pe"], 1)

                    def turn_y(i):
                        n = rows_of(i)
                        pe.wait_ge(S["yn_d"], i + 1)
                        if i >= 1:
                            pe.wait_ge(S["yg_d"], i)
                        for c in range(CC):
                            mm = pe.transpose(y_ps[:, c, 0:n], y_n[0:n, c * P:(c + 1) * P], ident[0:n, 0:n])
                        mm.then_inc(S["y_pe"], 1)

                    def turn_o(i):
                        n = rows_of(i)
                        pe.wait_ge(S["o_d"], i + 1)
                        if i >= 1:
                            pe.wait_ge(S["mlo_d"], 2 * i - 1)
                        for c in range(4):
                            mm = pe.transpose(a_ps[:, c, 0:n], o_n[0:n, c * P:(c + 1) * P], ident[0:n, 0:n])
                        mm.then_inc(S["a_pe"], 1)

                    def pointwise(i):
                        n = rows_of(i)
                        pe.wait_ge(S["ylo_d"], i + 1)
                        if i == 0:
                            pe.wait_ge(S["w_lod"], 2)
                        if i >= 1:
                            pe.wait_ge(S["mlo_d"], 2 * i)
                        for c in range(CC):
                            out, cols = c_ps[:, c, 0:n], slice(c * P, (c + 1) * P)
                            for k in range(CC):
                                pe.matmul(out, wp_hi[:, k, cols], y_hi[:, k, 0:n], start=k == 0, stop=False)
                                pe.matmul(out, wp_hi[:, k, cols], y_lo[:, k, 0:n], start=False, stop=False)
                                mm = pe.matmul(out, wp_lo[:, k, cols], y_hi[:, k, 0:n], start=False, stop=k == CC - 1)
                        mm.then_inc(S["c_pe"], 1)

                    def project(i, c):
                        n = rows_of(i)
                        if i >= 1:
                            pe.wait_ge(S["upd_d"], i)
                        for k in range(KT):
                            if c == 0 and k == 0:
                                pe.wait_ge(S["mlo_d"], 2 * i + 1)
                            if c == 0 and k == 4:
                                pe.wait_ge(S["mlo_d"], 2 * i + 2)
                            if i == 0 and c == 0:
                                pe.wait_ge(S["w_lod"], k + 3)
                            hi, lo, cols = m_hi[:, i % 2, k, 0:n], m_lo[:, i % 2, k, 0:n], slice(c * 512, (c + 1) * 512)
                            pe.matmul(z_ps[c][0:n], hi, wo_hi[:, k, cols], start=k == 0, stop=False)
                            pe.matmul(z_ps[c][0:n], hi, wo_lo[:, k, cols], start=False, stop=False)
                            mm = pe.matmul(z_ps[c][0:n], lo, wo_hi[:, k, cols], start=False, stop=k == KT - 1)
                        mm.then_inc(S["z_pe"], 1)

                    def turn_x(i):
                        n = rows_of(i)
                        pe.wait_ge(S["x1n_d"], i + 1)
                        if i >= 1:
                            pe.wait_ge(S["h2_d_"], i)
                        for k in range(KT):
                            mm = pe.transpose(h_ps[:, k, 0:n], x1n[0:n, k * P:(k + 1) * P], ident[0:n, 0:n])
                        mm.then_inc(S["h_pe"], 1)

                    turn_dw(0)
                    turn_y(0)
                    turn_o(0)
                    pointwise(0)
                    for i in range(NT + 1):
                        if i < NT:
                            turn_dw(i + 1)
                        project(i, 0)
                        if i < NT:
                            turn_y(i + 1)
                        project(i, 1)
                        if i < NT:
                            turn_o(i + 1)
                            pointwise(i + 1)
                        if i >= 1:
                            turn_x(i - 1)
                    turn_x(NT)

        end_stage()

        with ExitStack() as st:
            def sb(name, shape, dt=F32):
                return st.enter_context(nc.sbuf_tensor("ff_" + name, shape, dt))

            def ps(name, shape, dt=F32):
                return st.enter_context(nc.psum_tensor("ff_" + name, shape, dt))

            FB = 4
            NBLK = FF // P // FB
            MAXT = SEQ // 2 + NS
            w_raw = sb("w_raw", [P, 2, D])
            w_hi = sb("w_hi", [P, 2, D], F32R)
            w_lo = sb("w_lo", [P, 2, D], F32R)
            y = sb("y", [P, KT, MAXT])
            h_hi = sb("h_hi", [P, KT, MAXT], F32R)
            h_lo = sb("h_lo", [P, KT, MAXT], F32R)
            relu = sb("relu", [P, 2, 512])
            sqr = sb("sqr", [P, 2, 512])
            a_hi = sb("a_hi", [P, FB, MAXT], F32R)
            a_lo = sb("a_lo", [P, FB, MAXT], F32R)
            u_ps = [ps(f"u_ps{i}", [P, 512]) for i in range(6)]
            out_ps = ps("out_ps", [P, D])
            x1_t = sb("x1_t", [P, 2, D])

            for run, (t0, width, NCH) in enumerate(((0, 512, 2), (SEQ // 2, 352, 3))):
                if run:
                    end_stage()
                T = width * NCH
                tiles = [(j * P, P) for j in range(SEQ // 2 // P)] + ([(SEQ // 2, NS)] if run else [])

                def sm(name):
                    return sem(f"ff{run}_{name}")

                h_in, hhi_d, hlo_d, w_hid, w_lod, u_pe = sm("h_in"), sm("hhi_d"), sm("hlo_d"), sm("w_hid"), sm("w_lod"), sm("u_pe")
                relu_d, sqr_d, ahi_d, alo_d, y_d, ygate_d = sm("relu_d"), sm("sqr_d"), sm("ahi_d"), sm("alo_d"), sm("y_d"), sm("ygate_d")
                t_pe, out_d, fv = sm("t_pe"), sm("out_d"), sm("fv")
                w_ld, x1_in = ([sm(f"{x}{i}") for i in range(2)] for x in ("w_ld", "x1_in"))
                out_s = [stored[f"y_out{run}{i}"] for i in range(2)]
                UP, DOWN = FB * NCH, KT * NCH
                PER = UP + DOWN
                WT = FB + KT // 2

                def groups_before(n):
                    blk, m = divmod(n, WT)
                    return blk * PER + (m * NCH if m < FB else UP + (m - FB) * 2 * NCH)

                def store(sp, j):
                    o, n = tiles[j]
                    sp.wait_ge(out_d, j + 1)
                    dst = O["y_prompt"][0, t0 + o:t0 + o + n] if t0 + o < SEQ else O["y_sample"].rearrange("b t d -> (b t) d")
                    sp.dma_start(dst, x1_t[0:n, j % 2]).then_inc(out_s[j % 2], 16)

                def bank_free(eng, g):
                    blk, r = divmod(g, PER)
                    if r < UP:
                        eng.wait_ge(alo_d, blk * UP + r + 1)
                    else:
                        eng.wait_ge(y_d, blk * DOWN + r - UP + 1)

                with nc.Block() as block:
                    @block.sync
                    def _(sp):
                        for k in range(KT):
                            sp.dma_start(y[:, k, 0:T], h2_d[:, k, t0:t0 + T]).then_inc(h_in, 16)
                        for n in range(NBLK * WT):
                            blk, m = divmod(n, WT)
                            if n >= 2:
                                sp.wait_ge(w_lod, n - 1)
                            if m < FB:
                                f = blk * FB + m
                                src = I["w_ff1"][0, :, f * P:(f + 1) * P].rearrange("(k p) c -> p k c", p=P)
                                sp.dma_start(w_raw[:, n % 2].rearrange("p (k c) -> p k c", k=KT), src).then_inc(w_ld[n % 2], 16)
                            else:
                                src = I["w_ff2"][0, blk * FB * P:(blk + 1) * FB * P, (m - FB) * 2 * P:(m - FB + 1) * 2 * P].rearrange("(f p) c -> p f c", p=P)
                                sp.dma_start(w_raw[:, n % 2].rearrange("p (f c) -> p f c", f=FB), src).then_inc(w_ld[n % 2], 16)
                        for j, (o, n) in enumerate(tiles):
                            if j >= 2:
                                sp.wait_ge(out_s[j % 2], 16 * (j // 2))
                            sp.dma_start(x1_t[0:n, j % 2], x1_d[t0 + o:t0 + o + n]).then_inc(x1_in[j % 2], 16)
                            if j >= 1:
                                store(sp, j - 1)
                        store(sp, len(tiles) - 1)
                        for i in range(2):
                            sp.wait_ge(out_s[i], 16 * len(tiles[i::2]))

                    @block.gpsimd
                    def _(pool):
                        for n in (12 + 2 * run, 13 + 2 * run):
                            copy_cache(pool, n)

                        def split_w(n):
                            pool.wait_ge(w_hid, n + 1)
                            if n >= 2:
                                pool.wait_ge(u_pe, groups_before(n - 1))
                            pool.tensor_tensor(w_lo[:, n % 2], w_raw[:, n % 2], w_hi[:, n % 2].bitcast(F32), ALU.subtract).then_inc(w_lod, 1)

                        split_w(0)
                        for n in range(NBLK * WT):
                            if n + 1 < NBLK * WT:
                                split_w(n + 1)
                            blk, m = divmod(n, WT)
                            if m < FB:
                                for c in range(NCH):
                                    e = (blk * FB + m) * NCH + c
                                    pool.wait_ge(ahi_d, e + 1)
                                    pool.wait_ge(sqr_d, e + 1)
                                    pool.tensor_tensor(a_lo[:, m, c * width:(c + 1) * width], sqr[:, e % 2, 0:width],
                                                       a_hi[:, m, c * width:(c + 1) * width].bitcast(F32), ALU.subtract).then_inc(alo_d, 1)

                    @block.scalar
                    def _(act):
                        def split_w(n):
                            act.wait_ge(w_ld[n % 2], 16 * (n // 2 + 1))
                            if n >= 2:
                                act.wait_ge(u_pe, groups_before(n - 1))
                            act.activation(w_hi[:, n % 2], w_raw[:, n % 2], ACT.Copy).then_inc(w_hid, 1)

                        split_w(0)
                        for k in range(KT):
                            if k == 0:
                                act.wait_ge(h_in, 16 * KT)
                            act.activation(h_hi[:, k, 0:T], y[:, k, 0:T], ACT.Copy).then_inc(hhi_d, 1)
                        for n in range(NBLK * WT):
                            if n + 1 < NBLK * WT:
                                split_w(n + 1)
                            blk, m = divmod(n, WT)
                            if m < FB:
                                for c in range(NCH):
                                    e = (blk * FB + m) * NCH + c
                                    g = blk * PER + m * NCH + c
                                    act.wait_ge(u_pe, g + 1)
                                    if e >= 2:
                                        act.wait_ge(sqr_d, e - 1)
                                    act.activation(relu[:, e % 2, 0:width], u_ps[g % 6][:, 0:width], ACT.Relu).then_inc(relu_d, 1)
                                    act.wait_ge(relu_d, e + 1)
                                    if m == 0 and c == 0 and blk >= 1:
                                        act.wait_ge(u_pe, blk * PER)
                                    act.activation(a_hi[:, m, c * width:(c + 1) * width], relu[:, e % 2, 0:width], ACT.Square).then_inc(ahi_d, 1)
                        act.wait_ge(y_d, NBLK * DOWN)
                        for k in range(KT):
                            ins = act.activation(y[:, k, 0:SEQ // 2], y[:, k, 0:SEQ // 2], ACT.Copy, scale=modT[:, M_G2 + k, 8:9])
                        ins.then_inc(ygate_d, 1)

                    @block.vector
                    def _(v):
                        for k in range(KT):
                            v.wait_ge(hhi_d, k + 1)
                            v.tensor_tensor(h_lo[:, k, 0:T], y[:, k, 0:T], h_hi[:, k, 0:T].bitcast(F32), ALU.subtract).then_inc(hlo_d, 1)
                        v.wait_ge(hlo_d, KT)
                        for blk in range(NBLK):
                            for e in range(blk * UP, (blk + 1) * UP):
                                v.wait_ge(relu_d, e + 1)
                                if e >= 2:
                                    v.wait_ge(alo_d, e - 1)
                                v.tensor_tensor(sqr[:, e % 2, 0:width], relu[:, e % 2, 0:width], relu[:, e % 2, 0:width], ALU.mult).then_inc(sqr_d, 1)
                            for e in range(DOWN):
                                k, c = divmod(e, NCH)
                                g = blk * PER + UP + e
                                v.wait_ge(u_pe, g + 1)
                                dst, src = y[:, k, c * width:(c + 1) * width], u_ps[g % 6][:, 0:width]
                                if blk == 0:
                                    v.tensor_copy(dst, src).then_inc(y_d, 1)
                                else:
                                    v.wait_ge(y_d, (blk - 1) * DOWN + e + 1)
                                    v.tensor_tensor(dst, src, dst, ALU.add).then_inc(y_d, 1)
                        if run:
                            v.wait_ge(y_d, NBLK * DOWN)
                            for k in range(KT):
                                view = y[:, k, SEQ // 2:MAXT].rearrange("p (b t) -> p b t", t=DS)
                                ins = v.tensor_tensor(view, view, modT[:, M_G2 + k, 0:DB].unsqueeze(2).to_broadcast([P, DB, DS]), ALU.mult)
                            ins.then_inc(fv, 1)
                        for j, (o, n) in enumerate(tiles):
                            v.wait_ge(t_pe, j + 1)
                            v.wait_ge(x1_in[j % 2], 16 * (j // 2 + 1))
                            v.tensor_tensor(x1_t[0:n, j % 2], out_ps[0:n], x1_t[0:n, j % 2], ALU.add).then_inc(out_d, 1)

                    @block.tensor
                    def _(pe):
                        for n in range(NBLK * WT):
                            blk, m = divmod(n, WT)
                            pe.wait_ge(w_lod, n + 1)
                            up = m < FB
                            if not up and m == FB:
                                pe.wait_ge(alo_d, (blk + 1) * UP)
                            b = n % 2
                            for half in range(1 if up else 2):
                                for c in range(NCH):
                                    g = groups_before(n) + half * NCH + c
                                    if g >= 6:
                                        bank_free(pe, g - 6)
                                    out = u_ps[g % 6][:, 0:width]
                                    tok = slice(c * width, (c + 1) * width)
                                    last = KT if up else FB
                                    for k in range(last):
                                        if up:
                                            if n == 0 and c == 0:
                                                pe.wait_ge(hlo_d, k + 1)
                                            w = slice(k * P, (k + 1) * P)
                                            hi, lo = h_hi[:, k, tok], h_lo[:, k, tok]
                                        else:
                                            w = slice(k * 2 * P + half * P, k * 2 * P + (half + 1) * P)
                                            hi, lo = a_hi[:, k, tok], a_lo[:, k, tok]
                                        pe.matmul(out, w_hi[:, b, w], hi, start=k == 0, stop=False)
                                        pe.matmul(out, w_hi[:, b, w], lo, start=False, stop=False)
                                        mm = pe.matmul(out, w_lo[:, b, w], hi, start=False, stop=k == last - 1)
                                    mm.then_inc(u_pe, 1)
                        pe.wait_ge(ygate_d, 1)
                        if run:
                            pe.wait_ge(fv, 1)
                        for j, (o, n) in enumerate(tiles):
                            if j >= 1:
                                pe.wait_ge(out_d, j)
                            for k in range(KT):
                                mm = pe.transpose(out_ps[0:n, k * P:(k + 1) * P], y[:, k, o:o + n], ident[:])
                            mm.then_inc(t_pe, 1)

        with nc.Block() as block:
            @block.sync
            def _(sp):
                sp.wait_ge(copied, 16 * 2 * DB)


_INS = ["x_prompt", "x_sample", "cache_k", "cache_v", "state_conv", "c_prompt", "c_sample", "rel_bias", "norm1_g",
        "norm2_g", "w_ada", "b_ada", "w_in", "q_norm_g", "k_norm_g", "conv_dw", "conv_dw_b", "conv_ln_g", "conv_ln_b",
        "w_pw2", "w_o", "w_ff1", "w_ff2"]
_OUTS = [("y_prompt", (1, SEQ, D)), ("y_sample", (DB, DS, D)), ("new_k_prompt", (1, 1, WINC, H, DH)),
         ("new_v_prompt", (1, 1, WINC, H, DH)), ("new_conv_prompt", (1, 1, HIST, CW)),
         ("new_k_sample", (1, DB, WINC, H, DH)), ("new_v_sample", (1, DB, WINC, H, DH)),
         ("new_conv_sample", (1, DB, HIST, CW))]


def kernel(**inputs):
    import numpy as _np
    import concourse.bacc as _bacc
    from concourse.bass_utils import run_bass_kernel_spmd as _run

    nc = _bacc.Bacc("TRN2", target_bir_lowering=False, num_devices=1)
    arrays, ins, outs = {}, {}, {}
    given = {name: _np.ascontiguousarray(inputs[name]) for name in _INS}
    given.update(shape_constants())
    for name, a in given.items():
        arrays[f"in_{name}_dram"] = a
        ins[name] = nc.dram_tensor(f"in_{name}_dram", a.shape, mybir.dt.from_np(a.dtype), kind="ExternalInput").ap()
    for name, shape in _OUTS:
        outs[name] = nc.dram_tensor(f"out_{name}_dram", shape, F32, kind="ExternalOutput").ap()
    build(nc, ins, outs)
    r = _run(nc, [arrays], core_ids=[0])
    return tuple(r.results[0][f"out_{name}_dram"] for name, _ in _OUTS)
```

```python
from contextlib import ExitStack

import numpy as np

import concourse.bass as bass
from concourse import mybir

F32 = mybir.dt.float32
F32R = mybir.dt.float32r
U32 = mybir.dt.uint32
I32 = mybir.dt.int32
ALU = mybir.AluOpType
ACT = mybir.ActivationFunctionType
AX = mybir.AxisListType

P = 128
D = 1024
KT = D // P
SEQ = 2048
NT = SEQ // P
DB, DS = 8, 4
NS = DB * DS
WINC = 2048
H, DH = 8, 64
AW = H * DH
CW = 512
CC = CW // P
TAPS = 31
HIST = TAPS - 1
IN_W = 3 * AW + 2 * CW
FF = 4 * D
NMOD = 6 * D
NB = 128
PATTERNS = ((128, 1), (512, 4), (2048, 16))
BUCKETS = 32
MAXD = 2048
EPS = 1e-6
NEG = -1.0e30
MAGIC = 0x5F3759DF
TOK = SEQ + NS
V_N1, V_N2, V_CB, V_LG, V_LB, V_ALL = 0, 8, 16, 20, 24, 28
M_SH1, M_SC1, M_SH2, M_SC2, M_G2, M_ALL = 0, 8, 16, 24, 32, 40
M_SRC = (0, 1, 3, 4, 5)
SKEYS = 4 * P + 4 * P + DS
RW = 384


def rows_of(i):
    return P if i < NT else NS


def rel_bucket(dist):
    exact = BUCKETS // 2
    df = np.maximum(dist, 1).astype(np.float32)
    scale = np.float32(np.log(MAXD / exact))
    large = exact + (np.log(df / np.float32(exact)) / scale * np.float32(BUCKETS - exact)).astype(np.int32)
    return np.where(dist < exact, dist, np.minimum(large, BUCKETS - 1))


def shape_constants():
    hot_p = np.zeros((BUCKETS + 1, 3, RW), np.float32)
    for p, (_, d) in enumerate(PATTERNS):
        delta = 2 * NB - 1 - np.arange(RW)
        ok = (delta >= 0) & (delta <= NB)
        b = rel_bucket(np.maximum(delta, 0) * d)
        for y in range(RW):
            if ok[y]:
                hot_p[b[y], p, y] = -1.0
            else:
                hot_p[BUCKETS, p, y] = -NEG
    hot_s = np.zeros((DS, BUCKETS, 3, SKEYS), np.float32)
    out_s = np.zeros((DS, 3, SKEYS), np.float32)
    for t in range(DS):
        for col in range(SKEYS):
            if col < 512:
                kind, dist = 0, 512 + t - 4 * (col % 128) - col // 128
            elif col < 1024:
                kind, dist = 1, WINC + t - 16 * (col % 128) - (col - 512) // 128
            else:
                kind, dist = 2, t - (col - 1024)
            for p, (w, d) in enumerate(PATTERNS):
                ok = 0 <= dist <= w and dist % d == 0
                ok = ok and (kind == 2 or (kind == 1) == (p == 2))
                if ok:
                    hot_s[t, int(rel_bucket(np.array(dist))), p, col] = -1.0
                else:
                    out_s[t, p, col] = -NEG
    sel_t = np.zeros((DS, P), np.float32)
    for t in range(DS):
        sel_t[t, t::DS] = 1.0
    own_t = np.repeat(np.eye(DS, dtype=np.float32), BUCKETS, axis=0)
    return {"hot_p": hot_p.reshape(BUCKETS + 1, -1), "hot_s": hot_s.reshape(P, -1),
            "out_s": out_s.reshape(DS, -1), "sel_t": sel_t, "own_t": own_t,
            "mask_h": np.tile(np.repeat(np.eye(H, dtype=np.float32), DS, axis=0), (P // NS, 1))}


def build(nc, I, O):
    scratch = {}

    def dram(name, shape):
        scratch[name] = nc.dram_tensor(name, shape, F32, kind="Internal").ap()
        return scratch[name]

    mod_d = dram("mod_d", (9, NMOD))
    bias_d = dram("bias_d", (H, P, 3 * RW))
    sbias_d = dram("sbias_d", (P, 3 * SKEYS))
    qt_d = dram("qt_d", (P, 4, TOK))
    kt_d = dram("kt_d", (P, 4, TOK))
    acc_d = dram("acc_d", (3, SEQ, AW))
    st_d = dram("st_d", (3, SEQ, 2 * H))
    os_d = dram("os_d", (NS, AW))
    dw_d = dram("dw_d", (P, CC, TOK))
    x1_d = dram("x1_d", (TOK, D))
    h2_d = dram("h2_d", (P, KT, TOK))

    whole = ExitStack()
    with whole:
        stage_sems = []

        def sem(name):
            stage_sems.append(nc.alloc_semaphore(name=name))
            return stage_sems[-1]

        def end_stage():
            nc.clear_and_free_semaphores(list(stage_sems))
            stage_sems.clear()
            nc.all_engine_barrier()

        def keep(name, shape, dt=F32):
            return whole.enter_context(nc.sbuf_tensor(name, shape, dt))

        ident = keep("ident", [P, P])
        modT = keep("modT", [P, M_ALL, 9])
        vecT = keep("vecT", [P, V_ALL])
        tapT = keep("tapT", [P, TAPS * CC])
        gain1 = keep("gain1", [P, KT, 9])
        gain2 = keep("gain2", [P, KT, 9])
        rstd1 = keep("rstd1", [P, NT + 1])
        STORES = ("copied", "v_out0", "v_out1", "k_out0", "k_out1", "tail_out", "y_out0", "y_out1", "y_out2", "y_out3")
        stored = {name: whole.enter_context(nc.semaphore(name)) for name in STORES}
        copied = stored["copied"]

        def copy_cache(eng, n):
            b = n // 2
            for name, out in ((("cache_k", "new_k_sample"), ("cache_v", "new_v_sample"))[n % 2],):
                src = I[name][0, b].rearrange("r h d -> (r h d)")[DS * AW:WINC * AW]
                dst = O[out][0, b].rearrange("r h d -> (r h d)")[0:(WINC - DS) * AW]
                eng.dma_start(dst.rearrange("(a n) -> a n", a=16), src.rearrange("(a n) -> a n", a=16)).then_inc(copied, 16)

        class Chain:

            def __init__(self, eng, s):
                self.eng, self.s, self.n, self.last = eng, s, 0, 0

            def __call__(self, ins):
                self.n += 1
                ins.then_inc(self.s, 1)
                self.eng.wait_ge(self.s, self.n)

            def mark(self, ins):
                self.n += 1
                ins.then_inc(self.s, 1)
                return self.n

            def need(self, n):
                if n > 0:
                    self.eng.wait_ge(self.s, n)

        def rsqrt(v, step, y, a, t):
            step(v.tensor_scalar(t.bitcast(U32), a.bitcast(U32), 1, None, ALU.logical_shift_right))
            step(v.tensor_scalar(y.bitcast(I32), t.bitcast(I32), -1.0, float(MAGIC), ALU.mult, ALU.add))
            for _ in range(3):
                step(v.tensor_tensor(t, y, y, ALU.mult))
                step(v.tensor_tensor(t, t, a, ALU.mult))
                step(v.tensor_scalar(t, t, -0.5, 1.5, ALU.mult, ALU.add))
                step(v.tensor_tensor(y, y, t, ALU.mult))

        with ExitStack() as st:
            def sb(name, shape, dt=F32):
                return st.enter_context(nc.sbuf_tensor(name, shape, dt))

            def ps(name, shape, dt=F32):
                return st.enter_context(nc.psum_tensor(name, shape, dt))

            NW = 3
            WC = NMOD // 512
            c_sb = sb("c_sb", [9, D])
            sig_c = sb("sig_c", [9, D])
            silu_c = sb("silu_c", [9, D])
            cT = sb("cT", [P, KT, 9])
            w_ring = sb("w_ring", [P, NW, KT, 512])
            b_rows = sb("b_rows", [9, NMOD])
            mod = sb("mod", [9, NMOD])
            vecs = sb("vecs", [V_ALL, P])
            taps = sb("taps", [TAPS * CC, P])
            x_st = sb("x_st", [P, 2, D])
            x_sq = sb("x_sq", [P, D])
            ssq = sb("ssq", [P, NT + 1])
            rs_t = sb("rs_t", [P, NT + 1])
            rel33 = sb("rel33", [BUCKETS + 1, H])
            relB = sb("relB", [BUCKETS + 1, H, P])
            relS = sb("relS", [P, H])
            ownT = sb("ownT", [P, DS])
            selT = sb("selT", [DS, P])
            pairE = sb("pairE", [P, 4, H, DS])
            hotP = sb("hotP", [BUCKETS + 1, 3 * RW])
            hotS = sb("hotS", [P, 3 * SKEYS])
            outS = sb("outS", [DS, 3 * SKEYS])
            biasB = sb("biasB", [P, 2, 3 * RW])
            biasS = sb("biasS", [P, 3 * SKEYS])
            cT_ps = ps("cT_ps", [P, 512])
            mod_ps = [ps(f"mod_ps{i}", [P, 512]) for i in range(2)]
            vec_ps = ps("vec_ps", [P, 512])
            tb_ps = [ps(f"tb_ps{i}", [P, 512]) for i in range(2)]
            modT_ps = ps("modT_ps", [P, 512])
            id_zero, id_done = sem("id_zero"), sem("id_done")
            c_in, sig_done, silu_done, cT_pe, cT_done = sem("c_in"), sem("sig_done"), sem("silu_done"), sem("cT_pe"), sem("cT_done")
            w_in_ = [sem(f"wada_in{i}") for i in range(NW)]
            small_in, mod_pe, mod_done = sem("small_in"), sem("mod_pe"), sem("mod_done")
            vec_pe, vec_done, modT_pe, modT_done = sem("vec_pe"), sem("vec_done"), sem("modT_pe"), sem("modT_done")
            xs_in = [sem("xs_in0"), sem("xs_in1")]
            sq_done = sem("sq_done")
            rel_ready, tb_pe, tb_done, mod_out, v0 = sem("rel_ready"), sem("tb_pe"), sem("tb_done"), sem("mod_out"), sem("v0")
            tb_out = [sem("tb_out0"), sem("tb_out1")]
            TBN = 3 * H + 9
            SMALL = 15

            with nc.Block() as block:
                @block.gpsimd
                def _(pool):
                    pool.memset(ident[:], 0.0).then_inc(id_zero, 1)
                    pool.wait_ge(id_zero, 1)
                    pool.affine_select(out=ident[:], in_=ident[:], compare_op=ALU.not_equal, fill=1.0, base=0,
                                       pattern=[[-1, P]], channel_multiplier=1).then_inc(id_done, 1)
                    pool.wait_ge(id_done, 1)

                @block.sync
                def _(sp):
                    sp.dma_start(c_sb[8:9, :], I["c_prompt"]).then_inc(c_in, 16)
                    sp.dma_start(c_sb[0:8, :], I["c_sample"]).then_inc(c_in, 16)
                    w_view = I["w_ada"][0].rearrange("(k p) n -> p k n", p=P)
                    for n in range(WC):
                        if n >= NW:
                            sp.wait_ge(mod_pe, n - NW + 1)
                        sp.dma_start(w_ring[:, n % NW], w_view[:, :, n * 512:(n + 1) * 512]).then_inc(w_in_[n % NW], 16)
                    sp.wait_ge(mod_done, WC)
                    sp.dma_start(mod_d, mod[:]).then_inc(mod_out, 16)
                    sp.wait_ge(mod_out, 16)

                @block.scalar
                def _(act):
                    small = [(vecs[V_N1:V_N1 + 8, :], I["norm1_g"][0].rearrange("(k p) -> k p", p=P)),
                             (vecs[V_N2:V_N2 + 8, :], I["norm2_g"][0].rearrange("(k p) -> k p", p=P)),
                             (vecs[V_CB:V_CB + 4, :], I["conv_dw_b"][0].rearrange("(k p) -> k p", p=P)),
                             (vecs[V_LG:V_LG + 4, :], I["conv_ln_g"][0].rearrange("(k p) -> k p", p=P)),
                             (vecs[V_LB:V_LB + 4, :], I["conv_ln_b"][0].rearrange("(k p) -> k p", p=P)),
                             (taps[:], I["conv_dw"][0].rearrange("j (k p) -> (j k) p", p=P)),
                             (rel33[0:BUCKETS, :], I["rel_bias"]),
                             (hotP[:], I["hot_p"]), (hotS[:], I["hot_s"]), (outS[:], I["out_s"]),
                             (ownT[:], I["own_t"]), (selT[:], I["sel_t"])]
                    for t in range(2):
                        small.append((relS[64 * t:64 * t + 32, :], I["rel_bias"]))
                        small.append((relS[64 * t + 32:64 * t + 64, :], I["rel_bias"]))
                    small.append((b_rows[:], I["b_ada"].to_broadcast([9, NMOD])))
                    for dst, src in small:
                        act.dma_start(dst, src).then_inc(small_in, 16)
                    assert len(small) == SMALL + 2
                    act.wait_ge(c_in, 32)
                    act.activation(sig_c[:], c_sb[:], ACT.Sigmoid).then_inc(sig_done, 1)
                    for i in range(NT + 1):
                        n = rows_of(i)
                        if i >= 2:
                            act.wait_ge(sq_done, i - 1)
                        src = I["x_prompt"][0, i * P:(i + 1) * P, :] if i < NT else I["x_sample"].rearrange("b t d -> (b t) d")
                        act.dma_start(x_st[0:n, i % 2], src).then_inc(xs_in[i % 2], 16)
                        if i >= 1:
                            m = rows_of(i - 1)
                            act.wait_ge(xs_in[(i - 1) % 2], 16 * ((i - 1) // 2 + 1))
                            if i >= 2:
                                act.wait_ge(sq_done, i - 1)
                            else:
                                act.wait_ge(v0, 1)
                            act.activation(x_sq[0:m], x_st[0:m, (i - 1) % 2], ACT.Square,
                                           accum_out=ssq[0:m, i - 1:i]).then_inc(sq_done, 1)
                    act.wait_ge(xs_in[0], 16 * 9)
                    act.wait_ge(sq_done, NT)
                    act.activation(x_sq[0:NS], x_st[0:NS, 0], ACT.Square, accum_out=ssq[0:NS, NT:NT + 1]).then_inc(sq_done, 1)
                    for h in range(H):
                        act.wait_ge(tb_done, 3 * h + 3)
                        act.dma_start(bias_d[h], biasB[:, h % 2]).then_inc(tb_out[h % 2], 16)
                    act.wait_ge(tb_done, TBN)
                    act.dma_start(sbias_d, biasS[:]).then_inc(tb_out[0], 16)
                    act.wait_ge(tb_out[0], 16 * (H // 2 + 1))
                    act.wait_ge(tb_out[1], 16 * (H // 2))

                @block.tensor
                def _(pe):
                    pe.wait_ge(id_done, 1)
                    pe.wait_ge(silu_done, 1)
                    for k in range(KT):
                        mm = pe.transpose(cT_ps[:, k * 9:(k + 1) * 9], silu_c[:, k * P:(k + 1) * P], ident[0:9, 0:9])
                    mm.then_inc(cT_pe, 1)
                    pe.wait_ge(small_in, 16 * (SMALL + 2))
                    pe.transpose(vec_ps[:, 0:V_ALL], vecs[:], ident[0:V_ALL, 0:V_ALL])
                    pe.transpose(vec_ps[:, 128:128 + TAPS * CC], taps[:], ident[0:TAPS * CC, 0:TAPS * CC]).then_inc(vec_pe, 1)
                    pe.wait_ge(cT_done, 1)

                    def tables(g):
                        if g >= 2:
                            pe.wait_ge(tb_done, g - 1)
                        pe.wait_ge(rel_ready, 1)
                        if g < 3 * H:
                            h, p = divmod(g, 3)
                            pe.matmul(tb_ps[g % 2][:, 0:RW], relB[:, h, :], hotP[:, p * RW:(p + 1) * RW],
                                      start=True, stop=True).then_inc(tb_pe, 1)
                        else:
                            lo = (g - 3 * H) * 344
                            hi = min(lo + 344, 3 * SKEYS)
                            pe.matmul(tb_ps[g % 2][:, 0:hi - lo], pairE[:].rearrange("p b h t -> p (b h t)"), hotS[:, lo:hi], start=True, stop=False)
                            pe.matmul(tb_ps[g % 2][:, 0:hi - lo], selT[:], outS[:, lo:hi],
                                      start=False, stop=True).then_inc(tb_pe, 1)

                    g = 0
                    for n in range(WC):
                        pe.wait_ge(w_in_[n % NW], 16 * (n // NW + 1))
                        if n >= 2:
                            pe.wait_ge(mod_done, n - 1)
                        for k in range(KT):
                            mm = pe.matmul(mod_ps[n % 2][0:9, :], cT[:, k, :], w_ring[:, n % NW, k, :], start=k == 0, stop=k == KT - 1)
                        mm.then_inc(mod_pe, 1)
                        for _ in range(3):
                            if g < TBN:
                                tables(g)
                                g += 1
                    while g < TBN:
                        tables(g)
                        g += 1
                    pe.wait_ge(mod_done, WC)
                    for j in range(M_ALL):
                        c0 = M_SRC[j // 8] * D + (j % 8) * P
                        mm = pe.transpose(modT_ps[:, j * 9:(j + 1) * 9], mod[:, c0:c0 + P], ident[0:9, 0:9])
                    mm.then_inc(modT_pe, 1)

                @block.vector
                def _(v):
                    step = Chain(v, v0)
                    step(v.memset(ssq[:], 1.0))
                    v.wait_ge(small_in, 16 * (SMALL + 2))
                    step(v.memset(rel33[BUCKETS:BUCKETS + 1, :], 1.0))
                    v.tensor_copy(relB[:], rel33[:].unsqueeze(2).to_broadcast([BUCKETS + 1, H, P]))
                    for t in range(DS):
                        ins = v.tensor_scalar(pairE[:, :, :, t], relS[:].unsqueeze(1).to_broadcast([P, 4, H]), ownT[:, t:t + 1], None, ALU.mult)
                    step(ins)
                    v.sem_inc(rel_ready, 1)
                    v.wait_ge(sig_done, 1)
                    v.tensor_tensor(silu_c[:], c_sb[:], sig_c[:], ALU.mult).then_inc(silu_done, 1)
                    v.wait_ge(cT_pe, 1)
                    v.tensor_copy(cT[:].rearrange("p k b -> p (k b)"), cT_ps[:, 0:KT * 9]).then_inc(cT_done, 1)
                    v.wait_ge(vec_pe, 1)
                    v.tensor_copy(vecT[:], vec_ps[:, 0:V_ALL])
                    step(v.tensor_copy(tapT[:], vec_ps[:, 128:128 + TAPS * CC]))

                    def table_copy(g):
                        v.wait_ge(tb_pe, g + 1)
                        if g < 3 * H:
                            h, p = divmod(g, 3)
                            if h >= 2:
                                v.wait_ge(tb_out[h % 2], 16 * (h // 2))
                            v.tensor_copy(biasB[:, h % 2, p * RW:(p + 1) * RW], tb_ps[g % 2][:, 0:RW]).then_inc(tb_done, 1)
                        else:
                            lo = (g - 3 * H) * 344
                            hi = min(lo + 344, 3 * SKEYS)
                            v.tensor_copy(biasS[:, lo:hi], tb_ps[g % 2][:, 0:hi - lo]).then_inc(tb_done, 1)

                    g = 0
                    for n in range(WC):
                        v.wait_ge(mod_pe, n + 1)
                        v.tensor_tensor(mod[:, n * 512:(n + 1) * 512], mod_ps[n % 2][0:9, :],
                                        b_rows[:, n * 512:(n + 1) * 512], ALU.add).then_inc(mod_done, 1)
                        for _ in range(3):
                            if g < TBN:
                                table_copy(g)
                                g += 1
                    while g < TBN:
                        table_copy(g)
                        g += 1
                    v.wait_ge(sq_done, NT + 1)
                    step(v.tensor_scalar(ssq[:], ssq[:], 1.0 / D, EPS, ALU.mult, ALU.add))
                    rsqrt(v, step, rstd1[:], ssq[:], rs_t[:])
                    v.wait_ge(modT_pe, 1)
                    step(v.tensor_copy(modT[:].rearrange("p j b -> p (j b)"), modT_ps[:, 0:M_ALL * 9]))
                    for gain, m0, g0 in ((gain1, M_SC1, V_N1), (gain2, M_SC2, V_N2)):
                        step(v.scalar_tensor_tensor(out=gain[:], in0=modT[:, m0:m0 + 8, :], scalar=1.0,
                                                    in1=vecT[:, g0:g0 + 8].unsqueeze(2).to_broadcast([P, KT, 9]),
                                                    op0=ALU.add, op1=ALU.mult))

        end_stage()

        def projection(tag, col0, ncols, body):
            st = ExitStack()
            with st:
                def sb(name, shape, dt=F32):
                    return st.enter_context(nc.sbuf_tensor(tag + name, shape, dt))

                def ps(name, shape, dt=F32):
                    return st.enter_context(nc.psum_tensor(tag + name, shape, dt))

                def sm(name):
                    return sem(tag + name)

                NC = ncols // 512
                w_raw = sb("w_raw", [P, 2, ncols])
                w_hi = sb("w_hi", [P, KT, ncols], F32R)
                w_lo = sb("w_lo", [P, KT, ncols], F32R)
                x_in = sb("x_in", [P, 2, D])
                x_nrm = sb("x_nrm", [P, D])
                h_full = sb("h_full", [P, KT, P])
                h_hi = sb("h_hi", [P, 2, KT, P], F32R)
                h_lo = sb("h_lo", [P, 2, KT, P], F32R)
                xt_ps = ps("xt_ps", [P, KT, P])
                z_ps = [ps(f"z_ps{i}", [P, 512]) for i in range(4)]
                w_ld = [sm("w_ld0"), sm("w_ld1")]
                w_hid, w_lod = sm("w_hi_done"), sm("w_lo_done")
                x_ld = [sm("x_ld0"), sm("x_ld1")]
                x_nrmd, xt_pe, h_done, hi_done, lo_done = sm("x_nrm_done"), sm("xt_pe"), sm("h_done"), sm("hi_done"), sm("lo_done")
                z_pe, hv = sm("z_pe"), sm("hv")

                def load_w(sp):
                    for k in range(KT):
                        if k >= 2:
                            sp.wait_ge(w_lod, k - 1)
                        sp.dma_start(w_raw[:, k % 2], I["w_in"][0, k * P:(k + 1) * P, col0:col0 + ncols]).then_inc(w_ld[k % 2], 16)

                def load_x(sp, i):
                    if i >= 2:
                        sp.wait_ge(x_nrmd, i - 1)
                    src = I["x_prompt"][0, i * P:(i + 1) * P, :] if i < NT else I["x_sample"].rearrange("b t d -> (b t) d")
                    sp.dma_start(x_in[0:rows_of(i), i % 2], src).then_inc(x_ld[i % 2], 16)

                def split_w_hi(act):
                    for k in range(KT):
                        act.wait_ge(w_ld[k % 2], 16 * (k // 2 + 1))
                        act.activation(w_hi[:, k], w_raw[:, k % 2], ACT.Copy).then_inc(w_hid, 1)

                def split_w_lo(v):
                    for k in range(KT):
                        v.wait_ge(w_hid, k + 1)
                        v.tensor_tensor(w_lo[:, k], w_raw[:, k % 2], w_hi[:, k].bitcast(F32), ALU.subtract).then_inc(w_lod, 1)

                def norm_x(act, i):
                    n = rows_of(i)
                    act.wait_ge(x_ld[i % 2], 16 * (i // 2 + 1))
                    if i >= 1:
                        act.wait_ge(xt_pe, i)
                    act.activation(x_nrm[0:n], x_in[0:n, i % 2], ACT.Copy, scale=rstd1[0:n, i:i + 1]).then_inc(x_nrmd, 1)

                def turn_x(pe, i):
                    n = rows_of(i)
                    pe.wait_ge(x_nrmd, i + 1)
                    if i >= 1:
                        pe.wait_ge(h_done, i)
                    for k in range(KT):
                        mm = pe.transpose(xt_ps[:, k, 0:n], x_nrm[0:n, k * P:(k + 1) * P], ident[0:n, 0:n])
                    mm.then_inc(xt_pe, 1)

                def modulate(act, i):
                    act.wait_ge(xt_pe, i + 1)
                    if i >= 1:
                        act.wait_ge(lo_done, i)
                    for k in range(KT):
                        ins = act.activation(h_full[:, k, :], xt_ps[:, k, :], ACT.Identity,
                                             bias=modT[:, M_SH1 + k, 8:9], scale=gain1[:, k, 8:9])
                    ins.then_inc(h_done, 1)

                def modulate_sample(v, step):
                    v.wait_ge(xt_pe, NT + 1)
                    v.wait_ge(lo_done, NT)
                    for k in range(KT):
                        view = h_full[:, k, 0:NS].rearrange("p (b t) -> p b t", t=DS)
                        step(v.tensor_tensor(view, xt_ps[:, k, 0:NS].rearrange("p (b t) -> p b t", t=DS),
                                             gain1[:, k, 0:DB].unsqueeze(2).to_broadcast([P, DB, DS]), ALU.mult))
                        ins = v.tensor_tensor(view, view, modT[:, M_SH1 + k, 0:DB].unsqueeze(2).to_broadcast([P, DB, DS]), ALU.add)
                    ins.then_inc(h_done, 1)

                def split_hi(act, i):
                    n = rows_of(i)
                    act.wait_ge(h_done, i + 1)
                    if i >= 2:
                        act.wait_ge(z_pe, NC * (i - 1))
                    act.activation(h_hi[:, i % 2, :, 0:n], h_full[:, :, 0:n], ACT.Copy).then_inc(hi_done, 1)

                def split_lo(pool, i):
                    n = rows_of(i)
                    pool.wait_ge(hi_done, i + 1)
                    if i >= 2:
                        pool.wait_ge(z_pe, NC * (i - 1))
                    pool.tensor_tensor(h_lo[:, i % 2, :, 0:n], h_full[:, :, 0:n], h_hi[:, i % 2, :, 0:n].bitcast(F32),
                                       ALU.subtract).then_inc(lo_done, 1)

                def products(pe, i, bank_free):
                    n = rows_of(i)
                    pe.wait_ge(lo_done, i + 1)
                    for c in range(NC):
                        g = NC * i + c
                        if g >= 4:
                            bank_free(g - 4)
                        z = z_ps[g % 4][0:n, :]
                        for k in range(KT):
                            if i == 0 and c == 0:
                                pe.wait_ge(w_lod, k + 1)
                            hi, lo = h_hi[:, i % 2, k, 0:n], h_lo[:, i % 2, k, 0:n]
                            cols = slice(c * 512, (c + 1) * 512)
                            pe.matmul(z, hi, w_hi[:, k, cols], start=k == 0, stop=False)
                            pe.matmul(z, hi, w_lo[:, k, cols], start=False, stop=False)
                            mm = pe.matmul(z, lo, w_hi[:, k, cols], start=False, stop=k == KT - 1)
                        mm.then_inc(z_pe, 1)

                body(dict(sb=sb, ps=ps, sm=sm, z_ps=z_ps, z_pe=z_pe, hv=hv, load_w=load_w, load_x=load_x,
                                     split_w_hi=split_w_hi, split_w_lo=split_w_lo, norm_x=norm_x, turn_x=turn_x,
                                     modulate=modulate, modulate_sample=modulate_sample, split_hi=split_hi,
                                     split_lo=split_lo, products=products))

        conv = ExitStack()
        with conv:
            gluT = conv.enter_context(nc.sbuf_tensor("gluT", [P, CC, HIST + SEQ], F32))
            gluS = conv.enter_context(nc.sbuf_tensor("gluS", [P, CC, DB, HIST + DS], F32))

            PIECE = 4 * P
            dwp = conv.enter_context(nc.sbuf_tensor("dwp", [P, CC, PIECE], F32))
            conv_steps = [(s, j) for s in range(SEQ // PIECE) for j in range(TAPS)]
            IN_STAGE1 = 2 * TAPS

            def conv_tap(v, step, dw_done, dw_out, first_piece, s, j):
                if j == 0 and s > first_piece:
                    v.wait_ge(dw_out, 16 * (s - first_piece))
                for c in range(CC):
                    w = tapT[:, j * CC + c:j * CC + c + 1]
                    x = gluT[:, c, j + s * PIECE:j + (s + 1) * PIECE]
                    if j == 0:
                        ins = v.tensor_scalar(dwp[:, c], x, w, vecT[:, V_CB + c:V_CB + c + 1], ALU.mult, ALU.add)
                    else:
                        step.need(step.last - CC + 1)
                        ins = v.scalar_tensor_tensor(out=dwp[:, c], in0=x, scalar=w, in1=dwp[:, c], op0=ALU.mult, op1=ALU.add)
                    step.last = step.mark(ins)
                if j == TAPS - 1:
                    step.need(step.last)
                    v.sem_inc(dw_done, 1)

            def store_piece(sp, dw_done, dw_out, first_piece, s):
                sp.wait_ge(dw_done, s - first_piece + 1)
                sp.dma_start(dw_d[:, :, s * PIECE:(s + 1) * PIECE], dwp[:]).then_inc(dw_out, 16)

            def values_and_gates(f):
                sm = f["sm"]
                v_sb = f["sb"]("v_sb", [P, 2, AW])
                gate = f["sb"]("gate", [P, 2, CW])
                glu = f["sb"]("glu", [P, 2, CW])
                hist = f["sb"]("hist", [120, 2, CW])
                g_ps = f["ps"]("g_ps", [P, CC, P])
                v_done, gate_done, glu_done = sm("v_done"), sm("gate_done"), sm("glu_done")
                g_pe, g_out, v_out = sm("g_pe"), sm("g_out"), [stored["v_out0"], stored["v_out1"]]
                dw_done, dw_out = sm("dw_done"), sm("dw_out")
                tail_out, hist_in, hist_pe, hist_cp = stored["tail_out"], sm("hist_in"), sm("hist_pe"), sm("hist_cp")
                z_ps, z_pe = f["z_ps"], f["z_pe"]
                with nc.Block() as block:
                    @block.sync
                    def _(sp):
                        f["load_x"](sp, 0)
                        f["load_x"](sp, 1)
                        sp.dma_start(hist[:], I["state_conv"][0].rearrange("(a b) t c -> (b t) a c", a=2)).then_inc(hist_in, 16)
                        f["load_w"](sp)
                        sp.dma_start(O["new_conv_sample"][0, :, 0:HIST - DS, :], I["state_conv"][0, :, DS:HIST, :]).then_inc(tail_out, 16)
                        for i in range(NT + 1):
                            if i + 2 <= NT:
                                f["load_x"](sp, i + 2)
                            sp.wait_ge(v_done, i + 1)
                            if i < NT:
                                sp.dma_start(O["new_v_prompt"][0, 0, i * P:(i + 1) * P].rearrange("t h d -> t (h d)"),
                                             v_sb[:, i % 2]).then_inc(v_out[i % 2], 16)
                            else:
                                for b in range(DB):
                                    sp.dma_start(O["new_v_sample"][0, b, WINC - DS:WINC].rearrange("t h d -> t (h d)"),
                                                 v_sb[DS * b:DS * b + DS, i % 2]).then_inc(v_out[i % 2], 16)
                            if i == 10:
                                store_piece(sp, dw_done, dw_out, 0, 0)
                            if i == NT - 1:
                                sp.wait_ge(glu_done, NT)
                                sp.dma_start(O["new_conv_prompt"][0, 0], glu[P - HIST:P, i % 2]).then_inc(tail_out, 16)
                        sp.wait_ge(glu_done, NT + 1)
                        for b in range(DB):
                            sp.dma_start(O["new_conv_sample"][0, b, HIST - DS:HIST, :],
                                         glu[DS * b:DS * b + DS, NT % 2]).then_inc(tail_out, 16)
                        store_piece(sp, dw_done, dw_out, 0, 1)
                        sp.wait_ge(dw_out, 32)
                        sp.wait_ge(tail_out, 16 * (2 + DB))
                        sp.wait_ge(v_out[0], 16 * (8 + DB))
                        sp.wait_ge(v_out[1], 16 * 8)

                    @block.gpsimd
                    def _(pool):
                        for i in range(NT + 1):
                            f["split_lo"](pool, i)
                            if i in (2, 5, 8):
                                copy_cache(pool, i // 3)

                    @block.scalar
                    def _(act):
                        f["norm_x"](act, 0)
                        f["modulate"](act, 0)
                        f["split_hi"](act, 0)
                        f["norm_x"](act, 1)
                        f["split_w_hi"](act)
                        for i in range(NT + 1):
                            n = rows_of(i)
                            if i + 1 < NT:
                                f["modulate"](act, i + 1)
                            if i + 1 <= NT:
                                f["split_hi"](act, i + 1)
                            if i + 2 <= NT:
                                f["norm_x"](act, i + 2)
                            if i >= 2:
                                act.wait_ge(v_out[i % 2], 16 * (i // 2))
                            act.wait_ge(z_pe, 3 * i + 1)
                            act.activation(v_sb[0:n, i % 2], z_ps[(3 * i) % 4][0:n], ACT.Copy).then_inc(v_done, 1)
                            act.wait_ge(z_pe, 3 * i + 3)
                            if i >= 2:
                                act.wait_ge(glu_done, i - 1)
                            act.activation(gate[0:n, i % 2], z_ps[(3 * i + 2) % 4][0:n], ACT.Sigmoid).then_inc(gate_done, 1)

                    @block.vector
                    def _(v):
                        step = Chain(v, f["hv"])
                        v.memset(gluT[:, :, 0:HIST], 0.0)
                        for a in range(2):
                            v.wait_ge(hist_pe, a + 1)
                            for c in range(CC):
                                ins = v.tensor_copy(gluS[:, c, 4 * a:4 * a + 4, 0:HIST],
                                                    g_ps[:, c, 0:120].rearrange("p (b t) -> p b t", t=HIST))
                            ins.then_inc(hist_cp, 1)
                        f["split_w_lo"](v)
                        for i in range(NT + 1):
                            n = rows_of(i)
                            if i == NT - 1:
                                f["modulate_sample"](v, step)
                            v.wait_ge(gate_done, i + 1)
                            v.wait_ge(v_done, i + 1)
                            if i >= 2:
                                v.wait_ge(g_pe, i - 1)
                            if i == NT:
                                v.wait_ge(g_pe, NT)
                            v.tensor_tensor(glu[0:n, i % 2], z_ps[(3 * i + 1) % 4][0:n], gate[0:n, i % 2], ALU.mult).then_inc(glu_done, 1)
                            if i >= 1:
                                v.wait_ge(g_pe, i)
                                v.tensor_copy(gluT[:, :, HIST + (i - 1) * P:HIST + i * P], g_ps[:]).then_inc(g_out, 1)
                            if i in (4, 8):
                                v.wait_ge(g_out, i)
                            if i >= 4:
                                for s, j in conv_steps[5 * (i - 4):5 * (i - 3) if i < NT else IN_STAGE1]:
                                    conv_tap(v, step, dw_done, dw_out, 0, s, j)
                        v.wait_ge(g_pe, NT + 1)
                        for c in range(CC):
                            ins = v.tensor_copy(gluS[:, c, :, HIST:HIST + DS], g_ps[:, c, 0:NS].rearrange("p (b t) -> p b t", t=DS))
                        ins.then_inc(g_out, 1)

                    @block.tensor
                    def _(pe):
                        def turn_glu(i):
                            n = rows_of(i)
                            pe.wait_ge(glu_done, i + 1)
                            if i >= 1:
                                pe.wait_ge(g_out, i)
                            for c in range(CC):
                                mm = pe.transpose(g_ps[:, c, 0:n], glu[0:n, i % 2, c * P:(c + 1) * P], ident[0:n, 0:n])
                            mm.then_inc(g_pe, 1)

                        f["turn_x"](pe, 0)
                        pe.wait_ge(hist_in, 16)
                        for a in range(2):
                            if a == 1:
                                pe.wait_ge(hist_cp, 1)
                            for c in range(CC):
                                mm = pe.transpose(g_ps[:, c, 0:120], hist[:, a, c * P:(c + 1) * P], ident[0:120, 0:120])
                            mm.then_inc(hist_pe, 1)
                        pe.wait_ge(hist_cp, 2)
                        for i in range(NT + 1):
                            if i < NT:
                                f["turn_x"](pe, i + 1)
                            f["products"](pe, i, lambda g: pe.wait_ge(glu_done, g // 3 + 1))
                            if i >= 1:
                                turn_glu(i - 1)
                        turn_glu(NT)

            projection("vu_", 2 * AW, AW + 2 * CW, values_and_gates)
            end_stage()

            def queries_and_keys(f):
                sm = f["sm"]
                raw = f["sb"]("raw", [P, 2, 2 * AW])
                sqr = f["sb"]("sqr", [P, 2 * AW])
                nrm = f["sb"]("nrm", [P, 2, 2 * AW])
                gains = f["sb"]("gains", [P, 2, DH])
                ssq = f["sb"]("ssq", [P, 2 * H])
                rsq = f["sb"]("rsq", [P, 2, 2 * H])
                tmp = f["sb"]("tmp", [P, 2 * H])
                qkT = f["sb"]("qkT", [P, 2, 2, 4, P])
                t_ps = f["ps"]("t_ps", [P, 2, 4, P])
                dwS = f["sb"]("dwS", [P, CC, NS])
                gain_in, gain_set, raw_done, rs_done = sm("gain_in"), sm("gain_set"), sm("raw_done"), sm("rs_done")
                nrm_half, nrm_done, t_pe, t_done = sm("nrm_half"), sm("nrm_done"), sm("t_pe"), sm("t_done")
                k_out, t_out = [stored["k_out0"], stored["k_out1"]], [sm("t_out0"), sm("t_out1")]
                dw_done, dw_out = sm("dw_done"), sm("dw_out")
                z_ps, z_pe = f["z_ps"], f["z_pe"]
                with nc.Block() as block:
                    @block.sync
                    def _(sp):
                        f["load_x"](sp, 0)
                        f["load_x"](sp, 1)
                        sp.dma_start(gains[:, 0, :], I["q_norm_g"].to_broadcast([P, DH])).then_inc(gain_in, 16)
                        sp.dma_start(gains[:, 1, :], I["k_norm_g"].to_broadcast([P, DH])).then_inc(gain_in, 16)
                        f["load_w"](sp)
                        for i in range(NT + 1):
                            if i + 2 <= NT:
                                f["load_x"](sp, i + 2)
                            if i == 7:
                                store_piece(sp, dw_done, dw_out, 2, 2)
                        store_piece(sp, dw_done, dw_out, 2, 3)
                        sp.wait_ge(dw_done, 3)
                        sp.dma_start(dw_d[:, :, SEQ:TOK], dwS[:]).then_inc(dw_out, 16)
                        sp.wait_ge(dw_out, 16 * 3)
                        sp.wait_ge(k_out[0], 16 * (8 + DB))
                        sp.wait_ge(k_out[1], 16 * 8)
                        sp.wait_ge(t_out[0], 32 * 9)
                        sp.wait_ge(t_out[1], 32 * 8)

                    @block.gpsimd
                    def _(pool):
                        heads = lambda ap: ap.rearrange("p (s h d) -> p s h d", s=2, d=DH)

                        def norm_qk(i):
                            n = rows_of(i)
                            pool.wait_ge(rs_done, i + 1)
                            if i == 0:
                                pool.wait_ge(gain_set, 1)
                            if i >= 2:
                                pool.wait_ge(t_pe, 2 * (i - 1))
                                pool.wait_ge(k_out[i % 2], 16 * (i // 2))
                            out = nrm[0:n, i % 2].rearrange("p (h d) -> p h d", d=DH)
                            pool.tensor_tensor(out, raw[0:n, i % 2].rearrange("p (h d) -> p h d", d=DH),
                                               rsq[0:n, i % 2].unsqueeze(2).to_broadcast([n, 2 * H, DH]), ALU.mult).then_inc(nrm_half, 1)
                            pool.wait_ge(nrm_half, i + 1)
                            pool.tensor_tensor(heads(nrm[0:n, i % 2]), heads(nrm[0:n, i % 2]),
                                               gains[0:n].unsqueeze(2).to_broadcast([n, 2, H, DH]), ALU.mult).then_inc(nrm_done, 1)
                            pool.wait_ge(nrm_done, i + 1)
                            if i < NT:
                                pool.dma_start(O["new_k_prompt"][0, 0, i * P:(i + 1) * P].rearrange("t h d -> t (h d)"),
                                               nrm[:, i % 2, AW:]).then_inc(k_out[i % 2], 16)
                            else:
                                for b in range(DB):
                                    pool.dma_start(O["new_k_sample"][0, b, WINC - DS:WINC].rearrange("t h d -> t (h d)"),
                                                   nrm[DS * b:DS * b + DS, i % 2, AW:]).then_inc(k_out[i % 2], 16)

                        for i in range(NT + 1):
                            f["split_lo"](pool, i)
                            if i in (2, 5, 8):
                                copy_cache(pool, 3 + i // 3)
                            if i >= 1:
                                norm_qk(i - 1)
                        norm_qk(NT)

                    @block.scalar
                    def _(act):
                        def turned(i):
                            n = rows_of(i)
                            if i >= 2:
                                act.wait_ge(t_out[i % 2], 32 * (i // 2))
                            for s in range(2):
                                act.wait_ge(t_pe, 2 * i + s + 1)
                                ins = act.activation(qkT[:, i % 2, s, :, 0:n], t_ps[:, s, :, 0:n], ACT.Copy)
                            ins.then_inc(t_done, 1)
                            act.wait_ge(t_done, i + 1)
                            act.dma_start(qt_d[:, :, i * P:i * P + n], qkT[:, i % 2, 0, :, 0:n]).then_inc(t_out[i % 2], 16)
                            act.dma_start(kt_d[:, :, i * P:i * P + n], qkT[:, i % 2, 1, :, 0:n]).then_inc(t_out[i % 2], 16)

                        f["norm_x"](act, 0)
                        f["modulate"](act, 0)
                        f["split_hi"](act, 0)
                        f["norm_x"](act, 1)
                        f["split_w_hi"](act)
                        for i in range(NT + 1):
                            n = rows_of(i)
                            if i + 1 < NT:
                                f["modulate"](act, i + 1)
                            if i + 1 <= NT:
                                f["split_hi"](act, i + 1)
                            if i + 2 <= NT:
                                f["norm_x"](act, i + 2)
                            if i >= 2:
                                act.wait_ge(nrm_half, i - 1)
                            for s in range(2):
                                act.wait_ge(z_pe, 2 * i + s + 1)
                                act.activation(raw[0:n, i % 2, s * AW:(s + 1) * AW], z_ps[(2 * i + s) % 4][0:n], ACT.Copy)
                                if i >= 1 and s == 0:
                                    act.wait_ge(rs_done, i)
                                ins = act.activation(sqr[0:n, s * AW:(s + 1) * AW], z_ps[(2 * i + s) % 4][0:n], ACT.Square)
                            ins.then_inc(raw_done, 1)
                            if i >= 2:
                                turned(i - 2)
                        turned(NT - 1)
                        turned(NT)

                    @block.vector
                    def _(v):
                        step = Chain(v, f["hv"])
                        f["split_w_lo"](v)
                        v.wait_ge(gain_in, 32)
                        v.tensor_scalar(gains[:, 0, :], gains[:, 0, :], -float(DH) ** -0.5, None, ALU.mult).then_inc(gain_set, 1)

                        def head_norms(i):
                            n = rows_of(i)
                            v.wait_ge(raw_done, i + 1)
                            if i >= 2:
                                v.wait_ge(nrm_half, i - 1)
                            step(v.tensor_reduce(ssq[0:n], sqr[0:n].rearrange("p (h d) -> p h d", d=DH), AX.X, ALU.add))
                            step(v.tensor_scalar(ssq[0:n], ssq[0:n], 1.0 / DH, EPS, ALU.mult, ALU.add))
                            rsqrt(v, step, rsq[0:n, i % 2], ssq[0:n], tmp[0:n])
                            v.sem_inc(rs_done, 1)

                        for i in range(NT):
                            if i == NT - 1:
                                f["modulate_sample"](v, step)
                            for s, j in conv_steps[IN_STAGE1 + 4 * i:IN_STAGE1 + 4 * i + 4]:
                                conv_tap(v, step, dw_done, dw_out, 2, s, j)
                            head_norms(i)
                        for c in range(CC):
                            y = dwS[:, c, :].rearrange("p (b t) -> p b t", t=DS)
                            for j in range(TAPS):
                                x = gluS[:, c, :, j:j + DS]
                                w = tapT[:, j * CC + c:j * CC + c + 1]
                                if j == 0:
                                    step(v.tensor_scalar(y, x, w, vecT[:, V_CB + c:V_CB + c + 1], ALU.mult, ALU.add))
                                else:
                                    step(v.scalar_tensor_tensor(out=y, in0=x, scalar=w, in1=y, op0=ALU.mult, op1=ALU.add))
                        v.sem_inc(dw_done, 1)
                        head_norms(NT)

                    @block.tensor
                    def _(pe):
                        def turn_qk(i):
                            n = rows_of(i)
                            pe.wait_ge(nrm_done, i + 1)
                            if i >= 1:
                                pe.wait_ge(t_done, i)
                            for s in range(2):
                                for c in range(4):
                                    mm = pe.transpose(t_ps[:, s, c, 0:n], nrm[0:n, i % 2, (4 * s + c) * P:(4 * s + c + 1) * P], ident[0:n, 0:n])
                                mm.then_inc(t_pe, 1)

                        f["turn_x"](pe, 0)
                        for i in range(NT + 1):
                            if i < NT:
                                f["turn_x"](pe, i + 1)
                            f["products"](pe, i, lambda g: pe.wait_ge(raw_done, g // 2 + 1))
                            if i >= 2:
                                turn_qk(i - 2)
                        turn_qk(NT - 1)
                        turn_qk(NT)

            projection("qk_", 0, 2 * AW, queries_and_keys)
            end_stage()

        with ExitStack() as st:
            def sb(name, shape, dt=F32):
                return st.enter_context(nc.sbuf_tensor("pa_" + name, shape, dt))

            def ps(name, shape, dt=F32):
                return st.enter_context(nc.psum_tensor("pa_" + name, shape, dt))

            def sm(name):
                return sem("pa_" + name)

            PAIRS = H // 2
            bias = sb("bias", [P, H, 3, 2 * NB])
            qT = sb("qT", [P, 2, SEQ])
            kT = sb("kT", [P, 2, SEQ])
            vp = sb("vp", [P, 2, 3, NT, P])
            score = sb("score", [P, 4, 2, 2 * NB])
            prob = sb("prob", [P, 4, 2, 2 * NB])
            probT = sb("probT", [P, 3, 2, 2 * NB])
            o_sb = sb("o_sb", [P, 2, NT, P])
            stat = sb("stat", [P, 3, NT, 2, H])
            s_bank = [[ps(f"s_ps{hh}{i}", [P, 512]) for i in range(2)] for hh in range(2)]
            t_ps = [ps(f"t_ps{i}", [P, 2, 2 * NB]) for i in range(2)]
            o_ps = [ps(f"o_ps{i}", [P, 2, P]) for i in range(2)]
            bias_in, pair_in = sm("bias_in"), [sm("pair_in0"), sm("pair_in1")]
            s_pe, s_done, e_done, t_pe, tv_done, ta_done, o_pe, o_done = (
                sm(x) for x in ("s_pe", "s_done", "e_done", "t_pe", "tv_done", "ta_done", "o_pe", "o_done"))
            o_out, st_out = [sm("o_out0"), sm("o_out1")], sm("st_out")
            units = [(hp, p, t) for hp in range(PAIRS) for p in range(3) for t in range(NT)]
            N = len(units)

            def s_ps(u, hh):
                return s_bank[hh][u % 2]

            def by_act(u):
                return u % 4 == 3

            def turned(eng, u):
                if by_act(u):
                    eng.wait_ge(ta_done, u // 4 + 1)
                else:
                    eng.wait_ge(tv_done, u + 1 - u // 4)

            def blocks(p):
                d = PATTERNS[p][1]
                return d, NT // d

            def tokens(p, t, prev):
                d, nb = blocks(p)
                r, n = divmod(t, nb)
                first, count = (n - prev) * NB * d + r, (1 + prev) * NB
                return slice(first, first + (count - 1) * d + 1, d)

            def has_prev(p, t):
                return int(t % blocks(p)[1] > 0)

            def by_block(dram_rows, p, src):
                d, nb = blocks(p)
                view = dram_rows.rearrange("(n i r) c -> r i n c", i=NB, r=d)
                for r in range(d) if nb > 1 else [None]:
                    if r is None:
                        yield dram_rows.rearrange("(i r) c -> i r c", r=d), src
                    else:
                        yield view[r], src[:, r * nb:(r + 1) * nb, :]

            out_n = {q: (1, 4, 1)[q % 3] for q in range(3 * PAIRS)}

            def out_count(q):
                return 16 * sum(out_n[x] for x in range(q % 2, q + 1, 2))

            with nc.Block() as block:
                @block.sync
                def _(sp):
                    def load_pair(hp):
                        if hp >= 2:
                            sp.wait_ge(o_pe, (hp - 1) * 3 * NT)
                        b = hp % 2
                        sp.dma_start(qT[:, b], qt_d[:, hp, 0:SEQ]).then_inc(pair_in[b], 16)
                        sp.dma_start(kT[:, b], kt_d[:, hp, 0:SEQ]).then_inc(pair_in[b], 16)
                        rows = O["new_v_prompt"][0, 0].rearrange("t h d -> t (h d)")[:, hp * P:(hp + 1) * P]
                        for p in range(3):
                            for src, dst in by_block(rows, p, vp[:, b, p]):
                                sp.dma_start(dst, src).then_inc(pair_in[b], 16)

                    load_pair(0)
                    for h in range(H):
                        skew = bass.AP(bias_d.tensor, h * P * 3 * RW + NB - 1, [[3 * RW - 1, P], [RW, 3], [1, 2 * NB]])
                        sp.dma_start(bias[:, h], skew).then_inc(bias_in, 16)
                    load_pair(1)
                    for q in range(3 * PAIRS):
                        hp, p = divmod(q, 3)
                        if p == 0 and 1 <= hp < PAIRS - 1:
                            load_pair(hp + 1)
                        sp.wait_ge(o_done, (q + 1) * NT)
                        for dst, src in by_block(acc_d[p][:, hp * P:(hp + 1) * P], p, o_sb[:, q % 2]):
                            sp.dma_start(dst, src).then_inc(o_out[q % 2], 16)
                    sp.wait_ge(s_done, 2 * N)
                    sp.wait_ge(e_done, 2 * N)
                    for p in range(3):
                        for dst, src in by_block(st_d[p], p, stat[:, p].rearrange("i t s h -> i t (s h)")):
                            sp.dma_start(dst, src).then_inc(st_out, 16)
                    sp.wait_ge(st_out, 16 * 6)
                    sp.wait_ge(o_out[0], out_count(3 * PAIRS - 2))
                    sp.wait_ge(o_out[1], out_count(3 * PAIRS - 1))

                @block.gpsimd
                def _(pool):
                    for n in range(6, 11):
                        pool.wait_ge(o_pe, 30 * (n - 6) + 10)
                        copy_cache(pool, n)

                @block.tensor
                def _(pe):
                    def scores(u):
                        hp, p, t = units[u]
                        b, prev = hp % 2, has_prev(p, t)
                        if u % (3 * NT) == 0:
                            pe.wait_ge(pair_in[b], 16 * 8 * (hp // 2 + 1))
                        for hh in range(2):
                            if u >= 2:
                                pe.wait_ge(s_done, 2 * (u - 2) + hh + 1)
                            part = slice(hh * DH, hh * DH + DH)
                            pe.matmul(s_ps(u, hh)[:, 0:(1 + prev) * NB], qT[part, b, tokens(p, t, 0)], kT[part, b, tokens(p, t, prev)],
                                      start=True, stop=True).then_inc(s_pe, 1)

                    def turn(u):
                        prev = has_prev(*units[u][1:3])
                        pe.wait_ge(e_done, 2 * u + 2)
                        if u >= 2:
                            turned(pe, u - 2)
                        for hh in range(2):
                            for j in range(1 + prev):
                                mm = pe.transpose(t_ps[u % 2][:, hh, j * NB:(j + 1) * NB], prob[:, u % 4, hh, j * NB:(j + 1) * NB], ident[:])
                        mm.then_inc(t_pe, 1)

                    def weigh(u):
                        hp, p, t = units[u]
                        prev = has_prev(p, t)
                        turned(pe, u)
                        if u >= 2:
                            pe.wait_ge(o_done, u - 1)
                        for hh in range(2):
                            for j in range(1 + prev):
                                mm = pe.matmul(o_ps[u % 2][:, hh], probT[:, u % 3, hh, j * NB:(j + 1) * NB],
                                               vp[:, hp % 2, p, t - prev + j, :], start=j == 0, stop=j == prev)
                        mm.then_inc(o_pe, 1)

                    for u in range(N + 5):
                        if u < N:
                            scores(u)
                        if 3 <= u < N + 3:
                            turn(u - 3)
                        if u >= 5:
                            weigh(u - 5)

                def copy_turned(eng, u, copy, done):
                    cols = slice(0, (1 + has_prev(*units[u][1:3])) * NB)
                    eng.wait_ge(t_pe, u + 1)
                    if u >= 3:
                        eng.wait_ge(o_pe, u - 2)
                    copy(probT[:, u % 3, :, cols], t_ps[u % 2][:, :, cols]).then_inc(done, 1)

                @block.vector
                def _(v):
                    v.wait_ge(bias_in, 16 * H)
                    for u in range(N + 5):
                        if u < N:
                            hp, p, t = units[u]
                            prev = has_prev(p, t)
                            cols = slice(0, (1 + prev) * NB)
                            for hh in range(2):
                                h = 2 * hp + hh
                                v.wait_ge(s_pe, 2 * u + hh + 1)
                                if u >= 4:
                                    v.wait_ge(e_done, 2 * (u - 4) + hh + 1)
                                v.tensor_tensor_reduce(score[:, u % 4, hh, cols], s_ps(u, hh)[:, cols], bias[:, h, p, (1 - prev) * NB:2 * NB],
                                                       1.0, -NEG, ALU.add, ALU.min, stat[:, p, t, 0, h:h + 1]).then_inc(s_done, 1)
                        if 3 <= u < N + 3 and not by_act(u - 3):
                            copy_turned(v, u - 3, v.tensor_copy, tv_done)
                        if u >= 5:
                            w = u - 5
                            q = w // NT
                            v.wait_ge(o_pe, w + 1)
                            if w % NT == 0 and q >= 2:
                                v.wait_ge(o_out[q % 2], out_count(q - 2))
                            own = o_ps[w % 2][:].rearrange("p a c -> p (a c)")
                            own = own.rearrange("p (x d) -> p x d", d=DH)[:, 0:4:3, :]
                            v.tensor_copy(o_sb[:, q % 2, w % NT].rearrange("p (a d) -> p a d", d=DH), own).then_inc(o_done, 1)

                @block.scalar
                def _(act):
                    for u in range(N + 3):
                        if u < N:
                            hp, p, t = units[u]
                            cols = slice(0, (1 + has_prev(p, t)) * NB)
                            for hh in range(2):
                                h = 2 * hp + hh
                                act.wait_ge(s_done, 2 * u + hh + 1)
                                if u >= 4 and hh == 0:
                                    act.wait_ge(t_pe, u - 3)
                                act.activation(prob[:, u % 4, hh, cols], score[:, u % 4, hh, cols], ACT.Exp, bias=stat[:, p, t, 0, h:h + 1],
                                               scale=-1.0, accum_out=stat[:, p, t, 1, h:h + 1]).then_inc(e_done, 1)
                        if u >= 3 and by_act(u - 3):
                            copy_turned(act, u - 3, lambda out, src: act.activation(out, src, ACT.Copy), ta_done)

        end_stage()

        with ExitStack() as st:
            def sb(name, shape, dt=F32):
                return st.enter_context(nc.sbuf_tensor("sa_" + name, shape, dt))

            def ps(name, shape, dt=F32):
                return st.enter_context(nc.psum_tensor("sa_" + name, shape, dt))

            def sm(name):
                return sem("sa_" + name)

            G = 4
            qs = sb("qs", [P, 4, NS])
            ks = sb("ks", [P, 4, NS])
            qblk = sb("qblk", [P, DB, 4, NS])
            kn = sb("kn", [P, 2, 2, 4, AW])
            kTt = sb("kTt", [P, 2, 4, 4, P])
            vn = sb("vn", [P, G, 2, 4, AW])
            vnew = sb("vnew", [DS, DB, AW])
            sbias = sb("sbias", [P, 3, SKEYS])
            score = sb("score", [P, SKEYS])
            prob = sb("prob", [P, 3, SKEYS])
            mins = sb("mins", [P, 8])
            mask = sb("mask", [P, H])
            probT = sb("probT", [P, 8, P])
            probN = sb("probN", [DS, P])
            o_m = sb("o_m", [P, AW])
            o_r = sb("o_r", [P, 2, DH])
            k_ps = [ps(f"k_ps{i}", [P, 4, P]) for i in range(2)]
            s_ps = ps("s_ps", [P, 3, 512])
            p_ps = [ps(f"p_ps{i}", [P, 512]) for i in range(2)]
            o_ps = ps("o_ps", [P, 512])
            small_in, blk_zero, blk_done = sm("small_in"), sm("blk_zero"), sm("blk_done")
            k_in, v_in = [sm("k_in0"), sm("k_in1")], sm("v_in")
            k_pe, k_cp, s_pe, soft, p_pe, p_cp, o_pe, o_done, o_out, sv = (sm(x) for x in ("k_pe", "k_cp", "s_pe", "soft", "p_pe", "p_cp", "o_pe", "o_done", "o_out", "sv"))
            s_read, s_min, s_exp = sm("s_read"), sm("s_min"), sm("s_exp")
            units = [(b, a) for b in range(DB) for a in range(2)]

            def rows(cache, b, a):
                r = cache[0, b].rearrange("r h d -> r (h d)")
                if a == 0:
                    return r[WINC - 512:WINC].rearrange("(p j) c -> p j c", j=4)
                return r.rearrange("(p j) c -> p j c", j=16)[:, 0:DS, :]

            with nc.Block() as block:
                @block.sync
                def _(sp):
                    sp.dma_start(qs[:], qt_d[:, :, SEQ:TOK]).then_inc(small_in, 16)
                    sp.dma_start(ks[:], kt_d[:, :, SEQ:TOK]).then_inc(small_in, 16)
                    sp.dma_start(mask[:], I["mask_h"]).then_inc(small_in, 16)

                    def load_k(n):
                        b, a = units[n]
                        if n >= 4:
                            sp.wait_ge(k_pe, 4 * (n - 3))
                        sp.dma_start(kn[:, (n // 2) % 2, a], rows(I["cache_k"], b, a)).then_inc(k_in[(n // 2) % 2], 16)

                    for n in range(4):
                        load_k(n)
                    sp.dma_start(vnew[:], O["new_v_sample"][0, :, WINC - DS:WINC].rearrange("b t h d -> t b (h d)")).then_inc(small_in, 16)
                    sp.dma_start(sbias[:].rearrange("p a c -> p (a c)"), sbias_d).then_inc(small_in, 16)
                    for g in range(DB // G):
                        for b in range(G * g, G * g + G):
                            if b % G == 0 and g >= 1:
                                sp.wait_ge(o_pe, g)
                            for a in range(2):
                                sp.dma_start(vn[:, b % G, a], rows(I["cache_v"], b, a)).then_inc(v_in, 16)
                            for n in (2 * b + 4, 2 * b + 5):
                                if n < 2 * DB:
                                    load_k(n)
                    for g in range(DB // G):
                        sp.wait_ge(o_done, g + 1)
                        for j in range(G):
                            b = G * g + j
                            sp.dma_start(os_d[DS * b:DS * b + DS].rearrange("t (h d) -> h t d", d=DH),
                                         o_r[32 * j:32 * j + 32, g % 2]).then_inc(o_out, 16)
                    sp.wait_ge(o_out, 16 * DB)

                @block.gpsimd
                def _(pool):
                    pool.memset(qblk[:], 0.0).then_inc(blk_zero, 1)
                    pool.wait_ge(blk_zero, 1)
                    pool.wait_ge(small_in, 16 * 5)
                    for c in range(4):
                        for hh in range(2):
                            part = slice(hh * DH, hh * DH + DH)
                            col = DS * (2 * c + hh)
                            ins = pool.tensor_copy(qblk[part, :, c, col:col + DS], qs[part, c, :].rearrange("p (b t) -> p b t", t=DS))
                    ins.then_inc(blk_done, 1)

                @block.tensor
                def _(pe):
                    def turn(n, c):
                        b, a = units[n]
                        if c == 0:
                            pe.wait_ge(k_in[(n // 2) % 2], 16 * (2 * (n // 4) + 2))
                        g = 4 * n + c
                        if g >= 2:
                            pe.wait_ge(k_cp, g - 1)
                        for j in range(4):
                            mm = pe.transpose(k_ps[g % 2][:, j, :], kn[:, (n // 2) % 2, a, j, c * P:(c + 1) * P], ident[:])
                        mm.then_inc(k_pe, 1)

                    def scores(n):
                        b, a = units[n]
                        part = slice(32 * (b % G), 32 * (b % G) + 32)
                        pe.wait_ge(k_cp, 4 * n + 4)
                        if n == 0:
                            pe.wait_ge(blk_done, 1)
                        if b % G == 0 and a == 0 and b >= G:
                            pe.wait_ge(s_read, b // G)
                        for c in range(4):
                            mm = pe.matmul(s_ps[part, a, :], qblk[:, b, c, :], kTt[:, n % 2, c].rearrange("p j k -> p (j k)"), start=c == 0, stop=c == 3)
                        if a == 1:
                            for c in range(4):
                                mm = pe.matmul(s_ps[part, 2, 0:DS], qblk[:, b, c, :], ks[:, c, DS * b:DS * b + DS], start=c == 0, stop=c == 3)
                        mm.then_inc(s_pe, 1)

                    def values(g):
                        pe.wait_ge(soft, g + 1)
                        for j in range(3):
                            u = 3 * g + j
                            if u >= 2:
                                pe.wait_ge(p_cp, u - 1)
                            if j < 2:
                                for m in range(4):
                                    mm = pe.transpose(p_ps[u % 2][:, m * P:(m + 1) * P], prob[:, 0, (4 * j + m) * P:(4 * j + m + 1) * P], ident[:])
                            else:
                                mm = pe.transpose(p_ps[u % 2][0:DS, 0:P], prob[:, 0, 8 * P:8 * P + DS], ident[:])
                            mm.then_inc(p_pe, 1)
                        pe.wait_ge(p_cp, 3 * g + 3)
                        pe.wait_ge(v_in, 16 * 2 * G * (g + 1))
                        if g >= 1:
                            pe.wait_ge(o_done, g)
                        for j in range(G):
                            part = slice(32 * j, 32 * j + 32)
                            for m in range(8):
                                pe.matmul(o_ps[part, :], probT[:, m, part], vn[:, j, m // 4, m % 4, :], start=m == 0, stop=False)
                            mm = pe.matmul(o_ps[part, :], probN[:, part], vnew[:, G * g + j, :], start=False, stop=True)
                        mm.then_inc(o_pe, 1)

                    for n in range(2 * DB):
                        for c in range(4):
                            turn(n, c)
                        if n >= 1:
                            scores(n - 1)
                        if n == 2 * G + 2:
                            values(0)
                    scores(2 * DB - 1)
                    values(1)

                @block.vector
                def _(v):
                    step = Chain(v, sv)

                    def k_copy(g):
                        n, c = divmod(g, 4)
                        v.wait_ge(k_pe, g + 1)
                        if n >= 2:
                            v.wait_ge(s_pe, n - 1)
                        v.tensor_copy(kTt[:, n % 2, c], k_ps[g % 2][:]).then_inc(k_cp, 1)

                    def soften(g):
                        v.wait_ge(s_pe, 2 * G * (g + 1))
                        if g == 0:
                            v.wait_ge(small_in, 16 * 5)
                        v.tensor_copy(score[:, 0:8 * P], s_ps[:, 0:2, :].rearrange("p a k -> p (a k)"))
                        step(v.tensor_copy(score[:, 8 * P:SKEYS], s_ps[:, 2, 0:DS]))
                        v.sem_inc(s_read, 1)
                        if g >= 1:
                            v.wait_ge(o_pe, g)
                        for p in range(3):
                            ins = v.tensor_tensor_reduce(prob[:, p], score[:], sbias[:, p], 1.0, -NEG, ALU.add, ALU.min, mins[:, p:p + 1])
                        step(ins)
                        step(v.tensor_reduce(mins[:, 3:4], mins[:, 0:3], AX.X, ALU.min))
                        v.sem_inc(s_min, 1)
                        v.wait_ge(s_exp, g + 1)
                        step(v.tensor_reduce(mins[:, 7:8], mins[:, 4:7], AX.X, ALU.add))
                        step(v.reciprocal(mins[:, 7:8], mins[:, 7:8]))
                        step(v.tensor_tensor(prob[:, 0], prob[:, 0], prob[:, 1], ALU.add))
                        step(v.tensor_tensor(prob[:, 0], prob[:, 0], prob[:, 2], ALU.add))
                        v.tensor_scalar(prob[:, 0], prob[:, 0], mins[:, 7:8], None, ALU.mult).then_inc(soft, 1)

                    def p_copy(g):
                        for j in range(3):
                            u = 3 * g + j
                            v.wait_ge(p_pe, u + 1)
                            if j == 0 and g >= 1:
                                v.wait_ge(o_pe, g)
                            if j < 2:
                                v.tensor_copy(probT[:, 4 * j:4 * j + 4].rearrange("p m k -> p (m k)"), p_ps[u % 2][:]).then_inc(p_cp, 1)
                            else:
                                v.tensor_copy(probN[:], p_ps[u % 2][0:DS, 0:P]).then_inc(p_cp, 1)

                    def gather(g):
                        v.wait_ge(o_pe, g + 1)
                        step(v.tensor_tensor(o_m[:].rearrange("p (h d) -> p h d", d=DH), o_ps[:].rearrange("p (h d) -> p h d", d=DH),
                                             mask[:].unsqueeze(2).to_broadcast([P, H, DH]), ALU.mult))
                        v.tensor_reduce(o_r[:, g % 2], o_m[:].rearrange("p (h d) -> p d h", d=DH), AX.X, ALU.add).then_inc(o_done, 1)

                    for n in range(2 * DB):
                        for c in range(4):
                            k_copy(4 * n + c)
                        if n == 2 * G:
                            soften(0)
                        if n == 2 * G + 2:
                            p_copy(0)
                            gather(0)
                    soften(1)
                    p_copy(1)
                    gather(1)

                @block.scalar
                def _(act):
                    for g in range(DB // G):
                        act.wait_ge(s_min, g + 1)
                        for p in range(3):
                            ins = act.activation(prob[:, p], prob[:, p], ACT.Exp, bias=mins[:, 3:4], scale=-1.0, accum_out=mins[:, 4 + p:5 + p])
                        ins.then_inc(s_exp, 1)
        end_stage()

        with ExitStack() as st:
            def sb(name, shape, dt=F32):
                return st.enter_context(nc.sbuf_tensor("mx_" + name, shape, dt))

            def ps(name, shape, dt=F32):
                return st.enter_context(nc.psum_tensor("mx_" + name, shape, dt))

            def sm(name):
                return sem("mx_" + name)

            wo_hi = sb("wo_hi", [P, KT, D], F32R)
            wo_lo = sb("wo_lo", [P, KT, D], F32R)
            wp_hi = sb("wp_hi", [P, CC, CW], F32R)
            wp_lo = sb("wp_lo", [P, CC, CW], F32R)
            w_raw = sb("w_raw", [P, 2, D])
            gate_p = sb("gate_p", [P, D])
            gate_s = sb("gate_s", [NS, D])
            stat = sb("stat", [P, NT, 3, 2, H])
            least = sb("least", [P, NT, H])
            fac = sb("fac", [P, NT, 3, H])
            total = sb("total", [P, NT, H])
            acc = sb("acc", [P, 2, 3, AW])
            o_n = sb("o_n", [P, AW])
            dwt = sb("dwt", [P, 2, CC, P])
            x_in = sb("x_in", [P, 2, D])
            bn = sb("bn", [P, 6])
            mv = sb("mv", [P, 2])
            ln = sb("ln", [P, 4])
            y_n = sb("y_n", [P, CW])
            y_a = sb("y_a", [P, CC, P])
            y_g = sb("y_g", [P, CC, P])
            y_hi = sb("y_hi", [P, CC, P], F32R)
            y_lo = sb("y_lo", [P, CC, P], F32R)
            m_hi = sb("m_hi", [P, 2, KT, P], F32R)
            m_lo = sb("m_lo", [P, 2, KT, P], F32R)
            upd = sb("upd", [P, D])
            x1 = sb("x1", [P, 2, D])
            x1_sq = sb("x1_sq", [P, D])
            rs2 = sb("rs2", [P, 4])
            x1n = sb("x1n", [P, D])
            h2 = sb("h2", [P, 2, KT, P])
            dw_ps = ps("dw_ps", [P, CW])
            y_ps = ps("y_ps", [P, CC, P])
            c_ps = ps("c_ps", [P, CC, P])
            a_ps = ps("a_ps", [P, 4, P])
            z_ps = [ps(f"z_ps{i}", [P, 512]) for i in range(2)]
            h_ps = ps("h_ps", [P, KT, P])
            sems = ("fac_x w_hid w_lod gate_in stat_in fac_e fac_d dw_pe yn_d y_pe ya_d yg_d yf_d yhi_d ylo_d c_pe a_pe o_half o_d mhi_d mlo_d "
                    "z_pe upd_d x1_d_ sq_d rs2_d x1n_d h_pe h2_d_ mv_ x1q").split()
            S = {x: sm(x) for x in sems}
            w_ld, acc_in, dw_in, x_in_s = ([sm(f"{x}{i}") for i in range(2)] for x in ("w_ld", "acc_in", "dw_in", "x_in"))
            x1_out, h2_out = ([sm(f"{x}{i}") for i in range(2)] for x in ("x1_out", "h2_out"))
            WN = KT + 2

            def w_piece(n):
                if n < KT:
                    return I["w_o"][0, n * P:(n + 1) * P, :], w_raw[:, n % 2], wo_hi[:, n], wo_lo[:, n]
                m = 2 * (n - KT)
                flat = lambda ap: ap.rearrange("p k c -> p (k c)")
                return (I["w_pw2"][0, m * P:(m + 2) * P, :].rearrange("(k p) c -> p k c", p=P), w_raw[:, n % 2].rearrange("p (k c) -> p k c", k=2),
                        wp_hi[:, m:m + 2], wp_lo[:, m:m + 2])

            def like(n, ap):
                return ap if n < KT else ap.rearrange("p (k c) -> p k c", k=2)

            with nc.Block() as block:
                @block.sync
                def _(sp):
                    def load_conv(i):
                        n = rows_of(i)
                        if i >= 2:
                            sp.wait_ge(S["dw_pe"], i - 1)
                        sp.dma_start(dwt[:, i % 2, :, 0:n], dw_d[:, :, i * P:i * P + n]).then_inc(dw_in[i % 2], 16)

                    def load_rest(i):
                        n = rows_of(i)
                        t = slice(i * P, i * P + n)
                        if i >= 2:
                            sp.wait_ge(S["o_d"], i - 1)
                        if i < NT:
                            sp.dma_start(acc[:, i % 2], acc_d[:, t].rearrange("a t c -> t a c")).then_inc(acc_in[i % 2], 16)
                        else:
                            sp.dma_start(acc[0:n, i % 2, 0], os_d).then_inc(acc_in[i % 2], 16)
                        if i >= 2:
                            sp.wait_ge(S["x1_d_"], i - 1)
                        src = I["x_prompt"][0, t, :] if i < NT else I["x_sample"].rearrange("b t d -> (b t) d")
                        sp.dma_start(x_in[0:n, i % 2], src).then_inc(x_in_s[i % 2], 16)

                    load_conv(0)
                    for n in range(WN):
                        if n >= 2:
                            sp.wait_ge(S["w_lod"], n - 1)
                        src = w_piece((n + KT) % WN)[0]
                        sp.dma_start(like((n + KT) % WN, w_raw[:, n % 2]), src).then_inc(w_ld[n % 2], 16)
                        if n == 1:
                            for a in range(3):
                                sp.dma_start(stat[:, :, a].rearrange("p i s h -> p i (s h)"),
                                             st_d[a].rearrange("(i p) c -> p i c", p=P)).then_inc(S["stat_in"], 16)
                            load_conv(1)
                            load_rest(0)
                        if n == 2:
                            load_rest(1)
                            sp.dma_start(gate_p[:], mod_d[8:9, 2 * D:3 * D].to_broadcast([P, D])).then_inc(S["gate_in"], 16)
                            sp.dma_start(gate_s[:], bass.AP(mod_d.tensor, 2 * D, [[NMOD, DB], [0, DS], [1, D]])).then_inc(S["gate_in"], 16)
                    for i in range(2, NT + 1):
                        load_conv(i)
                        load_rest(i)
                    sp.wait_ge(S["h2_d_"], NT + 1)
                    sp.dma_start(h2_d[:, :, SEQ:TOK], h2[:, NT % 2, :, 0:NS]).then_inc(h2_out[NT % 2], 16)
                    for s in (x1_out, h2_out):
                        sp.wait_ge(s[0], 16 * 9)
                        sp.wait_ge(s[1], 16 * 8)

                @block.gpsimd
                def _(pool):
                    def merge(i):
                        n = rows_of(i)
                        if i < NT:
                            if i == 0:
                                pool.wait_ge(S["fac_d"], 1)
                            pool.wait_ge(acc_in[i % 2], 16 * (i // 2 + 1))
                            view = acc[:, i % 2].rearrange("p a (h d) -> p (a h) d", d=DH)
                            pool.tensor_tensor(view, view, fac[:, i].rearrange("p a h -> p (a h)").unsqueeze(2).to_broadcast([P, 3 * H, DH]),
                                               ALU.mult).then_inc(S["o_half"], 1)
                            pool.wait_ge(S["o_half"], 2 * i + 1)
                            pool.tensor_tensor(acc[:, i % 2, 0], acc[:, i % 2, 0], acc[:, i % 2, 1], ALU.add).then_inc(S["o_half"], 1)
                            pool.wait_ge(S["o_half"], 2 * i + 2)
                            if i >= 1:
                                pool.wait_ge(S["a_pe"], i)
                            pool.tensor_tensor(o_n[:], acc[:, i % 2, 0], acc[:, i % 2, 2], ALU.add).then_inc(S["o_d"], 1)
                        else:
                            pool.wait_ge(acc_in[i % 2], 16 * (i // 2 + 1))
                            pool.wait_ge(S["a_pe"], i)
                            pool.tensor_copy(o_n[0:n], acc[0:n, i % 2, 0]).then_inc(S["o_d"], 1)

                    def residual(i):
                        n = rows_of(i)
                        pool.wait_ge(S["upd_d"], i + 1)
                        pool.wait_ge(x_in_s[i % 2], 16 * (i // 2 + 1))
                        if i >= 2:
                            pool.wait_ge(x1_out[i % 2], 16 * (i // 2))
                            pool.wait_ge(S["x1n_d"], i - 1)
                        pool.tensor_tensor(x1[0:n, i % 2], upd[0:n], x_in[0:n, i % 2], ALU.add).then_inc(S["x1_d_"], 1)
                        pool.wait_ge(S["x1_d_"], i + 1)
                        pool.dma_start(x1_d[i * P:i * P + n], x1[0:n, i % 2]).then_inc(x1_out[i % 2], 16)

                    merge(0)
                    merge(1)
                    for i in range(NT + 1):
                        residual(i)
                        if i + 2 <= NT:
                            merge(i + 2)

                @block.scalar
                def _(act):
                    def swish(i):
                        n = rows_of(i)
                        act.wait_ge(S["y_pe"], i + 1)
                        if i >= 1:
                            act.wait_ge(S["ylo_d"], i)
                        for c in range(CC):
                            g, b = vecT[:, V_LG + c:V_LG + c + 1], vecT[:, V_LB + c:V_LB + c + 1]
                            act.activation(y_a[:, c, 0:n], y_ps[:, c, 0:n], ACT.Identity, bias=b, scale=g)
                            ins = act.activation(y_g[:, c, 0:n], y_ps[:, c, 0:n], ACT.Sigmoid, bias=b, scale=g)
                        ins.then_inc(S["yg_d"], 1)
                        act.wait_ge(S["yf_d"], i + 1)
                        if i >= 1:
                            act.wait_ge(S["c_pe"], i)
                        act.activation(y_hi[:, :, 0:n], y_a[:, :, 0:n], ACT.Copy).then_inc(S["yhi_d"], 1)

                    def split_mix(i, part):
                        n = rows_of(i)
                        if part == 0:
                            act.wait_ge(S["a_pe"], i + 1)
                            if i >= 2:
                                act.wait_ge(S["z_pe"], 2 * (i - 1))
                            act.activation(m_hi[:, i % 2, 0:4, 0:n], a_ps[:, :, 0:n], ACT.Copy).then_inc(S["mhi_d"], 1)
                        else:
                            act.wait_ge(S["c_pe"], i + 1)
                            act.activation(m_hi[:, i % 2, 4:8, 0:n], c_ps[:, :, 0:n], ACT.Copy).then_inc(S["mhi_d"], 1)

                    def square(i):
                        n = rows_of(i)
                        act.wait_ge(S["x1_d_"], i + 1)
                        if i >= 1:
                            act.wait_ge(S["rs2_d"], i)
                            act.wait_ge(S["x1q"], i)
                        act.activation(x1_sq[0:n], x1[0:n, i % 2], ACT.Square, accum_out=rs2[0:n, 1:2]).then_inc(S["x1q"], 1)

                    def modulate(i):
                        act.wait_ge(S["h_pe"], i + 1)
                        if i >= 2:
                            act.wait_ge(h2_out[i % 2], 16 * (i // 2))
                        for k in range(KT):
                            ins = act.activation(h2[:, i % 2, k], h_ps[:, k], ACT.Identity, bias=modT[:, M_SH2 + k, 8:9], scale=gain2[:, k, 8:9])
                        ins.then_inc(S["h2_d_"], 1)
                        act.wait_ge(S["h2_d_"], i + 1)
                        act.dma_start(h2_d[:, :, i * P:(i + 1) * P], h2[:, i % 2]).then_inc(h2_out[i % 2], 16)

                    for n in range(WN):
                        if n == 2:
                            swish(0)
                            act.wait_ge(S["fac_e"], 1)
                            act.activation(fac[:], fac[:], ACT.Exp).then_inc(S["fac_x"], 1)
                        m = (n + KT) % WN
                        act.wait_ge(w_ld[n % 2], 16 * (n // 2 + 1))
                        act.activation(w_piece(m)[2], like(m, w_raw[:, n % 2]), ACT.Copy).then_inc(S["w_hid"], 1)
                    split_mix(0, 0)
                    split_mix(0, 1)
                    for i in range(NT + 1):
                        if i < NT:
                            swish(i + 1)
                            split_mix(i + 1, 0)
                        if 1 <= i:
                            modulate(i - 1)
                        if i < NT:
                            split_mix(i + 1, 1)
                        square(i)

                @block.vector
                def _(v):
                    step = Chain(v, S["mv_"])

                    def split_w(n):
                        m = (n + KT) % WN
                        v.wait_ge(S["w_hid"], n + 1)
                        v.tensor_tensor(w_piece(m)[3], like(m, w_raw[:, n % 2]), w_piece(m)[2].bitcast(F32), ALU.subtract).then_inc(S["w_lod"], 1)

                    def layer_norm(i):
                        n = rows_of(i)
                        v.wait_ge(S["dw_pe"], i + 1)
                        step(v.bn_stats(bn[0:n], dw_ps[0:n]))
                        step(v.bn_aggr(mv[0:n], bn[0:n]))
                        step(v.tensor_scalar(ln[0:n, 0:1], mv[0:n, 1:2], EPS, None, ALU.add))
                        rsqrt(v, step, ln[0:n, 1:2], ln[0:n, 0:1], ln[0:n, 2:3])
                        if i >= 1:
                            v.wait_ge(S["y_pe"], i)
                        v.tensor_scalar(y_n[0:n], dw_ps[0:n], mv[0:n, 0:1], ln[0:n, 1:2], ALU.subtract, ALU.mult).then_inc(S["yn_d"], 1)

                    def gate_y(i):
                        n = rows_of(i)
                        v.wait_ge(S["yg_d"], i + 1)
                        v.tensor_tensor(y_a[:, :, 0:n], y_a[:, :, 0:n], y_g[:, :, 0:n], ALU.mult).then_inc(S["yf_d"], 1)

                    def split_mix(i):
                        n = rows_of(i)
                        v.wait_ge(S["mhi_d"], 2 * i + 1)
                        v.tensor_tensor(m_lo[:, i % 2, 0:4, 0:n], a_ps[:, :, 0:n], m_hi[:, i % 2, 0:4, 0:n].bitcast(F32), ALU.subtract).then_inc(S["mlo_d"], 1)
                        v.wait_ge(S["mhi_d"], 2 * i + 2)
                        v.tensor_tensor(m_lo[:, i % 2, 4:8, 0:n], c_ps[:, :, 0:n], m_hi[:, i % 2, 4:8, 0:n].bitcast(F32), ALU.subtract).then_inc(S["mlo_d"], 1)

                    def update(i):
                        n = rows_of(i)
                        gate = gate_p if i < NT else gate_s
                        if i >= 1:
                            v.wait_ge(S["x1_d_"], i)
                        if i == 0:
                            v.wait_ge(S["gate_in"], 32)
                        for c in range(2):
                            v.wait_ge(S["z_pe"], 2 * i + c + 1)
                            ins = v.tensor_tensor(upd[0:n, c * 512:(c + 1) * 512], z_ps[c][0:n], gate[0:n, c * 512:(c + 1) * 512], ALU.mult)
                        ins.then_inc(S["upd_d"], 1)

                    def second_norm(i):
                        n = rows_of(i)
                        v.wait_ge(S["x1q"], i + 1)
                        if i >= 1:
                            v.wait_ge(S["x1n_d"], i)
                        step(v.tensor_scalar(rs2[0:n, 2:3], rs2[0:n, 1:2], 1.0 / D, EPS, ALU.mult, ALU.add))
                        rsqrt(v, step, rs2[0:n, 0:1], rs2[0:n, 2:3], rs2[0:n, 3:4])
                        v.sem_inc(S["rs2_d"], 1)

                    def split_y(i):
                        n = rows_of(i)
                        v.wait_ge(S["yhi_d"], i + 1)
                        if i >= 1:
                            v.wait_ge(S["c_pe"], i)
                        v.tensor_tensor(y_lo[:, :, 0:n], y_a[:, :, 0:n], y_hi[:, :, 0:n].bitcast(F32), ALU.subtract).then_inc(S["ylo_d"], 1)

                    def norm2(i):
                        n = rows_of(i)
                        v.wait_ge(S["rs2_d"], i + 1)
                        if i >= 1:
                            v.wait_ge(S["h_pe"], i)
                        v.tensor_scalar(x1n[0:n], x1[0:n, i % 2], rs2[0:n, 0:1], None, ALU.mult).then_inc(S["x1n_d"], 1)

                    layer_norm(0)
                    split_w(0)
                    split_w(1)
                    v.wait_ge(S["stat_in"], 48)
                    step(v.tensor_tensor(least[:], stat[:, :, 0, 0], stat[:, :, 1, 0], ALU.min))
                    step(v.tensor_tensor(least[:], least[:], stat[:, :, 2, 0], ALU.min))
                    for a in range(3):
                        step(v.tensor_tensor(fac[:, :, a], least[:], stat[:, :, a, 0], ALU.subtract))
                    v.sem_inc(S["fac_e"], 1)
                    gate_y(0)
                    split_y(0)
                    v.wait_ge(S["fac_x"], 1)
                    step(v.tensor_tensor(total[:], fac[:, :, 0], stat[:, :, 0, 1], ALU.mult))
                    for a in (1, 2):
                        step(v.tensor_tensor(least[:], fac[:, :, a], stat[:, :, a, 1], ALU.mult))
                        step(v.tensor_tensor(total[:], total[:], least[:], ALU.add))
                    step(v.reciprocal(total[:], total[:]))
                    for a in range(3):
                        step(v.tensor_tensor(fac[:, :, a], fac[:, :, a], total[:], ALU.mult))
                    v.sem_inc(S["fac_d"], 1)
                    for n in range(2, WN):
                        split_w(n)
                    split_mix(0)
                    for i in range(NT + 1):
                        if i < NT:
                            layer_norm(i + 1)
                        if i >= 1:
                            second_norm(i - 1)
                            norm2(i - 1)
                        if i < NT:
                            gate_y(i + 1)
                            split_y(i + 1)
                        update(i)
                        if i < NT:
                            split_mix(i + 1)
                    second_norm(NT)
                    norm2(NT)
                    v.wait_ge(S["h_pe"], NT + 1)
                    v.wait_ge(h2_out[NT % 2], 16 * (NT // 2))
                    for k in range(KT):
                        view = h2[:, NT % 2, k, 0:NS].rearrange("p (b t) -> p b t", t=DS)
                        step(v.tensor_tensor(view, h_ps[:, k, 0:NS].rearrange("p (b t) -> p b t", t=DS),
                                             gain2[:, k, 0:DB].unsqueeze(2).to_broadcast([P, DB, DS]), ALU.mult))
                        ins = v.tensor_tensor(view, view, modT[:, M_SH2 + k, 0:DB].unsqueeze(2).to_broadcast([P, DB, DS]), ALU.add)
                    ins.then_inc(S["h2_d_"], 1)

                @block.tensor
                def _(pe):
                    def turn_dw(i):
                        n = rows_of(i)
                        pe.wait_ge(dw_in[i % 2], 16 * (i // 2 + 1))
                        if i >= 1:
                            pe.wait_ge(S["yn_d"], i)
                        for c in range(CC):
                            mm = pe.transpose(dw_ps[0:n, c * P:(c + 1) * P], dwt[:, i % 2, c, 0:n], ident[:])
                        mm.then_inc(S["dw_pe"], 1)

                    def turn_y(i):
                        n = rows_of(i)
                        pe.wait_ge(S["yn_d"], i + 1)
                        if i >= 1:
                            pe.wait_ge(S["yg_d"], i)
                        for c in range(CC):
                            mm = pe.transpose(y_ps[:, c, 0:n], y_n[0:n, c * P:(c + 1) * P], ident[0:n, 0:n])
                        mm.then_inc(S["y_pe"], 1)

                    def turn_o(i):
                        n = rows_of(i)
                        pe.wait_ge(S["o_d"], i + 1)
                        if i >= 1:
                            pe.wait_ge(S["mlo_d"], 2 * i - 1)
                        for c in range(4):
                            mm = pe.transpose(a_ps[:, c, 0:n], o_n[0:n, c * P:(c + 1) * P], ident[0:n, 0:n])
                        mm.then_inc(S["a_pe"], 1)

                    def pointwise(i):
                        n = rows_of(i)
                        pe.wait_ge(S["ylo_d"], i + 1)
                        if i == 0:
                            pe.wait_ge(S["w_lod"], 2)
                        if i >= 1:
                            pe.wait_ge(S["mlo_d"], 2 * i)
                        for c in range(CC):
                            out, cols = c_ps[:, c, 0:n], slice(c * P, (c + 1) * P)
                            for k in range(CC):
                                pe.matmul(out, wp_hi[:, k, cols], y_hi[:, k, 0:n], start=k == 0, stop=False)
                                pe.matmul(out, wp_hi[:, k, cols], y_lo[:, k, 0:n], start=False, stop=False)
                                mm = pe.matmul(out, wp_lo[:, k, cols], y_hi[:, k, 0:n], start=False, stop=k == CC - 1)
                        mm.then_inc(S["c_pe"], 1)

                    def project(i, c):
                        n = rows_of(i)
                        if i >= 1:
                            pe.wait_ge(S["upd_d"], i)
                        for k in range(KT):
                            if c == 0 and k == 0:
                                pe.wait_ge(S["mlo_d"], 2 * i + 1)
                            if c == 0 and k == 4:
                                pe.wait_ge(S["mlo_d"], 2 * i + 2)
                            if i == 0 and c == 0:
                                pe.wait_ge(S["w_lod"], k + 3)
                            hi, lo, cols = m_hi[:, i % 2, k, 0:n], m_lo[:, i % 2, k, 0:n], slice(c * 512, (c + 1) * 512)
                            pe.matmul(z_ps[c][0:n], hi, wo_hi[:, k, cols], start=k == 0, stop=False)
                            pe.matmul(z_ps[c][0:n], hi, wo_lo[:, k, cols], start=False, stop=False)
                            mm = pe.matmul(z_ps[c][0:n], lo, wo_hi[:, k, cols], start=False, stop=k == KT - 1)
                        mm.then_inc(S["z_pe"], 1)

                    def turn_x(i):
                        n = rows_of(i)
                        pe.wait_ge(S["x1n_d"], i + 1)
                        if i >= 1:
                            pe.wait_ge(S["h2_d_"], i)
                        for k in range(KT):
                            mm = pe.transpose(h_ps[:, k, 0:n], x1n[0:n, k * P:(k + 1) * P], ident[0:n, 0:n])
                        mm.then_inc(S["h_pe"], 1)

                    turn_dw(0)
                    turn_y(0)
                    turn_o(0)
                    pointwise(0)
                    for i in range(NT + 1):
                        if i < NT:
                            turn_dw(i + 1)
                        project(i, 0)
                        if i < NT:
                            turn_y(i + 1)
                        project(i, 1)
                        if i < NT:
                            turn_o(i + 1)
                        if i >= 1:
                            turn_x(i - 1)
                        if i < NT:
                            pointwise(i + 1)
                    turn_x(NT)

        end_stage()

        with ExitStack() as st:
            def sb(name, shape, dt=F32):
                return st.enter_context(nc.sbuf_tensor("ff_" + name, shape, dt))

            def ps(name, shape, dt=F32):
                return st.enter_context(nc.psum_tensor("ff_" + name, shape, dt))

            FB = 4
            NBLK = FF // P // FB
            MAXT = SEQ // 2 + NS
            w_raw = sb("w_raw", [P, 2, D])
            w_hi = sb("w_hi", [P, 2, D], F32R)
            w_lo = sb("w_lo", [P, 2, D], F32R)
            y = sb("y", [P, KT, MAXT])
            h_hi = sb("h_hi", [P, KT, MAXT], F32R)
            h_lo = sb("h_lo", [P, KT, MAXT], F32R)
            relu = sb("relu", [P, 2, 512])
            sqr = sb("sqr", [P, 2, 512])
            a_hi = sb("a_hi", [P, FB, MAXT], F32R)
            a_lo = sb("a_lo", [P, FB, MAXT], F32R)
            u_ps = [ps(f"u_ps{i}", [P, 512]) for i in range(6)]
            out_ps = ps("out_ps", [P, D])
            XR = 4
            x1_t = sb("x1_t", [P, XR, D])
            h_raw = sb("h_raw", [P, 2, MAXT])

            def sm(name):
                return sem("ff_" + name)

            hhi_d, hlo_d, w_hid, w_lod, u_pe = sm("hhi_d"), sm("hlo_d"), sm("w_hid"), sm("w_lod"), sm("u_pe")
            relu_d, sqr_d, ahi_d, alo_d, y_d, ygate_d = sm("relu_d"), sm("sqr_d"), sm("ahi_d"), sm("alo_d"), sm("y_d"), sm("ygate_d")
            t_pe, out_d, fv = sm("t_pe"), sm("out_d"), sm("fv")
            w_ld, h_in = ([sm(f"{x}{i}") for i in range(2)] for x in ("w_ld", "h_in"))
            x1_in = [sm(f"x1_in{i}") for i in range(XR)]
            out_s = [stored[f"y_out{i}"] for i in range(XR)]
            RUNS = ((0, 512, 2), (SEQ // 2, MAXT // 3, 3))
            WT = FB + KT // 2
            PER_RUN = NBLK * WT
            tiles = [[(t0 + j * P, P) for j in range(SEQ // 2 // P)] for t0, _, _ in RUNS]
            tiles[1].append((SEQ, NS))
            flat = tiles[0] + tiles[1]

            def up_count(run, blk=0):
                return sum(NBLK * FB * r[2] for r in RUNS[:run]) + blk * FB * RUNS[run][2]

            def down_count(run, blk=0):
                return sum(NBLK * KT * r[2] for r in RUNS[:run]) + blk * KT * RUNS[run][2]

            def groups_before(n):
                run, r = divmod(n, PER_RUN)
                if run == len(RUNS):
                    return up_count(1, NBLK) + down_count(1, NBLK)
                blk, m = divmod(r, WT)
                nch = RUNS[run][2]
                return up_count(run, blk) + down_count(run, blk) + (m * nch if m < FB else FB * nch + (m - FB) * 2 * nch)

            group_kind = []
            for n in range(2 * PER_RUN):
                run, r = divmod(n, PER_RUN)
                kind = "up" if r % WT < FB else "down"
                group_kind += [kind] * (groups_before(n + 1) - groups_before(n))
            kind_count = []
            seen = {"up": 0, "down": 0}
            for kind in group_kind:
                seen[kind] += 1
                kind_count.append(seen[kind])

            def bank_free(eng, g):
                eng.wait_ge(alo_d if group_kind[g] == "up" else y_d, kind_count[g])

            with nc.Block() as block:
                @block.sync
                def _(sp):
                    def load_h(run, k):
                        t0, width, nch = RUNS[run]
                        i = run * KT + k
                        if i >= 2:
                            sp.wait_ge(hlo_d, i - 1)
                        sp.dma_start(h_raw[:, k % 2, 0:width * nch], h2_d[:, k, t0:t0 + width * nch]).then_inc(h_in[k % 2], 16)

                    def load_w(n):
                        blk, m = divmod(n % PER_RUN, WT)
                        if n >= 2:
                            sp.wait_ge(w_lod, n - 1)
                        if m < FB:
                            f = blk * FB + m
                            src = I["w_ff1"][0, :, f * P:(f + 1) * P].rearrange("(k p) c -> p k c", p=P)
                            sp.dma_start(w_raw[:, n % 2].rearrange("p (k c) -> p k c", k=KT), src).then_inc(w_ld[n % 2], 16)
                        else:
                            src = I["w_ff2"][0, blk * FB * P:(blk + 1) * FB * P, (m - FB) * 2 * P:(m - FB + 1) * 2 * P].rearrange("(f p) c -> p f c", p=P)
                            sp.dma_start(w_raw[:, n % 2].rearrange("p (f c) -> p f c", f=FB), src).then_inc(w_ld[n % 2], 16)

                    def store(j):
                        o, n = flat[j]
                        sp.wait_ge(out_d, j + 1)
                        dst = O["y_prompt"][0, o:o + n] if o < SEQ else O["y_sample"].rearrange("b t d -> (b t) d")
                        sp.dma_start(dst, x1_t[0:n, j % XR]).then_inc(out_s[j % XR], 16)

                    def load_x1(j):
                        o, n = flat[j]
                        if j >= XR:
                            sp.wait_ge(out_s[j % XR], 16 * (j // XR))
                        sp.dma_start(x1_t[0:n, j % XR], x1_d[o:o + n]).then_inc(x1_in[j % XR], 16)

                    def finish(run):
                        first = len(tiles[0]) * run
                        for j in range(first + 2, first + len(tiles[run]) + 2):
                            store(j - 2)
                            if j < len(flat):
                                load_x1(j)

                    load_w(0)
                    load_w(1)
                    for k in range(KT):
                        load_h(0, k)
                    load_x1(0)
                    load_x1(1)
                    for n in range(2, 2 * PER_RUN):
                        if n == PER_RUN + FB + 2:
                            finish(0)
                        load_w(n)
                        d = n - (PER_RUN - KT // 2 + 1)
                        if 0 <= d < KT // 2:
                            load_h(1, 2 * d)
                            load_h(1, 2 * d + 1)
                    finish(1)
                    for i in range(XR):
                        sp.wait_ge(out_s[i], 16 * len(flat[i::XR]))

                @block.gpsimd
                def _(pool):
                    def split_w(n):
                        pool.wait_ge(w_hid, n + 1)
                        if n >= 2:
                            pool.wait_ge(u_pe, groups_before(n - 1))
                        pool.tensor_tensor(w_lo[:, n % 2], w_raw[:, n % 2], w_hi[:, n % 2].bitcast(F32), ALU.subtract).then_inc(w_lod, 1)

                    split_w(0)
                    for n in range(2 * PER_RUN):
                        run, r = divmod(n, PER_RUN)
                        blk, m = divmod(r, WT)
                        _, width, nch = RUNS[run]
                        if n + 1 < 2 * PER_RUN:
                            split_w(n + 1)
                        if n % 16 == 8 and n // 16 < 5:
                            copy_cache(pool, 11 + n // 16)
                        if m < FB:
                            for c in range(nch):
                                e = up_count(run, blk) + m * nch + c
                                pool.wait_ge(ahi_d, e + 1)
                                pool.wait_ge(sqr_d, e + 1)
                                pool.tensor_tensor(a_lo[:, m, c * width:(c + 1) * width], sqr[:, e % 2, 0:width],
                                                   a_hi[:, m, c * width:(c + 1) * width].bitcast(F32), ALU.subtract).then_inc(alo_d, 1)

                @block.scalar
                def _(act):
                    def split_w(n):
                        act.wait_ge(w_ld[n % 2], 16 * (n // 2 + 1))
                        if n >= 2:
                            act.wait_ge(u_pe, groups_before(n - 1))
                        act.activation(w_hi[:, n % 2], w_raw[:, n % 2], ACT.Copy).then_inc(w_hid, 1)

                    def split_h(run, k):
                        T = RUNS[run][1] * RUNS[run][2]
                        act.wait_ge(h_in[k % 2], 16 * ((run * KT + k) // 2 + 1))
                        if run and k == 0:
                            act.wait_ge(u_pe, groups_before(PER_RUN - KT // 2))
                        act.activation(h_hi[:, k, 0:T], h_raw[:, k % 2, 0:T], ACT.Copy).then_inc(hhi_d, 1)

                    def gate(run, k):
                        act.wait_ge(y_d, down_count(run, NBLK - 1) + (k + 1) * RUNS[run][2])
                        act.activation(y[:, k, 0:SEQ // 2], y[:, k, 0:SEQ // 2], ACT.Copy, scale=modT[:, M_G2 + k, 8:9]).then_inc(ygate_d, 1)

                    split_w(0)
                    for k in range(KT):
                        split_h(0, k)
                    for n in range(2 * PER_RUN):
                        run, r = divmod(n, PER_RUN)
                        blk, m = divmod(r, WT)
                        _, width, nch = RUNS[run]
                        if n + 1 < 2 * PER_RUN:
                            split_w(n + 1)
                        if m < FB:
                            for c in range(nch):
                                e = up_count(run, blk) + m * nch + c
                                g = groups_before(n) + c
                                act.wait_ge(u_pe, g + 1)
                                if e >= 2:
                                    act.wait_ge(sqr_d, e - 1)
                                    act.wait_ge(ahi_d, e - 1)
                                act.activation(relu[:, e % 2, 0:width], u_ps[g % 6][:, 0:width], ACT.Relu).then_inc(relu_d, 1)
                                act.wait_ge(relu_d, e + 1)
                                if m == 0 and c == 0 and n >= WT:
                                    act.wait_ge(u_pe, groups_before(n))
                                act.activation(a_hi[:, m, c * width:(c + 1) * width], relu[:, e % 2, 0:width], ACT.Square).then_inc(ahi_d, 1)
                        elif blk == NBLK - 1:
                            d = m - FB
                            if run == 0:
                                split_h(1, 2 * d)
                                split_h(1, 2 * d + 1)
                            if d >= 1:
                                gate(run, 2 * d - 2)
                                gate(run, 2 * d - 1)
                            if d == KT // 2 - 1:
                                gate(run, KT - 2)
                                gate(run, KT - 1)

                @block.vector
                def _(v):
                    def split_h(run, k):
                        T = RUNS[run][1] * RUNS[run][2]
                        v.wait_ge(hhi_d, run * KT + k + 1)
                        v.tensor_tensor(h_lo[:, k, 0:T], h_raw[:, k % 2, 0:T], h_hi[:, k, 0:T].bitcast(F32), ALU.subtract).then_inc(hlo_d, 1)

                    def finish(run):
                        first = len(tiles[0]) * run
                        for j in range(first, first + len(tiles[run])):
                            n = flat[j][1]
                            v.wait_ge(t_pe, j + 1)
                            v.wait_ge(x1_in[j % XR], 16 * (j // XR + 1))
                            v.tensor_tensor(x1_t[0:n, j % XR], out_ps[0:n], x1_t[0:n, j % XR], ALU.add).then_inc(out_d, 1)

                    for k in range(KT):
                        split_h(0, k)
                    for run, (_, width, nch) in enumerate(RUNS):
                        for blk in range(NBLK):
                            for e in range(up_count(run, blk), up_count(run, blk + 1)):
                                v.wait_ge(relu_d, e + 1)
                                if e >= 2:
                                    v.wait_ge(alo_d, e - 1)
                                v.tensor_tensor(sqr[:, e % 2, 0:width], relu[:, e % 2, 0:width], relu[:, e % 2, 0:width], ALU.mult).then_inc(sqr_d, 1)
                            if run == 1 and blk == 0:
                                finish(0)
                            for e in range(KT * nch):
                                k, c = divmod(e, nch)
                                g = groups_before(run * PER_RUN + blk * WT + FB) + e
                                v.wait_ge(u_pe, g + 1)
                                dst, src = y[:, k, c * width:(c + 1) * width], u_ps[g % 6][:, 0:width]
                                if blk == 0:
                                    v.tensor_copy(dst, src).then_inc(y_d, 1)
                                else:
                                    v.wait_ge(y_d, down_count(run, blk - 1) + e + 1)
                                    v.tensor_tensor(dst, src, dst, ALU.add).then_inc(y_d, 1)
                                if run == 0 and blk == NBLK - 1 and e % 2 == 1:
                                    split_h(1, e // 2)
                    v.wait_ge(y_d, down_count(1, NBLK))
                    for k in range(KT):
                        view = y[:, k, SEQ // 2:MAXT].rearrange("p (b t) -> p b t", t=DS)
                        ins = v.tensor_tensor(view, view, modT[:, M_G2 + k, 0:DB].unsqueeze(2).to_broadcast([P, DB, DS]), ALU.mult)
                    ins.then_inc(fv, 1)
                    finish(1)

                @block.tensor
                def _(pe):
                    def finish(run):
                        first = len(tiles[0]) * run
                        pe.wait_ge(ygate_d, KT * (run + 1))
                        for j in range(first, first + len(tiles[run])):
                            n = flat[j][1]
                            o = flat[j][0] - RUNS[run][0]
                            if n < P:
                                pe.wait_ge(fv, 1)
                            if j >= 1:
                                pe.wait_ge(out_d, j)
                            for k in range(KT):
                                mm = pe.transpose(out_ps[0:n, k * P:(k + 1) * P], y[:, k, o:o + n], ident[:])
                            mm.then_inc(t_pe, 1)

                    for n in range(2 * PER_RUN):
                        run, r = divmod(n, PER_RUN)
                        blk, m = divmod(r, WT)
                        _, width, nch = RUNS[run]
                        up = m < FB
                        if n == PER_RUN + FB:
                            finish(0)
                        pe.wait_ge(w_lod, n + 1)
                        if m == FB:
                            pe.wait_ge(alo_d, up_count(run, blk + 1))
                        b = n % 2
                        for half in range(1 if up else 2):
                            for c in range(nch):
                                g = groups_before(n) + half * nch + c
                                if g >= 6:
                                    bank_free(pe, g - 6)
                                out = u_ps[g % 6][:, 0:width]
                                tok = slice(c * width, (c + 1) * width)
                                last = KT if up else FB
                                for k in range(last):
                                    if up:
                                        if r == 0 and c == 0:
                                            pe.wait_ge(hlo_d, run * KT + k + 1)
                                        w = slice(k * P, (k + 1) * P)
                                        hi, lo = h_hi[:, k, tok], h_lo[:, k, tok]
                                    else:
                                        w = slice(k * 2 * P + half * P, k * 2 * P + (half + 1) * P)
                                        hi, lo = a_hi[:, k, tok], a_lo[:, k, tok]
                                    pe.matmul(out, w_hi[:, b, w], hi, start=k == 0, stop=False)
                                    pe.matmul(out, w_hi[:, b, w], lo, start=False, stop=False)
                                    mm = pe.matmul(out, w_lo[:, b, w], hi, start=False, stop=k == last - 1)
                                mm.then_inc(u_pe, 1)
                    finish(1)

        with nc.Block() as block:
            @block.sync
            def _(sp):
                sp.wait_ge(copied, 16 * 2 * DB)


_INS = ["x_prompt", "x_sample", "cache_k", "cache_v", "state_conv", "c_prompt", "c_sample", "rel_bias", "norm1_g",
        "norm2_g", "w_ada", "b_ada", "w_in", "q_norm_g", "k_norm_g", "conv_dw", "conv_dw_b", "conv_ln_g", "conv_ln_b",
        "w_pw2", "w_o", "w_ff1", "w_ff2"]
_OUTS = [("y_prompt", (1, SEQ, D)), ("y_sample", (DB, DS, D)), ("new_k_prompt", (1, 1, WINC, H, DH)),
         ("new_v_prompt", (1, 1, WINC, H, DH)), ("new_conv_prompt", (1, 1, HIST, CW)),
         ("new_k_sample", (1, DB, WINC, H, DH)), ("new_v_sample", (1, DB, WINC, H, DH)),
         ("new_conv_sample", (1, DB, HIST, CW))]


def kernel(**inputs):
    import numpy as _np
    import concourse.bacc as _bacc
    from concourse.bass_utils import run_bass_kernel_spmd as _run

    nc = _bacc.Bacc("TRN2", target_bir_lowering=False, num_devices=1)
    arrays, ins, outs = {}, {}, {}
    given = {name: _np.ascontiguousarray(inputs[name]) for name in _INS}
    given.update(shape_constants())
    for name, a in given.items():
        arrays[f"in_{name}_dram"] = a
        ins[name] = nc.dram_tensor(f"in_{name}_dram", a.shape, mybir.dt.from_np(a.dtype), kind="ExternalInput").ap()
    for name, shape in _OUTS:
        outs[name] = nc.dram_tensor(f"out_{name}_dram", shape, F32, kind="ExternalOutput").ap()
    build(nc, ins, outs)
    r = _run(nc, [arrays], core_ids=[0])
    return tuple(r.results[0][f"out_{name}_dram"] for name, _ in _OUTS)
```
